# Optimizing a Trainium2 kernel written in Bass

```python
import math
import jax, jax.numpy as jnp
from jax import lax
import numpy as np

D_MODEL = 1024
BATCH = 1
SEQ = 256
DEPTH = 2

MEM_LEN = 256
Q_BLOCK = 128
EPS = 1e-6
NEG = -1e30
FFN_RESIDUAL = 0.5
D_FF = 2816

SB_HEADS = 8
SB_HEAD_DIM = 64
SB_WIDTH = SB_HEADS * SB_HEAD_DIM

MLA_HEADS = 8
MLA_Q_RANK = 384
MLA_KV_RANK = 128
MLA_NOPE_DIM = 64
MLA_ROPE_DIM = 32
MLA_V_DIM = 64
MLA_WIDTH = MLA_HEADS * MLA_V_DIM
ROPE_THETA = 10000.0

DIL_GROUPS = ((128, 1), (512, 4), (2048, 16))
DIL_HEADS = 8
DIL_HEAD_DIM = 64
DIL_WIDTH = DIL_HEADS * DIL_HEAD_DIM

REL_BUCKETS = 32
REL_MAX_DIST = 2048

X_HEADS = 4
X_HEAD_DIM = 128
X_WIDTH = X_HEADS * X_HEAD_DIM

N_BRANCH = 3
IN_SPLITS = ([SB_WIDTH] * 3
             + [MLA_Q_RANK, MLA_KV_RANK, MLA_ROPE_DIM]
             + [DIL_WIDTH] * (3 * len(DIL_GROUPS))
             + [D_MODEL] * N_BRANCH)
N_IN = sum(IN_SPLITS)
IN_OFFSETS = [int(o) for o in np.cumsum(IN_SPLITS)[:-1]]

kernel_name = "hybrid_gated_sb_mla_dilated_macaron"

def rms_norm(x, g):
    xf = x.astype(jnp.float32)
    y = xf * lax.rsqrt(jnp.mean(xf * xf, axis=-1, keepdims=True) + EPS)
    return (y * g.astype(jnp.float32)).astype(x.dtype)

def swiglu(x, w_gate, w_up, w_down):
    return (jax.nn.silu(x @ w_gate) * (x @ w_up)) @ w_down

def rope(x, pos):
    half = x.shape[-1] // 2
    freqs = ROPE_THETA ** (-jnp.arange(half, dtype=jnp.float32) / half)
    ang = pos.astype(jnp.float32)[:, None] * freqs[None, :]
    cos = jnp.cos(ang)[:, None, :]
    sin = jnp.sin(ang)[:, None, :]
    x1, x2 = x[..., :half], x[..., half:]
    return jnp.concatenate([x1 * cos - x2 * sin, x1 * sin + x2 * cos], axis=-1).astype(x.dtype)

def to_blocks(t):
    b, s = t.shape[:2]
    return t.reshape(b, s // Q_BLOCK, Q_BLOCK, *t.shape[2:]).swapaxes(0, 1)

def from_blocks(t):
    t = t.swapaxes(0, 1)
    return t.reshape(t.shape[0], t.shape[1] * t.shape[2], *t.shape[3:])

def stick_breaking_attention(q, k, v):
    s = q.shape[1]
    scale = q.shape[-1] ** -0.5
    key_pos = jnp.arange(s)

    def block(args):
        qb, q0 = args
        z = jnp.einsum('bqhd,bkhd->bhqk', qb, k).astype(jnp.float32) * scale
        strict = key_pos[None, :] < (q0 + jnp.arange(Q_BLOCK))[:, None]
        log_beta = jax.nn.log_sigmoid(z)
        log_keep = jnp.where(strict, jax.nn.log_sigmoid(-z), 0.0)
        after = lax.cumsum(log_keep, axis=3, reverse=True) - log_keep
        w = jnp.where(strict, jnp.exp(log_beta + after), 0.0)
        return jnp.einsum('bhqk,bkhd->bqhd', w.astype(v.dtype), v)

    starts = jnp.arange(s // Q_BLOCK, dtype=jnp.int32) * Q_BLOCK
    return from_blocks(lax.map(block, (to_blocks(q), starts)))

def causal_softmax_attention(q, k, v, scale):
    s = q.shape[1]
    key_pos = jnp.arange(s)

    def block(args):
        qb, q0 = args
        logits = jnp.einsum('bqhd,bkhd->bhqk', qb, k).astype(jnp.float32) * scale
        causal = key_pos[None, :] <= (q0 + jnp.arange(Q_BLOCK))[:, None]
        p = jax.nn.softmax(jnp.where(causal, logits, NEG), axis=-1)
        return jnp.einsum('bhqk,bkhd->bqhd', p.astype(v.dtype), v)

    starts = jnp.arange(s // Q_BLOCK, dtype=jnp.int32) * Q_BLOCK
    return from_blocks(lax.map(block, (to_blocks(q), starts)))

def rel_bucket(dist):
    exact = REL_BUCKETS // 2
    d = jnp.maximum(dist, exact).astype(jnp.float32)
    large = exact + (jnp.log(d / exact) / math.log(REL_MAX_DIST / exact)
                     * (REL_BUCKETS - exact)).astype(jnp.int32)
    return jnp.where(dist < exact, dist, jnp.minimum(large, REL_BUCKETS - 1))

def dilated_group_attention(q, k, v, dilation, taps, bias_table):
    b, s, h, d = q.shape
    r = dilation
    L = s // r
    nb = -(-L // Q_BLOCK)
    Lp = nb * Q_BLOCK

    def residue_major(t):
        return t.reshape(b, L, r, h, d).swapaxes(1, 2)

    def pad(t, front):
        return jnp.pad(t, ((0, 0), (0, 0), (front, Lp - L), (0, 0), (0, 0)))

    qr = pad(residue_major(q), 0).reshape(b, r, nb, Q_BLOCK, h, d)
    kr = pad(residue_major(k), Q_BLOCK).reshape(b, r, nb + 1, Q_BLOCK, h, d)
    vr = pad(residue_major(v), Q_BLOCK).reshape(b, r, nb + 1, Q_BLOCK, h, d)
    kb = jnp.concatenate([kr[:, :, :-1], kr[:, :, 1:]], axis=3)
    vb = jnp.concatenate([vr[:, :, :-1], vr[:, :, 1:]], axis=3)

    logits = jnp.einsum('brnqhd,brnkhd->brnhqk', qr, kb).astype(jnp.float32) * d ** -0.5
    qi = jnp.arange(Q_BLOCK)
    kj = jnp.arange(2 * Q_BLOCK)
    steps = (qi[:, None] + Q_BLOCK) - kj[None, :]
    in_window = (steps >= 0) & (steps <= taps)
    key_idx = jnp.arange(nb)[:, None, None] * Q_BLOCK + kj[None, None, :] - Q_BLOCK
    valid = in_window[None] & (key_idx >= 0)
    bias = bias_table[rel_bucket(jnp.clip(steps, 0, taps) * r)]
    logits = logits + jnp.transpose(bias, (2, 0, 1)).astype(jnp.float32)
    logits = jnp.where(valid[None, None, :, None], logits, NEG)

    lse = jax.nn.logsumexp(logits, axis=-1)
    p = jnp.exp(logits - lse[..., None])
    out = jnp.einsum('brnhqk,brnkhd->brnqhd', p.astype(v.dtype), vb)
    out = out.reshape(b, r, Lp, h, d)[:, :, :L].swapaxes(1, 2).reshape(b, s, h, d)
    lse = jnp.transpose(lse, (0, 1, 2, 4, 3)).reshape(b, r, Lp, h)[:, :, :L]
    lse = lse.swapaxes(1, 2).reshape(b, s, h)
    return out, lse

def parallel_mixer(u, w_in, gate_bias, mla_q_norm, mla_w_uq, mla_kv_norm, mla_w_ukv,
                   w_branch_a, w_branch_b, w_branch_c, w_mix_out, rel_bias):
    b, s, _ = u.shape
    parts = jnp.split(u @ w_in, IN_OFFSETS, axis=-1)
    sb_q, sb_k, sb_v, c_q, c_kv, k_rope = parts[:6]
    dil = parts[6:6 + 3 * len(DIL_GROUPS)]
    g_a, g_b, g_c = parts[6 + 3 * len(DIL_GROUPS):]

    def heads(t, n):
        return t.reshape(b, s, n, -1)

    o_a = stick_breaking_attention(heads(sb_q, SB_HEADS), heads(sb_k, SB_HEADS),
                                   heads(sb_v, SB_HEADS)).reshape(b, s, SB_WIDTH)

    pos = jnp.arange(s)
    q = (rms_norm(c_q, mla_q_norm) @ mla_w_uq).reshape(b, s, MLA_HEADS, MLA_NOPE_DIM + MLA_ROPE_DIM)
    q = jnp.concatenate([q[..., :MLA_NOPE_DIM], rope(q[..., MLA_NOPE_DIM:], pos)], axis=-1)
    kv = (rms_norm(c_kv, mla_kv_norm) @ mla_w_ukv).reshape(b, s, MLA_HEADS, MLA_NOPE_DIM + MLA_V_DIM)
    k_pe = rope(k_rope[:, :, None, :], pos)
    k = jnp.concatenate([kv[..., :MLA_NOPE_DIM],
                         jnp.broadcast_to(k_pe, (b, s, MLA_HEADS, MLA_ROPE_DIM))], axis=-1)
    v = kv[..., MLA_NOPE_DIM:]
    o_b = causal_softmax_attention(q, k, v, (MLA_NOPE_DIM + MLA_ROPE_DIM) ** -0.5)
    o_b = o_b.reshape(b, s, MLA_WIDTH)

    outs, lses = [], []
    for g, (window, dilation) in enumerate(DIL_GROUPS):
        qg, kg, vg = (heads(t, DIL_HEADS) for t in dil[3 * g:3 * g + 3])
        o, lse = dilated_group_attention(qg, kg, vg, dilation, window // dilation,
                                         rel_bias[:, g * DIL_HEADS:(g + 1) * DIL_HEADS])
        outs.append(o)
        lses.append(lse)
    outs = jnp.stack(outs)
    alpha = jax.nn.softmax(jnp.stack(lses), axis=0)
    o_c = jnp.einsum('gbsh,gbshd->bshd', alpha.astype(outs.dtype), outs).reshape(b, s, DIL_WIDTH)

    merged = (jax.nn.sigmoid(g_a + gate_bias[0]) * (o_a @ w_branch_a)
              + jax.nn.sigmoid(g_b + gate_bias[1]) * (o_b @ w_branch_b)
              + jax.nn.sigmoid(g_c + gate_bias[2]) * (o_c @ w_branch_c))
    return merged @ w_mix_out

def memory_cross_attention(h, mem, w_q, w_kv, w_o):
    b, s, _ = h.shape
    m = mem.shape[1]
    q = (h @ w_q).reshape(b, s, X_HEADS, X_HEAD_DIM)
    kv = (mem @ w_kv).reshape(b, m, 2, X_HEADS, X_HEAD_DIM)
    k, v = kv[:, :, 0], kv[:, :, 1]
    logits = jnp.einsum('bshd,bmhd->bhsm', q, k).astype(jnp.float32) * X_HEAD_DIM ** -0.5
    p = jax.nn.softmax(logits, axis=-1)
    o = jnp.einsum('bhsm,bmhd->bshd', p.astype(v.dtype), v)
    return o.reshape(b, s, X_WIDTH) @ w_o

def setup_inputs(seed: int = 0) -> dict:
    key = jax.random.key(seed)
    ks = iter(jax.random.split(key, 32))

    def dense(shape, fan_in):
        return jax.random.normal(next(ks), shape, jnp.float32) * fan_in ** -0.5

    def gain(shape):
        return 1.0 + 0.02 * jax.random.normal(next(ks), shape, jnp.float32)

    Ld = DEPTH
    return {
        "x": jax.random.normal(next(ks), (BATCH, SEQ, D_MODEL), jnp.float32),
        "mem": jax.random.normal(next(ks), (BATCH, MEM_LEN, D_MODEL), jnp.float32),
        "ffn1_norm": gain((Ld, D_MODEL)),
        "ffn1_w_gate": dense((Ld, D_MODEL, D_FF), D_MODEL),
        "ffn1_w_up": dense((Ld, D_MODEL, D_FF), D_MODEL),
        "ffn1_w_down": dense((Ld, D_FF, D_MODEL), D_FF),
        "mix_norm": gain((Ld, D_MODEL)),
        "w_in": dense((Ld, D_MODEL, N_IN), D_MODEL),
        "gate_bias": 0.1 * jax.random.normal(next(ks), (Ld, N_BRANCH, D_MODEL), jnp.float32),
        "mla_q_norm": gain((Ld, MLA_Q_RANK)),
        "mla_w_uq": dense((Ld, MLA_Q_RANK, MLA_HEADS * (MLA_NOPE_DIM + MLA_ROPE_DIM)), MLA_Q_RANK),
        "mla_kv_norm": gain((Ld, MLA_KV_RANK)),
        "mla_w_ukv": dense((Ld, MLA_KV_RANK, MLA_HEADS * (MLA_NOPE_DIM + MLA_V_DIM)), MLA_KV_RANK),
        "w_branch_a": dense((Ld, SB_WIDTH, D_MODEL), SB_WIDTH),
        "w_branch_b": dense((Ld, MLA_WIDTH, D_MODEL), MLA_WIDTH),
        "w_branch_c": dense((Ld, DIL_WIDTH, D_MODEL), DIL_WIDTH),
        "w_mix_out": dense((Ld, D_MODEL, D_MODEL), D_MODEL),
        "rel_bias": 0.5 * jax.random.normal(next(ks), (REL_BUCKETS, DIL_HEADS * len(DIL_GROUPS)), jnp.float32),
        "xattn_norm": gain((Ld, D_MODEL)),
        "mem_norm": gain((Ld, D_MODEL)),
        "xattn_w_q": dense((Ld, D_MODEL, X_WIDTH), D_MODEL),
        "xattn_w_kv": dense((Ld, D_MODEL, 2 * X_WIDTH), D_MODEL),
        "xattn_w_o": dense((Ld, X_WIDTH, D_MODEL), X_WIDTH),
        "ffn2_norm": gain((Ld, D_MODEL)),
        "ffn2_w_gate": dense((Ld, D_MODEL, D_FF), D_MODEL),
        "ffn2_w_up": dense((Ld, D_MODEL, D_FF), D_MODEL),
        "ffn2_w_down": dense((Ld, D_FF, D_MODEL), D_FF),
        "final_norm": gain((D_MODEL,)),
    }

def reference(x, mem, ffn1_norm, ffn1_w_gate, ffn1_w_up, ffn1_w_down, mix_norm, w_in, gate_bias,
              mla_q_norm, mla_w_uq, mla_kv_norm, mla_w_ukv, w_branch_a, w_branch_b, w_branch_c,
              w_mix_out, rel_bias, xattn_norm, mem_norm, xattn_w_q, xattn_w_kv, xattn_w_o,
              ffn2_norm, ffn2_w_gate, ffn2_w_up, ffn2_w_down, final_norm):
    h = x
    for l in range(DEPTH):
        h = h + FFN_RESIDUAL * swiglu(rms_norm(h, ffn1_norm[l]),
                                      ffn1_w_gate[l], ffn1_w_up[l], ffn1_w_down[l])
        h = h + parallel_mixer(rms_norm(h, mix_norm[l]), w_in[l], gate_bias[l],
                               mla_q_norm[l], mla_w_uq[l], mla_kv_norm[l], mla_w_ukv[l],
                               w_branch_a[l], w_branch_b[l], w_branch_c[l], w_mix_out[l], rel_bias)
        h = h + memory_cross_attention(rms_norm(h, xattn_norm[l]), rms_norm(mem, mem_norm[l]),
                                       xattn_w_q[l], xattn_w_kv[l], xattn_w_o[l])
        h = h + FFN_RESIDUAL * swiglu(rms_norm(h, ffn2_norm[l]),
                                      ffn2_w_gate[l], ffn2_w_up[l], ffn2_w_down[l])
    return rms_norm(h, final_norm)


_drawn_inputs = setup_inputs


def setup_inputs(seed=0):
    import zlib

    import numpy as np

    out = dict(_drawn_inputs(seed))
    spreads = {}
    factors = {'ffn1_norm': 4.475,
     'mix_norm': 4.13,
     'gate_bias': 2.907,
     'mla_q_norm': 8.0,
     'mla_kv_norm': 8.0,
     'xattn_norm': 8.0,
     'mem_norm': 8.0,
     'ffn2_norm': 5.47,
     'final_norm': 3.118}
    for name, (base, spread) in spreads.items():
        noise = np.random.default_rng([zlib.crc32(name.encode()), seed]).standard_normal(out[name].shape)
        drawn = base * np.exp(spread * noise) if base else spread * noise
        out[name] = __import__('jax').numpy.asarray(drawn.astype(out[name].dtype))
    for name, factor in factors.items():
        out[name] = (out[name] * factor).astype(out[name].dtype)
    return out
```

```python
import math
from contextlib import ExitStack

import numpy as np
import concourse.bass as bass
from concourse import mybir

F32 = mybir.dt.float32
F32R = mybir.dt.float32r
ALU = mybir.AluOpType
ACT = mybir.ActivationFunctionType
AX = mybir.AxisListType

P = 128
D = 1024
S = 256
M = 256
DEPTH = 2
D_FF = 2816
KT = D // P
TT = S // P
FT = D_FF // P
EPS = 1e-6
NEG = -1e30
HEADS = 8
HD = 64
WIDTH = HEADS * HD
Q_RANK, KV_RANK, NOPE, ROPE = 384, 128, 64, 32
QK = NOPE + ROPE
GROUPS = ((128, 1), (512, 4), (2048, 16))
NG = len(GROUPS)
BUCKETS, MAX_DIST = 32, 2048
XH, XD = 4, 128
RING = 4

C_SBQ, C_SBK, C_SBV = 0, WIDTH, 2 * WIDTH
C_LAT = 3 * WIDTH
C_KR = C_LAT + Q_RANK + KV_RANK
C_DIL = C_KR + ROPE
C_GATE = C_DIL + 3 * NG * WIDTH

FFN_UNITS = 3 * FT
U_FFN1 = 0
U_LAT = U_FFN1 + FFN_UNITS
U_KR = U_LAT + 4
U_SBQ = U_KR + 1
U_SBK = U_SBQ + 4
U_SBV = U_SBK + 4
U_UQ = U_SBV + 4
U_UKV = U_UQ + 6
U_DQK = U_UKV + 1
U_DV = U_DQK + 8 * NG
U_GATE = U_DV + 4 * NG
U_MK = U_GATE + 8 * 3
U_MV = U_MK + 4
U_BR = U_MV + 4
U_MIX = U_BR + 12
U_XQ = U_MIX + 8
U_XO = U_XQ + 4
U_FFN2 = U_XO + 4
UNITS = U_FFN2 + FFN_UNITS
assert UNITS % RING == 0 and (12 % RING) == 0

D_SBQ = 0
D_SBK = D_SBQ + 4
D_SBV = D_SBK + 4
D_UQ = D_SBV + 2
D_UKV = D_UQ + 4
D_DQK = D_UKV + 4
D_DV = D_DQK + 8 * NG
D_GATE = D_DV + 2 * NG
D_MK = D_GATE + 24
D_MV = D_MK + 4
D_BR = D_MV + 2
D_XQ = D_BR + 12
OUTS = D_XQ + 4
assert OUTS % 2 == 0

N_MLA, N_DIL, N_X = 2 * HEADS, 2 * HEADS, 2 * XH
M_DIL = N_MLA
M_X = M_DIL + N_DIL
PIECES = M_X + N_X
N_FFN1, N_MIX, N_MEM, N_XA, N_FFN2, NORMS = 0, 1, 2, 3, 4, 5
R_FFN1, R_MIX, R_XA, R_FFN2, RESIDUALS = 0, 1, 2, 3, 4

BIAS_W = 384


def constants():
    i = np.arange(P)
    key, query = i[:, None], i[None, :]
    strict = (key < query).astype(np.float32)
    block = np.where(strict > 0, 0.0, NEG).astype(np.float32)
    strict_neg = np.concatenate([block, np.zeros((P, P), np.float32), block], 1)
    causal = np.where(i[None, :] <= i[:, None], 0.0, NEG).astype(np.float32)
    tri = np.where(key >= query, -1.0, 0.0).astype(np.float32)
    half = ROPE // 2
    freqs = np.float32(10000.0) ** (-np.arange(half, dtype=np.float32) / np.float32(half))
    ang = np.arange(S, dtype=np.float32)[:, None] * freqs[None, :].astype(np.float32)
    cs = np.stack([np.cos(ang), np.sin(ang)], 1).astype(np.float32)
    cs = cs.reshape(TT, P, 2, half).transpose(1, 2, 0, 3).reshape(P, 2 * TT * half)
    dist = 255 - np.arange(BIAS_W)
    exact = BUCKETS // 2
    d = np.maximum(dist, exact).astype(np.float32)
    large = exact + (np.log(d / exact) / math.log(MAX_DIST / exact) * (BUCKETS - exact)).astype(np.int32)
    bucket = np.where(dist < exact, np.maximum(dist, 0), np.minimum(large, BUCKETS - 1))
    onehot = (bucket[None, :] == np.arange(BUCKETS)[:, None]).astype(np.float32)
    allowed = np.stack([(dist >= 0) & (dist % r == 0) & (dist // r <= w // r) for w, r in GROUPS])
    window = np.repeat(np.where(allowed, 0.0, NEG).astype(np.float32), HEADS, 0)
    return {
        "c_ident": np.eye(P, dtype=np.float32), "c_tri": tri, "c_strict": strict,
        "c_strict_neg": strict_neg, "c_flip": np.ascontiguousarray(np.eye(P, dtype=np.float32)[::-1]), "c_causal": causal, "c_rope": np.ascontiguousarray(cs),
        "c_onehot": onehot, "c_window": np.ascontiguousarray(window),
    }


def pack_weights(w, np):
    stream = np.zeros((DEPTH, UNITS, P, 1024), np.float32)

    def tiles(u, m, k0, k1, c0, c1):
        n = (k1 - k0) * (c1 - c0)
        part = m[:, k0 * P:k1 * P, c0:c1].reshape(DEPTH, k1 - k0, P, c1 - c0)
        stream[:, u, :, 0:n] = part.transpose(0, 2, 1, 3).reshape(DEPTH, P, n)

    def feature_major(u0, m, c, n):
        for j in range(n):
            tiles(u0 + j, m, 0, KT, c + P * j, c + P * j + P)

    def token_major(u0, m, c):
        for j in range(4):
            tiles(u0 + j, m, 2 * j, 2 * j + 2, c, c + 512)

    def rows(u0, m, n):
        for k in range(n):
            tiles(u0 + k, m, k, k + 1, 0, D)

    for u0, gate, up, down in ((U_FFN1, "ffn1_w_gate", "ffn1_w_up", "ffn1_w_down"),
                               (U_FFN2, "ffn2_w_gate", "ffn2_w_up", "ffn2_w_down")):
        for i in range(FT):
            u = u0 + (3 * i - 1 if i else 0)
            feature_major(u, w[gate], P * i, 1)
            feature_major(u + 1, w[up], P * i, 1)
            tiles(u0 + (3 * i + 4 if i < FT - 1 else FFN_UNITS - 1), w[down], i, i + 1, 0, D)
    w_in = w["w_in"]
    token_major(U_LAT, w_in, C_LAT)
    tiles(U_KR, w_in, 0, KT, C_KR, C_KR + ROPE)
    feature_major(U_SBQ, w_in, C_SBQ, 8)
    token_major(U_SBV, w_in, C_SBV)
    for c in range(2):
        for k in range(3):
            tiles(U_UQ + 3 * c + k, w["mla_w_uq"], k, k + 1, 384 * c, 384 * c + 384)
    tiles(U_UKV, w["mla_w_ukv"], 0, 1, 0, 1024)
    for g in range(NG):
        feature_major(U_DQK + 8 * g, w_in, C_DIL + 3 * WIDTH * g, 8)
        token_major(U_DV + 4 * g, w_in, C_DIL + 3 * WIDTH * g + 2 * WIDTH)
    feature_major(U_GATE, w_in, C_GATE, 24)
    feature_major(U_MK, w["xattn_w_kv"], 0, 4)
    token_major(U_MV, w["xattn_w_kv"], XH * XD)
    for b, name in enumerate(("w_branch_a", "w_branch_b", "w_branch_c")):
        for j in range(4):
            tiles(U_BR + 4 * b + j, w[name], 0, 4, 2 * P * j, 2 * P * j + 2 * P)
    rows(U_MIX, w["w_mix_out"], KT)
    feature_major(U_XQ, w["xattn_w_q"], 0, 4)
    rows(U_XO, w["xattn_w_o"], XH)
    return stream.reshape(DEPTH * UNITS, P, 1024)


STREAMED = ("ffn1_w_gate", "ffn1_w_up", "ffn1_w_down", "w_in", "mla_w_uq", "mla_w_ukv", "w_branch_a",
            "w_branch_b", "w_branch_c", "w_mix_out", "xattn_w_q", "xattn_w_kv", "xattn_w_o",
            "ffn2_w_gate", "ffn2_w_up", "ffn2_w_down")


def trunk(nc, a, out):
    ctx = ExitStack()
    with ctx:
        def sb(name, n, dt=F32, parts=P):
            return ctx.enter_context(nc.sbuf_tensor(name, [parts, n], dt))

        def sem(name):
            return ctx.enter_context(nc.semaphore(name))

        raw = sb("raw", RING * 1024)
        w_hi = sb("w_hi", RING * 1024, F32R)
        w_lo = sb("w_lo", RING * 1024, F32R)
        u_hi = sb("u_hi", KT * S, F32R)
        u_lo = sb("u_lo", KT * S, F32R)
        v_hi = sb("v_hi", KT * S, F32R)
        v_lo = sb("v_lo", KT * S, F32R)
        h = sb("h", TT * D)
        dil_q = sb("dil_q", NG * 4 * S)
        dil_k = sb("dil_k", NG * 4 * S)
        dil_v = sb("dil_v", NG * TT * WIDTH)
        mla_q = sb("mla_q", HEADS * S)
        mla_k = sb("mla_k", HEADS * S)
        mla_v = sb("mla_v", TT * WIDTH)
        o_a = sb("o_a", 4 * S)
        o_b = sb("o_b", TT * WIDTH)
        o_c = sb("o_c", TT * WIDTH)
        sg = sb("sg", 3 * KT * S)
        work = sb("work", 3072)
        bias_sb = sb("bias_sb", 2 * NG * S)
        lat_gain = sb("lat_gain", Q_RANK + KV_RANK)
        ident = sb("ident", P)
        tri = sb("tri", P)
        minus1 = sb("minus1", P)
        strict = sb("strict", P)
        strict_neg = sb("strict_neg", 3 * P)
        causal = sb("causal", P)
        flip = sb("flip", P)
        rope_cs = sb("rope_cs", 2 * TT * 16)
        gate_b = sb("gate_b", 24)
        k_raw = sb("k_raw", TT * ROPE)
        k_pe = sb("k_pe", TT * ROPE)
        sumsq = sb("sumsq", TT)
        mean = sb("mean", TT)
        rstd = sb("rstd", TT)
        lat_ss = sb("lat_ss", 4)
        lat_ms = sb("lat_ms", 4)
        lat_rs = sb("lat_rs", 4)
        half_neg = sb("half_neg", 4)
        p_max = sb("p_max", 2)
        p_negmax = sb("p_negmax", 2)
        p_sum = sb("p_sum", 2)
        p_inv = sb("p_inv", 2)
        ps = ctx.enter_context(nc.psum_tensor("ps", [P, 8, 512], F32))
        bias_dram = nc.dram_tensor("bias_rows", (NG * HEADS, BIAS_W), F32, kind="Internal").ap()

        norm_x = sg[:, 0:2 * D].rearrange("p (t d) -> p t d", t=TT)
        gain = sg[:, 2 * D:3 * D]
        q_tok = sg[:, 3 * D:3 * D + 1536].rearrange("p (t h c) -> p t h c", t=TT, h=HEADS)
        k_cat = sg[:, 3 * D + 1536:6 * D].rearrange("p (t h c) -> p t h c", t=TT, h=HEADS)
        lat_n = mla_q[:, 0:TT * 512].rearrange("p (t c) -> p t c", t=TT)
        sb_q = dil_v[:, 0:4 * S].rearrange("p (f t) -> p f t", f=4)
        sb_k = dil_v[:, 4 * S:8 * S].rearrange("p (f t) -> p f t", f=4)
        sb_v = dil_v[:, 8 * S:12 * S].rearrange("p (t c) -> p t c", t=TT)
        dq = dil_q[:, :].rearrange("p (g f t) -> p g f t", g=NG, f=4)
        dk = dil_k[:, :].rearrange("p (g f t) -> p g f t", g=NG, f=4)
        dv = dil_v[:, :].rearrange("p (g t c) -> p g t c", g=NG, t=TT)
        mq = mla_q[:, :].rearrange("p (h t) -> p h t", h=HEADS)
        mk = mla_k[:, :].rearrange("p (h t) -> p h t", h=HEADS)
        mv = mla_v[:, :].rearrange("p (t c) -> p t c", t=TT)
        x_k = mla_q[:, 0:XH * M].rearrange("p (h t) -> p h t", h=XH)
        x_v = mla_q[:, XH * M:2 * XH * M].rearrange("p (t c) -> p t c", t=TT)
        x_q = mla_k[:, 0:XH * S].rearrange("p (h t) -> p h t", h=XH)
        oa = o_a[:, :].rearrange("p (f t) -> p f t", f=4)
        merged = dil_q[:, 0:KT * S].rearrange("p (j c) -> p j c", j=4)
        addend = dil_q[:, KT * S:KT * S + 1024].rearrange("p (b c) -> p b c", b=2)
        bias3 = bias_sb[:, :].rearrange("p (b g k) -> p b g k", b=2, g=NG)
        junk = bias_sb[:, 0:D]
        cosv = rope_cs[:, 0:TT * 16].rearrange("p (t c) -> p t c", t=TT)
        sinv = rope_cs[:, TT * 16:2 * TT * 16].rearrange("p (t c) -> p t c", t=TT)
        rope_t = work[:, 2304:2304 + 512].rearrange("p (b c) -> p b c", b=4)

        def probs_sb(m):
            return work[:, 768 * (m % 2):768 * (m % 2) + 768]

        def probs_t(m):
            return work[:, 1536 + 768 * (m % 2):1536 + 768 * (m % 2) + 768]

        def sb_soft(hd):
            return work[:, 384 * (hd % 2):384 * (hd % 2) + 384]

        def sb_sp(hd):
            return work[:, 768 + 384 * (hd % 2):768 + 384 * (hd % 2) + 384]

        def sb_w(hd):
            return work[:, 1536 + 384 * (hd % 2):1536 + 384 * (hd % 2) + 384]

        def silu_b(i):
            return work[:, S * (i % 2):S * (i % 2) + S]

        def prod_b(i):
            return work[:, 2 * S + S * (i % 2):2 * S + S * (i % 2) + S]

        def prod_t(t, i):
            return t[:, S * (i % 4):S * (i % 4) + S]

        def kt(t, k):
            return t[:, k * S:(k + 1) * S]

        def slot(t, u):
            return t[:, 1024 * (u % RING):1024 * (u % RING) + 1024]

        const_in = sem("const_in")
        x_in = sem("x_in")
        setup_mem = sem("setup_mem")
        bias_mm = sem("bias_mm")
        bias_row = sem("bias_row")
        bias_out = sem("bias_out")
        raw_in = [sem(f"raw_in{i}") for i in range(RING)]
        hi_made = sem("hi_made")
        lo_made = sem("lo_made")
        unit_used = sem("unit_used")
        taken = [sem("taken0"), sem("taken1")]
        gain_in = sem("gain_in")
        mem_in = sem("mem_in")
        small_in = sem("small_in")
        sq_done = sem("sq_done")
        mean_done = sem("mean_done")
        rstd_done = sem("rstd_done")
        x_normed = sem("x_normed")
        x_turned = sem("x_turned")
        x_hi = sem("x_hi")
        x_lo = sem("x_lo")
        resid = sem("resid")
        silu_done = sem("silu_done")
        prod_done = sem("prod_done")
        prod_hi = sem("prod_hi")
        prod_lo = sem("prod_lo")
        lat_sq = sem("lat_sq")
        lat_mean = sem("lat_mean")
        lat_rstd = sem("lat_rstd")
        lat_normed = sem("lat_normed")
        lat_turned = sem("lat_turned")
        lat_hi = sem("lat_hi")
        lat_lo = sem("lat_lo")
        kr_copied = sem("kr_copied")
        rope_step = sem("rope_step")
        mla_turned = sem("mla_turned")
        mla_copied = sem("mla_copied")
        ukv_done = sem("ukv_done")
        z_done = sem("z_done")
        z_abs = sem("z_abs")
        z_exp = sem("z_exp")
        z_ln = sem("z_ln")
        sp_done = sem("sp_done")
        sp_masked = sem("sp_masked")
        stick_sum = sem("stick_sum")
        stick_arg = sem("stick_arg")
        stick_w = sem("stick_w")
        stick_o = sem("stick_o")
        oa_copied = sem("oa_copied")
        bias_in = [sem("bias_in0"), sem("bias_in1")]
        logits_ps = sem("logits_ps")
        max_done = sem("max_done")
        negmax_done = sem("negmax_done")
        probs_done = sem("probs_done")
        probs_turned = sem("probs_turned")
        probs_t_act = sem("probs_t_act")
        probs_t_dve = sem("probs_t_dve")
        inv_done = sem("inv_done")
        pv_done = sem("pv_done")
        o_taken = sem("o_taken")
        o_turned = sem("o_turned")
        o_hi = sem("o_hi")
        o_lo = sem("o_lo")
        sig_done = sem("sig_done")
        merged_sum = sem("merged_sum")
        merged_hi = sem("merged_hi")
        merged_lo = sem("merged_lo")
        final_sem = sem("final_sem")
        out_sent = sem("out_sent")

        POOL_STEPS = 8 + 2 * 6
        O_SPLITS = 1 + 2 + 2 + 2
        O_TURNS = 6
        N_PT_DVE = N_MLA + N_DIL // 2 + N_X

        def pt_waits(eng, layer, m):
            if m < M_DIL:
                eng.wait_ge(probs_t_dve, layer * N_PT_DVE + m + 1)
            elif m < M_X:
                n = m - M_DIL
                eng.wait_ge(probs_t_act, layer * N_DIL + n + 1)
                if n % 2:
                    eng.wait_ge(probs_t_dve, layer * N_PT_DVE + N_MLA + n // 2 + 1)
            else:
                eng.wait_ge(probs_t_dve, layer * N_PT_DVE + N_MLA + N_DIL // 2 + m - M_X + 1)

        def out_taken(eng, layer, d):
            eng.wait_ge(taken[d % 2], layer * (OUTS // 2) + d // 2 + 1)

        def key_w(m):
            if m < M_DIL:
                return P * (m % 2 + 1)
            if m < M_X:
                return NG * P * (m % 2 + 1)
            return M

        def logits_of(m):
            if M_DIL <= m < M_X:
                return ps[:, 2:4, :].rearrange("p b c -> p (b c)")[:, 0:key_w(m)]
            return ps[:, 2 + m % 2, 0:key_w(m)]

        block = ctx.enter_context(nc.Block())

        @block.sync
        def _(sp):
            sp.dma_start(h[:, :].rearrange("p (t d) -> p t d", t=TT),
                         a["x"][0].rearrange("(t p) d -> p t d", p=P)).then_inc(x_in, 16)
            stream = a["weights"]
            for r in range(RING):
                sp.dma_start(slot(raw, r), stream[r]).then_inc(raw_in[r], 16)
            with sp.Fori(1, DEPTH * UNITS // RING) as i:
                for r in range(RING):
                    sp.wait_ge(lo_made, i * RING + (r + 1 - RING))
                    sp.dma_start(slot(raw, r), stream[i * RING + r]).then_inc(raw_in[r], 16)
            sp.wait_ge(final_sem, TT)
            sp.dma_start(out[0].rearrange("(t p) d -> p t d", p=P), norm_x).then_inc(out_sent, 16)
            sp.wait_ge(out_sent, 16)

        @block.gpsimd
        def _(pool):
            for dst, name in ((ident, "c_ident"), (tri, "c_tri"), (strict, "c_strict"),
                              (strict_neg, "c_strict_neg"), (causal, "c_causal"), (flip, "c_flip"), (rope_cs, "c_rope")):
                pool.dma_start(dst[:, :], a[name]).then_inc(const_in, 16)
            pool.dma_start(work[0:BUCKETS, 0:BIAS_W], a["c_onehot"]).then_inc(const_in, 16)
            pool.dma_start(work[0:NG * HEADS, BIAS_W:2 * BIAS_W], a["c_window"]).then_inc(const_in, 16)
            pool.dma_start(work[0:BUCKETS, 2 * BIAS_W:2 * BIAS_W + NG * HEADS], a["rel_bias"]).then_inc(const_in, 16)
            pool.memset(minus1[:, :], -1.0).then_inc(setup_mem, 1)
            pool.memset(half_neg[:, :], -0.5).then_inc(setup_mem, 1)
            pool.wait_ge(setup_mem, 2)
            pool.wait_ge(bias_row, 1)
            pool.dma_start(bias_dram, work[0:NG * HEADS, 3 * BIAS_W:4 * BIAS_W]).then_inc(bias_out, 16)

            def wait(s, value):
                value = pool.compute_val(value)
                pool.wait_ge(setup_mem, 2)
                pool.wait_ge(s, value)

            def load_gain(layer, j, src):
                if j:
                    wait(x_normed, layer * (2 * NORMS) + 2 * j)
                pool.dma_start(gain, src.partition_broadcast(P)).then_inc(gain_in, 16)

            def rstd_of(n):
                for t in range(TT):
                    wait(sq_done, n + t + 1)
                    pool.tensor_scalar(mean[:, t:t + 1], sumsq[:, t:t + 1], 1.0 / D, EPS,
                                       ALU.mult, ALU.add).then_inc(mean_done, 1)
                    wait(mean_done, n + t + 1)
                    pool.tensor_tensor(rstd[:, t:t + 1], mean[:, t:t + 1], half_neg[:, 0:1],
                                       ALU.pow).then_inc(rstd_done, 1)

            with pool.Fori(0, DEPTH) as layer:
                load_gain(layer, N_FFN1, a["ffn1_norm"][layer])
                rstd_of(layer * (2 * NORMS) + 2 * N_FFN1)
                load_gain(layer, N_MIX, a["mix_norm"][layer])
                pool.dma_start(lat_gain[:, 0:Q_RANK], a["mla_q_norm"][layer].partition_broadcast(P)).then_inc(small_in, 16)
                pool.dma_start(lat_gain[:, Q_RANK:Q_RANK + KV_RANK],
                               a["mla_kv_norm"][layer].partition_broadcast(P)).then_inc(small_in, 16)
                pool.dma_start(gate_b[:, :], a["gate_bias"][layer]).then_inc(small_in, 16)
                rstd_of(layer * (2 * NORMS) + 2 * N_MIX)
                wait(x_turned, layer * (2 * NORMS) + 2 * N_MIX + 2)
                pool.dma_start(norm_x, a["mem"][0].rearrange("(t p) d -> p t d", p=P)).then_inc(mem_in, 16)
                load_gain(layer, N_MEM, a["mem_norm"][layer])
                wait(lat_sq, layer * 4 + 4)
                for c, rank in ((0, Q_RANK), (1, KV_RANK)):
                    pool.tensor_scalar(lat_ms[:, 2 * c:2 * c + 2], lat_ss[:, 2 * c:2 * c + 2], 1.0 / rank, EPS,
                                       ALU.mult, ALU.add).then_inc(lat_mean, 1)
                wait(lat_mean, layer * 2 + 2)
                pool.tensor_tensor(lat_rs[:, :], lat_ms[:, :], half_neg[:, :], ALU.pow).then_inc(lat_rstd, 1)

                step = [0]

                def tick(ins):
                    step[0] += 1
                    ins.then_inc(rope_step, 1)

                def settled():
                    wait(rope_step, layer * POOL_STEPS + step[0])

                def rotate(x1, x2, y1, y2, cos, sin, t):
                    tick(pool.tensor_tensor(t[0], x1, cos, ALU.mult))
                    tick(pool.tensor_tensor(t[1], x2, sin, ALU.mult))
                    tick(pool.tensor_tensor(t[2], x1, sin, ALU.mult))
                    tick(pool.tensor_tensor(t[3], x2, cos, ALU.mult))
                    settled()
                    tick(pool.tensor_tensor(y1, t[0], t[1], ALU.subtract))
                    tick(pool.tensor_tensor(y2, t[2], t[3], ALU.add))
                    settled()

                wait(kr_copied, layer + 1)
                kr = k_raw[:, :].rearrange("p (t c) -> p t c", t=TT)
                kp = k_pe[:, :].rearrange("p (t c) -> p t c", t=TT)
                tk = [rope_t[:, b, 0:TT * 16].rearrange("p (t c) -> p t c", t=TT) for b in range(4)]
                rotate(kr[:, :, 0:16], kr[:, :, 16:32], kp[:, :, 0:16], kp[:, :, 16:32], cosv, sinv, tk)
                for t in range(TT):
                    tick(pool.tensor_copy(k_cat[:, t, :, NOPE:QK],
                                          kp[:, t, :].unsqueeze(1).broadcast_to([P, HEADS, ROPE])))
                for d in (D_UQ + 2, D_UQ + 3):
                    wait(taken[d % 2], layer * (OUTS // 2) + d // 2 + 1)
                for t in range(TT):
                    tq = [rope_t[:, b, :].rearrange("p (h c) -> p h c", h=HEADS) for b in range(4)]
                    rotate(q_tok[:, t, :, NOPE:NOPE + 16], q_tok[:, t, :, NOPE + 16:QK],
                           q_tok[:, t, :, NOPE:NOPE + 16], q_tok[:, t, :, NOPE + 16:QK],
                           cosv[:, t, :].unsqueeze(1).broadcast_to([P, HEADS, 16]),
                           sinv[:, t, :].unsqueeze(1).broadcast_to([P, HEADS, 16]), tq)
                assert step[0] == POOL_STEPS
                rstd_of(layer * (2 * NORMS) + 2 * N_MEM)

                pool.wait_ge(bias_out, 16)
                for hd in range(HEADS):
                    if hd >= 2:
                        wait(logits_ps, layer * PIECES + M_DIL + 2 * (hd - 1))
                    src = bass.AP(tensor=bias_dram.tensor, offset=hd * BIAS_W,
                                  ap=[[1, P], [HEADS * BIAS_W, NG], [1, S]])
                    pool.dma_start(bias3[:, hd % 2], src).then_inc(bias_in[hd % 2], 16)

                for d in (D_BR + 10, D_BR + 11):
                    wait(taken[d % 2], layer * (OUTS // 2) + d // 2 + 1)
                load_gain(layer, N_XA, a["xattn_norm"][layer])
                rstd_of(layer * (2 * NORMS) + 2 * N_XA)
                load_gain(layer, N_FFN2, a["ffn2_norm"][layer])
                rstd_of(layer * (2 * NORMS) + 2 * N_FFN2)
                wait(x_normed, layer * (2 * NORMS) + 2 * NORMS)
            load_gain(DEPTH, 0, a["final_norm"])
            rstd_of(DEPTH * 2 * NORMS)

        @block.scalar
        def _(act):
            def split(layer, u, n):
                act.wait_ge(raw_in[n % RING], (layer * (UNITS // RING) + 1) * 16 + (u - n % RING) * (16 // RING))
                if not (isinstance(u, int) and u < RING):
                    act.wait_ge(unit_used, layer * UNITS + u - (RING - 1))
                act.activation(slot(w_hi, n), slot(raw, n), ACT.Copy).then_inc(hi_made, 1)

            done = [0]

            def ahead(layer, n):
                while done[0] < min(n, UNITS):
                    split(layer, done[0], done[0])
                    done[0] += 1

            def square(n, src):
                for t in range(TT):
                    if src is h:
                        s = h[:, t * D:(t + 1) * D]
                    else:
                        s = norm_x[:, t, :]
                    if t:
                        act.wait_ge(sq_done, n + t)
                    act.activation(junk, s, ACT.Square, accum_out=sumsq[:, t:t + 1]).then_inc(sq_done, 1)

            def norm_hi(n, dst, banks):
                for t in range(TT):
                    act.wait_ge(x_turned, n + t + 1)
                    for b in range(2):
                        o = dst[:, :].rearrange("p (k t) -> p k t", k=KT)[:, 4 * b:4 * b + 4, t * P:(t + 1) * P]
                        last = act.activation(o, ps[:, banks[2 * t + b], :].rearrange("p (k c) -> p k c", k=4), ACT.Copy)
                    last.then_inc(x_hi, 1)

            def norm(layer, j, r, u):
                n = layer * (2 * NORMS) + 2 * j
                act.wait_ge(resid, layer * (4 * RESIDUALS) + 4 * r + 1)
                square(n, h)
                ahead(layer, u + 2)
                norm_hi(n, u_hi, (4, 5, 6, 7))

            def ffn(layer, u0, f):
                def step(i, u, s):
                    act.wait_ge(unit_used, layer * UNITS + u + 1)
                    c = layer * (2 * FT) + f * FT
                    act.activation(silu_b(s), ps[:, 4 + s % 4, 0:S], ACT.Silu).then_inc(silu_done, 1)
                    act.wait_ge(prod_done, c + i + 1)
                    act.activation(prod_t(v_hi, s), prod_b(s), ACT.Copy).then_inc(prod_hi, 1)

                ahead(layer, u0 + 5)
                step(0, u0 + 1, 0)
                with act.Fori(0, 5) as t:
                    for s in range(4):
                        for j in range(3):
                            n = u0 + 5 + 3 * s + j
                            split(layer, t * 12 + n, n)
                        step(t * 4 + (1 + s), t * 12 + (u0 + 3 + 3 * s), 1 + s)
                done[0] += 60
                ahead(layer, u0 + FFN_UNITS)
                step(FT - 1, u0 + 63, FT - 1)

            act.wait_ge(const_in, 16 * 10)
            with act.Fori(0, DEPTH) as layer:
                done[0] = 0
                norm(layer, N_FFN1, 0, U_FFN1)
                ffn(layer, U_FFN1, 0)
                norm(layer, N_MIX, 1, U_LAT)

                def take(d, u, dst, src, **kw):
                    assert d % 2 == 0
                    ahead(layer, u + 5)
                    act.wait_ge(unit_used, layer * UNITS + u + 1)
                    act.activation(dst, src, kw.pop("func", ACT.Copy), **kw).then_inc(taken[0], 1)

                def take_f(d, u, dst, scale=1.0):
                    take(d, u, dst, ps[:, 0, 0:S], scale=scale)

                ahead(layer, U_KR + 4)
                act.wait_ge(unit_used, layer * UNITS + U_LAT + 4)
                for t in range(TT):
                    for c, (lo, hi) in enumerate(((0, Q_RANK), (Q_RANK, 512))):
                        if t + c:
                            act.wait_ge(lat_sq, layer * 4 + 2 * t + c)
                        act.activation(junk[:, 0:hi - lo], ps[:, 2 + t, lo:hi], ACT.Square,
                                       accum_out=lat_ss[:, 2 * c + t:2 * c + t + 1]).then_inc(lat_sq, 1)
                ahead(layer, U_SBQ + 4)
                for f in range(0, 4, 2):
                    take_f(D_SBQ + f, U_SBQ + f, sb_q[:, f, :], HD ** -0.5)
                for t in range(TT):
                    act.wait_ge(lat_turned, layer * TT + t + 1)
                    act.activation(v_hi[:, 0:4 * S].rearrange("p (k t) -> p k t", k=4)[:, :, t * P:(t + 1) * P],
                                   ps[:, 5 + t, :].rearrange("p (k c) -> p k c", k=4), ACT.Copy).then_inc(lat_hi, 1)
                for f in range(0, 4, 2):
                    take_f(D_SBK + f, U_SBK + f, sb_k[:, f, :])
                take(D_SBV, U_SBV + 3, sb_v[:, 0, :], ps[:, 0, :])
                for c in range(2):
                    take(D_UQ + 2 * c, U_UQ + 3 * c + 2, q_tok[:, 0, 4 * c:4 * c + 4, :],
                         ps[:, 0, 0:384].rearrange("p (h c) -> p h c", h=4), scale=QK ** -0.5)
                for c in range(2):
                    ahead(layer, U_UKV + 4)
                    act.wait_ge(ukv_done, layer * 3 + 2 * c + 1)
                    kv = ps[:, 0, :].rearrange("p (h c) -> p h c", h=4)
                    act.activation(k_cat[:, 0, 4 * c:4 * c + 4, 0:NOPE], kv[:, :, 0:NOPE], ACT.Copy)
                    act.activation(mv[:, 0, 256 * c:256 * c + 256].rearrange("p (h c) -> p h c", h=4),
                                   kv[:, :, NOPE:NOPE + HD], ACT.Copy).then_inc(taken[0], 1)

                def take_dil(u):
                    if u < U_DV:
                        i = u - U_DQK
                        g, part, f = i // 8, i % 8 // 4, i % 4
                        if i % 2 == 0:
                            take_f(D_DQK + i, u, (dq, dk)[part][:, g, f, :], (HD ** -0.5, 1.0)[part])
                    elif (u - U_DV) % 4 == 3:
                        g = (u - U_DV) // 4
                        take(D_DV + 2 * g, u, dv[:, g, 0, :], ps[:, 0, :])
                    ahead(layer, u + 5)

                for hd in range(HEADS + 1):
                    u = U_DQK + 2 * hd
                    n = layer * HEADS + hd
                    if hd < HEADS:
                        z = ps[:, 2 + hd % 2, 0:384]
                        act.wait_ge(z_done, n + 1)
                        if hd >= 2:
                            act.wait_ge(sp_done, n - 1)
                        act.activation(sb_soft(hd), z, ACT.Abs).then_inc(z_abs, 1)
                        act.wait_ge(z_abs, n + 1)
                        act.activation(sb_soft(hd), sb_soft(hd), ACT.Exp, scale=-1.0).then_inc(z_exp, 1)
                        act.wait_ge(z_exp, n + 1)
                        act.activation(sb_soft(hd), sb_soft(hd), ACT.Ln, bias=1.0).then_inc(z_ln, 1)
                    if hd >= 1:
                        act.wait_ge(stick_arg, n)
                        act.activation(sb_w(hd - 1), sb_w(hd - 1), ACT.Exp).then_inc(stick_w, 1)
                    take_dil(u)
                    if hd < HEADS:
                        take_dil(u + 1)

                act.wait_ge(mem_in, layer * 16 + 16)
                n = layer * (2 * NORMS) + 2 * N_MEM
                square(n, None)
                norm_hi(n, v_hi, (2, 3, 4, 5))

                def exp_piece(m):
                    act.wait_ge(negmax_done, layer * PIECES + m + 1)
                    if m >= 2:
                        act.wait_ge(probs_turned, layer * PIECES + m - 1)
                    act.activation(probs_sb(m)[:, 0:key_w(m)], logits_of(m), ACT.Exp, bias=p_negmax[:, m % 2:m % 2 + 1],
                                   accum_out=p_sum[:, m % 2:m % 2 + 1]).then_inc(probs_done, 1)

                for m in range(N_MLA + 1):
                    if m < N_MLA:
                        exp_piece(m)
                    take_dil(U_DQK + 2 * HEADS + 1 + m)
                for u in range(U_DQK + 2 * HEADS + 2 + N_MLA, U_GATE):
                    take_dil(u)

                def take_gate(u):
                    i = u - U_GATE
                    if i < 24:
                        if i % 2 == 0:
                            take(D_GATE + i, u, kt(sg, i), ps[:, 0, 0:S], func=ACT.Identity, bias=gate_b[:, i:i + 1])
                    elif i < 28:
                        if i % 2 == 0:
                            take_f(D_GATE + i, u, x_k[:, i - 24, :])
                    elif i == 31:
                        take(D_MV, u, x_v[:, 0, :], ps[:, 0, :])
                    ahead(layer, u + 5)

                act.wait_ge(small_in, layer * 48 + 48)
                for i in range(N_DIL + 1):
                    m = M_DIL + i
                    if i < N_DIL:
                        exp_piece(m)
                    if i >= 1:
                        act.wait_ge(probs_turned, layer * PIECES + m)
                        if m - 1 >= 2:
                            act.wait_ge(pv_done, layer * PIECES + m - 2)
                        w = min(key_w(m - 1), 512)
                        act.activation(probs_t(m - 1)[:, 0:w], ps[:, 4, 0:w], ACT.Copy).then_inc(probs_t_act, 1)
                    if i < N_DIL:
                        take_gate(U_GATE + 2 * i)
                        take_gate(U_GATE + 2 * i + 1)

                act.wait_ge(oa_copied, layer * 4 + 4)
                act.activation(u_hi[:, 0:4 * S], o_a[:, :], ACT.Copy).then_inc(o_hi, 1)
                out_taken(act, layer, D_GATE + 23)
                for b in range(3):
                    out_taken(act, layer, D_GATE + 22)
                    s = sg[:, b * KT * S:(b + 1) * KT * S]
                    act.activation(s, s, ACT.Sigmoid).then_inc(sig_done, 1)
                    if b:
                        ahead(layer, U_BR + 4 * b + RING)
                    if b < 2:
                        if b == 1:
                            act.wait_ge(unit_used, layer * UNITS + U_BR + 4)
                        for t in range(TT):
                            act.wait_ge(o_turned, layer * O_TURNS + 2 * b + t + 1)
                            o = u_hi[:, (1 - b) * 4 * S:(2 - b) * 4 * S].rearrange("p (k t) -> p k t", k=4)
                            act.activation(o[:, :, t * P:(t + 1) * P],
                                           ps[:, 4 + 2 * b + t, :].rearrange("p (k c) -> p k c", k=4),
                                           ACT.Copy).then_inc(o_hi, 1)
                for j in range(4):
                    ahead(layer, U_BR + 8 + j + 5)
                    act.wait_ge(merged_sum, layer * 8 + 4 + j + 1)
                    act.activation(v_hi[:, 512 * j:512 * j + 512], merged[:, j, :], ACT.Copy).then_inc(merged_hi, 1)
                ahead(layer, U_XQ)
                norm(layer, N_XA, 2, U_XQ)
                for f in range(0, 4, 2):
                    take_f(D_XQ + f, U_XQ + f, x_q[:, f, :], XD ** -0.5)
                ahead(layer, U_FFN2)
                for m in range(M_X, PIECES):
                    exp_piece(m)
                for t in range(TT):
                    act.wait_ge(o_turned, layer * O_TURNS + 4 + t + 1)
                    act.activation(v_hi[:, 0:4 * S].rearrange("p (k t) -> p k t", k=4)[:, :, t * P:(t + 1) * P],
                                   ps[:, 6 + t, :].rearrange("p (k c) -> p k c", k=4), ACT.Copy).then_inc(o_hi, 1)
                ahead(layer, U_FFN2)
                norm(layer, N_FFN2, 3, U_FFN2)
                ffn(layer, U_FFN2, 1)
                assert done[0] == UNITS
            act.wait_ge(resid, DEPTH * 4 * RESIDUALS + 1)
            square(DEPTH * 2 * NORMS, h)

        @block.vector
        def _(dve):
            def split(layer, u, n):
                dve.wait_ge(hi_made, layer * UNITS + u + 1)
                dve.tensor_tensor(slot(w_lo, n), slot(raw, n), slot(w_hi, n).bitcast(F32), ALU.subtract).then_inc(lo_made, 1)

            done = [0]

            def ahead(layer, n):
                while done[0] < min(n, UNITS):
                    split(layer, done[0], done[0])
                    done[0] += 1

            def rest(dst, src, hi, s, n=1):
                dve.tensor_tensor(dst, src, hi.bitcast(F32), ALU.subtract).then_inc(s, n)

            def normalise(n, src):
                for t in range(TT):
                    dve.wait_ge(rstd_done, n + t + 1)
                    dve.scalar_tensor_tensor(out=norm_x[:, t, :], in0=src(t), scalar=rstd[:, t:t + 1],
                                             in1=gain, op0=ALU.mult, op1=ALU.mult).then_inc(x_normed, 1)

            def norm_lo(n, hi, lo, banks):
                for t in range(TT):
                    dve.wait_ge(x_hi, n + t + 1)
                    for b in range(2):
                        def part(x):
                            return x[:, :].rearrange("p (k t) -> p k t", k=KT)[:, 4 * b:4 * b + 4, t * P:(t + 1) * P]
                        last = dve.tensor_tensor(part(lo), ps[:, banks[2 * t + b], :].rearrange("p (k c) -> p k c", k=4),
                                                 part(hi).bitcast(F32), ALU.subtract)
                    last.then_inc(x_lo, 1)

            def norm(layer, j, u):
                n = layer * (2 * NORMS) + 2 * j
                dve.wait_ge(gain_in, (layer * NORMS + j + 1) * 16)
                normalise(n, lambda t: h[:, t * D:(t + 1) * D])
                ahead(layer, u + 2)
                norm_lo(n, u_hi, u_lo, (4, 5, 6, 7))

            def residual(layer, u, scale):
                dve.wait_ge(unit_used, layer * UNITS + u + 1)
                for t in range(TT):
                    for c in range(2):
                        hh = h[:, t * D + 512 * c:t * D + 512 * c + 512]
                        dve.scalar_tensor_tensor(out=hh, in0=ps[:, 2 * t + c, :], scalar=scale, in1=hh,
                                                 op0=ALU.mult, op1=ALU.add).then_inc(resid, 1)

            def ffn(layer, u0, f):
                c = layer * (2 * FT) + f * FT

                def step(i, s):
                    dve.wait_ge(silu_done, c + i + 1)
                    dve.tensor_tensor(prod_b(s), ps[:, 4 + s % 4, S:2 * S], silu_b(s), ALU.mult).then_inc(prod_done, 1)
                    dve.wait_ge(prod_hi, c + i + 1)
                    rest(prod_t(v_lo, s), prod_b(s), prod_t(v_hi, s), prod_lo)

                ahead(layer, u0 + 5)
                step(0, 0)
                with dve.Fori(0, 5) as t:
                    for s in range(4):
                        for j in range(3):
                            n = u0 + 5 + 3 * s + j
                            split(layer, t * 12 + n, n)
                        step(t * 4 + (1 + s), 1 + s)
                done[0] += 60
                ahead(layer, u0 + FFN_UNITS)
                step(FT - 1, FT - 1)
                residual(layer, u0 + FFN_UNITS - 1, 0.5)

            dve.wait_ge(const_in, 16 * 10)
            dve.wait_ge(x_in, 16)
            dve.wait_ge(bias_mm, 1)
            dve.tensor_tensor(work[0:NG * HEADS, 3 * BIAS_W:4 * BIAS_W], ps[0:NG * HEADS, 0, 0:BIAS_W],
                              work[0:NG * HEADS, BIAS_W:2 * BIAS_W], ALU.add).then_inc(bias_row, 1)
            dve.wait_ge(bias_out, 16)
            dve.memset(p_max[:, :], 0.0).then_inc(resid, 1)
            with dve.Fori(0, DEPTH) as layer:
                done[0] = 0
                norm(layer, N_FFN1, U_FFN1)
                ffn(layer, U_FFN1, 0)
                norm(layer, N_MIX, U_LAT)

                def take(d, u, dst, src, op=None):
                    assert d % 2 == 1
                    ahead(layer, u + 5)
                    dve.wait_ge(unit_used, layer * UNITS + u + 1)
                    if op is None:
                        ins = dve.tensor_copy(dst, src)
                    else:
                        ins = dve.tensor_scalar(dst, src, op[1], None, op[0])
                    ins.then_inc(taken[1], 1)

                def take_f(d, u, dst, scale=None):
                    take(d, u, dst, ps[:, 1, 0:S], None if scale is None else (ALU.mult, scale))

                ahead(layer, U_KR + 4)
                dve.wait_ge(unit_used, layer * UNITS + U_KR + 1)
                dve.tensor_copy(k_raw[:, :], ps[:, 4, 0:TT * ROPE]).then_inc(kr_copied, 1)
                dve.wait_ge(small_in, layer * 48 + 48)
                dve.wait_ge(lat_rstd, layer + 1)
                for t in range(TT):
                    for c, (lo, hi) in enumerate(((0, Q_RANK), (Q_RANK, 512))):
                        last = dve.scalar_tensor_tensor(out=lat_n[:, t, lo:hi], in0=ps[:, 2 + t, lo:hi],
                                                        scalar=lat_rs[:, 2 * c + t:2 * c + t + 1],
                                                        in1=lat_gain[:, lo:hi], op0=ALU.mult, op1=ALU.mult)
                    last.then_inc(lat_normed, 1)
                for f in range(1, 4, 2):
                    take_f(D_SBQ + f, U_SBQ + f, sb_q[:, f, :], HD ** -0.5)
                for t in range(TT):
                    dve.wait_ge(lat_hi, layer * TT + t + 1)

                    def part(x):
                        return x[:, 0:4 * S].rearrange("p (k t) -> p k t", k=4)[:, :, t * P:(t + 1) * P]
                    rest(part(v_lo), ps[:, 5 + t, :].rearrange("p (k c) -> p k c", k=4), part(v_hi), lat_lo)
                for f in range(1, 4, 2):
                    take_f(D_SBK + f, U_SBK + f, sb_k[:, f, :])
                take(D_SBV + 1, U_SBV + 3, sb_v[:, 1, :], ps[:, 1, :])
                for c in range(2):
                    take(D_UQ + 2 * c + 1, U_UQ + 3 * c + 2, q_tok[:, 1, 4 * c:4 * c + 4, :],
                         ps[:, 1, 0:384].rearrange("p (h c) -> p h c", h=4), (ALU.mult, QK ** -0.5))
                for c in range(2):
                    ahead(layer, U_UKV + 4)
                    if c == 0:
                        dve.wait_ge(ukv_done, layer * 3 + 2)
                    else:
                        dve.wait_ge(unit_used, layer * UNITS + U_UKV + 1)
                    kv = ps[:, 1, :].rearrange("p (h c) -> p h c", h=4)
                    dve.tensor_copy(k_cat[:, 1, 4 * c:4 * c + 4, 0:NOPE], kv[:, :, 0:NOPE])
                    dve.tensor_copy(mv[:, 1, 256 * c:256 * c + 256].rearrange("p (h c) -> p h c", h=4),
                                    kv[:, :, NOPE:NOPE + HD]).then_inc(taken[1], 1)

                def take_dil(u):
                    if u < U_DV:
                        i = u - U_DQK
                        g, part, f = i // 8, i % 8 // 4, i % 4
                        if i % 2 == 1:
                            take_f(D_DQK + i, u, (dq, dk)[part][:, g, f, :], (HD ** -0.5, None)[part])
                    elif (u - U_DV) % 4 == 3:
                        g = (u - U_DV) // 4
                        take(D_DV + 2 * g + 1, u, dv[:, g, 1, :], ps[:, 1, :])
                    ahead(layer, u + 5)

                for hd in range(HEADS + 1):
                    u = U_DQK + 2 * hd
                    n = layer * HEADS + hd
                    if hd >= 1:
                        e = sb_w(hd - 1)
                        dve.wait_ge(stick_sum, n)
                        if hd - 1 >= 2:
                            dve.wait_ge(stick_o, n - 2)
                        dve.tensor_tensor(e, ps[:, 2 + (hd - 1) % 2, 0:384], strict_neg[:, :], ALU.add).then_inc(stick_arg, 1)
                    if hd < HEADS:
                        dve.wait_ge(z_ln, n + 1)
                        if hd >= 2:
                            dve.wait_ge(stick_sum, n - 1)
                        dve.scalar_tensor_tensor(out=sb_sp(hd), in0=ps[:, 2 + hd % 2, 0:384], scalar=0.0,
                                                 in1=sb_soft(hd), op0=ALU.max, op1=ALU.add).then_inc(sp_done, 1)
                        dve.wait_ge(sp_done, n + 1)
                        diag = sb_sp(hd).rearrange("p (b c) -> p b c", b=3)[:, 0:3:2, :]
                        dve.tensor_tensor(diag, diag, strict[:, :].unsqueeze(1).broadcast_to([P, 2, P]),
                                          ALU.mult).then_inc(sp_masked, 1)
                    take_dil(u)
                    if hd >= 1 and hd % 2 == 0:
                        pair = (hd - 1) // 2
                        dve.wait_ge(stick_o, n)
                        dve.tensor_copy(oa[:, pair, :], ps[:, 4 + pair % 2, 0:S]).then_inc(oa_copied, 1)
                    if hd < HEADS:
                        dve.wait_ge(mla_turned, n + 1)
                        dst = (mk if hd < 4 else mq)[0:QK, 2 * (hd % 4):2 * (hd % 4) + 2, :]
                        dve.tensor_copy(dst, ps[0:QK, 6 + hd % 2, :].rearrange("p (h t) -> p h t", h=2)).then_inc(mla_copied, 1)
                        take_dil(u + 1)

                n = layer * (2 * NORMS) + 2 * N_MEM
                dve.wait_ge(gain_in, (layer * NORMS + N_MEM + 1) * 16)
                normalise(n, lambda t: norm_x[:, t, :])
                norm_lo(n, v_hi, v_lo, (2, 3, 4, 5))

                def soft_front(m):
                    base = layer * PIECES + m
                    dve.wait_ge(logits_ps, base + 1)
                    if m >= 2:
                        dve.wait_ge(probs_done, base - 1)
                    dve.reduce_max(p_max[:, m % 2:m % 2 + 1], logits_of(m), AX.X).then_inc(max_done, 1)
                    dve.wait_ge(max_done, base + 1)
                    dve.tensor_scalar(p_negmax[:, m % 2:m % 2 + 1], p_max[:, m % 2:m % 2 + 1], -1.0, None,
                                      ALU.mult).then_inc(negmax_done, 1)

                def soft_back(m):
                    base = layer * PIECES + m
                    w = key_w(m)
                    if m < M_DIL or m >= M_X or m % 2:
                        dve.wait_ge(probs_turned, base + 1)
                        if m >= 2:
                            dve.wait_ge(pv_done, base - 1)
                        if m < M_DIL or m >= M_X:
                            dve.tensor_copy(probs_t(m)[:, 0:w], ps[:, 4 + m % 2, 0:w]).then_inc(probs_t_dve, 1)
                        else:
                            dve.tensor_copy(probs_t(m)[:, 512:w], ps[:, 5, 0:w - 512]).then_inc(probs_t_dve, 1)
                    dve.wait_ge(probs_done, base + 1)
                    dve.reciprocal(p_inv[:, m % 2:m % 2 + 1], p_sum[:, m % 2:m % 2 + 1]).then_inc(inv_done, 1)

                def take_o(m):
                    base = layer * PIECES + m
                    if m < M_DIL:
                        t, c, dst = m % 2, HD * (m // 2), o_b
                        w = HD
                    elif m < M_X:
                        t, c, dst = m % 2, HD * ((m - M_DIL) // 2), o_c
                        w = HD
                    else:
                        t, c, dst = m % 2, XD * ((m - M_X) // 2), o_b
                        w = XD
                    dve.wait_ge(inv_done, base + 1)
                    dve.wait_ge(pv_done, base + 1)
                    dve.tensor_scalar(dst[:, t * WIDTH + c:t * WIDTH + c + w], ps[:, 6 + m % 2, 0:w],
                                      p_inv[:, m % 2:m % 2 + 1], None, ALU.mult).then_inc(o_taken, 1)

                for m in range(N_MLA + 1):
                    if m < N_MLA:
                        soft_front(m)
                    if m >= 1:
                        soft_back(m - 1)
                    take_dil(U_DQK + 2 * HEADS + 1 + m)
                    if m >= 1:
                        take_o(m - 1)
                for u in range(U_DQK + 2 * HEADS + 2 + N_MLA, U_GATE):
                    take_dil(u)

                def take_gate(u):
                    i = u - U_GATE
                    if i < 24:
                        if i % 2 == 1:
                            take(D_GATE + i, u, kt(sg, i), ps[:, 1, 0:S], (ALU.add, gate_b[:, i:i + 1]))
                    elif i < 28:
                        if i % 2 == 1:
                            take_f(D_GATE + i, u, x_k[:, i - 24, :])
                    elif i == 31:
                        take(D_MV + 1, u, x_v[:, 1, :], ps[:, 1, :])
                    ahead(layer, u + 5)

                for i in range(N_DIL + 1):
                    m = M_DIL + i
                    if i < N_DIL:
                        soft_front(m)
                    if i >= 1:
                        soft_back(m - 1)
                    if i < N_DIL:
                        take_gate(U_GATE + 2 * i)
                    if i >= 1:
                        take_o(m - 1)
                    if i < N_DIL:
                        take_gate(U_GATE + 2 * i + 1)

                dve.wait_ge(o_hi, layer * O_SPLITS + 1)
                rest(u_lo[:, 0:4 * S], o_a[:, :], u_hi[:, 0:4 * S], o_lo)
                for b in range(3):
                    if b < 2:
                        for t in range(TT):
                            dve.wait_ge(o_hi, layer * O_SPLITS + 1 + 2 * b + t + 1)

                            def part(x):
                                return x[:, (1 - b) * 4 * S:(2 - b) * 4 * S].rearrange(
                                    "p (k t) -> p k t", k=4)[:, :, t * P:(t + 1) * P]
                            rest(part(u_lo), ps[:, 4 + 2 * b + t, :].rearrange("p (k c) -> p k c", k=4), part(u_hi), o_lo)
                    dve.wait_ge(sig_done, layer * 3 + b + 1)
                    for j in range(4):
                        d = D_BR + 4 * b + j
                        u = U_BR + 4 * b + j
                        ahead(layer, u + 5)
                        dve.wait_ge(unit_used, layer * UNITS + u + 1)
                        g = sg[:, b * KT * S + 512 * j:b * KT * S + 512 * j + 512]
                        if b == 0:
                            dve.tensor_tensor(merged[:, j, :], ps[:, d % 2, :], g, ALU.mult).then_inc(taken[d % 2], 1)
                        else:
                            if 4 * b + j - 4 >= 2:
                                dve.wait_ge(merged_sum, layer * 8 + 4 * (b - 1) + j - 1)
                            dve.tensor_tensor(addend[:, j % 2, :], ps[:, d % 2, :], g, ALU.mult).then_inc(taken[d % 2], 1)
                            out_taken(dve, layer, d)
                        if b == 0:
                            continue
                        dve.tensor_tensor(merged[:, j, :], merged[:, j, :], addend[:, j % 2, :], ALU.add)\
                            .then_inc(merged_sum, 1)
                for j in range(4):
                    dve.wait_ge(merged_hi, layer * 4 + j + 1)
                    rest(v_lo[:, 512 * j:512 * j + 512], merged[:, j, :], v_hi[:, 512 * j:512 * j + 512], merged_lo)
                    ahead(layer, U_MIX + j + 4)
                ahead(layer, U_XQ)
                residual(layer, U_MIX + KT - 1, 1.0)
                norm(layer, N_XA, U_XQ)
                for f in range(1, 4, 2):
                    take_f(D_XQ + f, U_XQ + f, x_q[:, f, :], XD ** -0.5)
                ahead(layer, U_FFN2)
                for i in range(N_X + 1):
                    m = M_X + i
                    if i < N_X:
                        soft_front(m)
                    if i >= 1:
                        soft_back(m - 1)
                        take_o(m - 1)
                for t in range(TT):
                    dve.wait_ge(o_hi, layer * O_SPLITS + 5 + t + 1)

                    def part(x):
                        return x[:, 0:4 * S].rearrange("p (k t) -> p k t", k=4)[:, :, t * P:(t + 1) * P]
                    rest(part(v_lo), ps[:, 6 + t, :].rearrange("p (k c) -> p k c", k=4), part(v_hi), o_lo)
                ahead(layer, U_FFN2)
                residual(layer, U_XO + XH - 1, 1.0)
                norm(layer, N_FFN2, U_FFN2)
                ffn(layer, U_FFN2, 1)
                assert done[0] == UNITS
            dve.wait_ge(gain_in, (DEPTH * NORMS + 1) * 16)
            for t in range(TT):
                dve.wait_ge(rstd_done, DEPTH * 2 * NORMS + t + 1)
                dve.scalar_tensor_tensor(out=norm_x[:, t, :], in0=h[:, t * D:(t + 1) * D], scalar=rstd[:, t:t + 1],
                                         in1=gain, op0=ALU.mult, op1=ALU.mult).then_inc(final_sem, 1)

        @block.tensor
        def _(pe):
            def ready(layer, u):
                pe.wait_ge(lo_made, layer * UNITS + u + 1)

            def mm3(o, ah, al, bh, bl, first, last):
                pe.matmul(o, ah, bh, start=first, stop=False)
                pe.matmul(o, ah, bl, start=False, stop=False)
                return pe.matmul(o, al, bh, start=False, stop=last)

            def weights_still(o, n, j, c, x_hi_, x_lo_, k, first, last):
                w = slice(j * c, j * c + P)
                return mm3(o, slot(w_hi, n)[:, w], slot(w_lo, n)[:, w], kt(x_hi_, k), kt(x_lo_, k), first, last)

            def tokens_still(o, x_hi_, x_lo_, k, t, n, c0, c1, first, last):
                x = slice(k * S + t * P, k * S + t * P + P)
                return mm3(o, x_hi_[:, x], x_lo_[:, x], slot(w_hi, n)[:, c0:c1], slot(w_lo, n)[:, c0:c1], first, last)

            def feature_unit(layer, u, n, o, x_hi_, x_lo_):
                ready(layer, u)
                for k in range(KT):
                    last = weights_still(o, n, k, P, x_hi_, x_lo_, k, k == 0, k == KT - 1)
                last.then_inc(unit_used, 1)

            def bank_free(layer, d):
                if d >= 2:
                    pe.wait_ge(taken[d % 2], layer * (OUTS // 2) + d // 2)

            def feature_out(layer, d, u, x_hi_=u_hi, x_lo_=u_lo):
                bank_free(layer, d)
                feature_unit(layer, u, u, ps[:, d % 2, 0:S], x_hi_, x_lo_)

            def token_unit(layer, u, j, banks, x_hi_=u_hi, x_lo_=u_lo):
                ready(layer, u)
                for kk in range(2):
                    k = 2 * j + kk
                    for t in range(TT):
                        last = tokens_still(ps[:, banks[t], :], x_hi_, x_lo_, k, t, u, 512 * kk, 512 * kk + 512,
                                            k == 0, k == KT - 1)
                last.then_inc(unit_used, 1)

            def token_out(layer, d, u, j, x_hi_=u_hi, x_lo_=u_lo):
                if j == 0:
                    bank_free(layer, d)
                    bank_free(layer, d + 1)
                token_unit(layer, u, j, (d % 2, (d + 1) % 2), x_hi_, x_lo_)

            def row_unit(layer, u, n, x_hi_, x_lo_, k, first, last):
                ready(layer, u)
                for t in range(TT):
                    for c in range(2):
                        ins = tokens_still(ps[:, 2 * t + c, :], x_hi_, x_lo_, k, t, n, 512 * c, 512 * c + 512,
                                           first, last)
                ins.then_inc(unit_used, 1)

            def turn_norm(layer, j, banks):
                n = layer * (2 * NORMS) + 2 * j
                for t in range(TT):
                    pe.wait_ge(x_normed, n + t + 1)
                    for k in range(KT):
                        last = pe.transpose(ps[:, banks[2 * t + k // 4], P * (k % 4):P * (k % 4) + P],
                                            norm_x[:, t, k * P:(k + 1) * P], ident[:, :])
                    last.then_inc(x_turned, 1)

            def normed(layer, j):
                pe.wait_ge(x_lo, layer * (2 * NORMS) + 2 * j + 2)

            def ffn(layer, u0, f):
                c = layer * (2 * FT) + f * FT

                def gate_up(u, n, s):
                    for j in range(2):
                        feature_unit(layer, u + j, n + j, ps[:, 4 + s % 4, j * S:(j + 1) * S], u_hi, u_lo)

                def down(i, u, n, s, first, last):
                    pe.wait_ge(prod_lo, c + i + 1)
                    row_unit(layer, u, n, v_hi, v_lo, s % 4, first, last)

                gate_up(u0, u0, 0)
                gate_up(u0 + 2, u0 + 2, 1)
                down(0, u0 + 4, u0 + 4, 0, True, False)
                with pe.Fori(0, 5) as t:
                    for s in range(4):
                        n = u0 + 5 + 3 * s
                        gate_up(t * 12 + n, n, 2 + s)
                        down(t * 4 + (1 + s), t * 12 + (n + 2), n + 2, 1 + s, False, False)
                down(FT - 1, u0 + 65, u0 + 65, FT - 1, False, True)

            pe.wait_ge(const_in, 16 * 10)
            pe.wait_ge(setup_mem, 2)
            pe.matmul(ps[0:NG * HEADS, 0, 0:BIAS_W], work[0:BUCKETS, 2 * BIAS_W:2 * BIAS_W + NG * HEADS],
                      work[0:BUCKETS, 0:BIAS_W], start=True, stop=True).then_inc(bias_mm, 1)
            with pe.Fori(0, DEPTH) as layer:
                turn_norm(layer, N_FFN1, (4, 5, 6, 7))
                normed(layer, N_FFN1)
                ffn(layer, U_FFN1, 0)
                turn_norm(layer, N_MIX, (4, 5, 6, 7))
                normed(layer, N_MIX)

                for j in range(4):
                    token_unit(layer, U_LAT + j, j, (2, 3))
                ready(layer, U_KR)
                for t in range(TT):
                    for k in range(KT):
                        last = tokens_still(ps[:, 4, t * ROPE:(t + 1) * ROPE], u_hi, u_lo, k, t, U_KR,
                                            k * ROPE, (k + 1) * ROPE, k == 0, k == KT - 1)
                last.then_inc(unit_used, 1)
                for f in range(4):
                    feature_out(layer, D_SBQ + f, U_SBQ + f)
                for t in range(TT):
                    pe.wait_ge(lat_normed, layer * TT + t + 1)
                    for k in range(4):
                        last = pe.transpose(ps[:, 5 + t, k * P:(k + 1) * P], lat_n[:, t, k * P:(k + 1) * P], ident[:, :])
                    last.then_inc(lat_turned, 1)
                for f in range(4):
                    feature_out(layer, D_SBK + f, U_SBK + f)
                for j in range(4):
                    token_out(layer, D_SBV, U_SBV + j, j)
                pe.wait_ge(lat_lo, layer * TT + TT)
                for c in range(2):
                    d = D_UQ + 2 * c
                    bank_free(layer, d)
                    bank_free(layer, d + 1)
                    for k in range(3):
                        u = U_UQ + 3 * c + k
                        ready(layer, u)
                        for t in range(TT):
                            last = tokens_still(ps[:, t, 0:384], v_hi, v_lo, k, t, u, 0, 384, k == 0, k == 2)
                        last.then_inc(unit_used, 1)
                ready(layer, U_UKV)
                for c in range(2):
                    for t in range(TT):
                        bank_free(layer, D_UKV + 2 * c + t)
                        last = tokens_still(ps[:, t, :], v_hi, v_lo, 3, t, U_UKV, 512 * c, 512 * c + 512, True, True)
                        if c == 0 or t == 0:
                            last.then_inc(ukv_done, 1)
                last.then_inc(unit_used, 1)

                def dil_unit(u):
                    if u < U_DV:
                        feature_out(layer, D_DQK + u - U_DQK, u)
                    else:
                        g, j = divmod(u - U_DV, 4)
                        token_out(layer, D_DV + 2 * g, u, j)

                out_taken(pe, layer, D_SBV)
                out_taken(pe, layer, D_SBV + 1)
                for hd in range(HEADS + 1):
                    n = layer * HEADS + hd
                    u = U_DQK + 2 * hd
                    if hd < HEADS:
                        r = slice(HD * (hd % 2), HD * (hd % 2) + HD)
                        f = hd // 2
                        if hd >= 2:
                            pe.wait_ge(stick_arg, n - 1)
                        z = ps[:, 2 + hd % 2, :]
                        pe.matmul(z[:, 0:S], sb_k[r, f, 0:P], sb_q[r, f, :], start=True, stop=True)
                        pe.matmul(z[:, S:S + P], sb_k[r, f, P:S], sb_q[r, f, P:S], start=False, stop=True,
                                  skip_group_check=True).then_inc(z_done, 1)
                    if hd >= 1:
                        z = ps[:, 2 + (hd - 1) % 2, :]
                        sp_ = sb_sp(hd - 1)
                        pe.wait_ge(sp_masked, n)
                        pe.matmul(z[:, 0:S], tri[:, :], sp_[:, 0:S], start=False, stop=True, skip_group_check=True)
                        pe.matmul(z[:, P:S], minus1[:, :], sp_[:, S:S + P], start=False, stop=True,
                                  skip_group_check=True)
                        pe.matmul(z[:, S:S + P], tri[:, :], sp_[:, S:S + P], start=False, stop=True,
                                  skip_group_check=True).then_inc(stick_sum, 1)
                    dil_unit(u)
                    if hd >= 1:
                        g = hd - 1
                        r = slice(HD * (g % 2), HD * (g % 2) + HD)
                        o = ps[r, 4 + (g // 2) % 2, :]
                        pe.wait_ge(stick_w, n)
                        if g % 2 == 0 and g >= 4:
                            pe.wait_ge(oa_copied, layer * 4 + g // 2 - 1)
                        pe.matmul(o[:, 0:S], sb_v[:, 0, g * HD:(g + 1) * HD], sb_w(g)[:, 0:S], start=True, stop=False)
                        pe.matmul(o[:, P:S], sb_v[:, 1, g * HD:(g + 1) * HD], sb_w(g)[:, S:S + P], start=False,
                                  stop=True).then_inc(stick_o, 1)
                    if hd < HEADS:
                        src = k_cat if hd < 4 else q_tok
                        if hd == 0:
                            out_taken(pe, layer, D_UKV + 2)
                            out_taken(pe, layer, D_UKV + 3)
                            pe.wait_ge(rope_step, layer * POOL_STEPS + 8)
                        if hd == 4:
                            pe.wait_ge(rope_step, layer * POOL_STEPS + POOL_STEPS)
                        if hd >= 2:
                            pe.wait_ge(mla_copied, n - 1)
                        for x in range(2):
                            for t in range(TT):
                                last = pe.transpose(ps[0:QK, 6 + hd % 2, S * x + P * t:S * x + P * t + P],
                                                    src[:, t, 2 * (hd % 4) + x, :], ident[:, :])
                        last.then_inc(mla_turned, 1)
                        dil_unit(u + 1)

                pe.wait_ge(stick_arg, layer * HEADS + HEADS)
                pe.wait_ge(oa_copied, layer * 4 + 4)
                turn_norm(layer, N_MEM, (2, 3, 4, 5))
                normed(layer, N_MEM)
                pe.wait_ge(mla_copied, layer * HEADS + HEADS)

                def turn_probs(m):
                    base = layer * PIECES + m
                    pe.wait_ge(probs_done, base + 1)
                    src = probs_sb(m)
                    b0 = 4 if M_DIL <= m < M_X else 4 + m % 2
                    for b in range(key_w(m) // P):
                        last = pe.transpose(ps[:, b0 + b // 4, P * (b % 4):P * (b % 4) + P],
                                            src[:, P * b:P * b + P], ident[:, :])
                    last.then_inc(probs_turned, 1)

                def logits_free(m):
                    same = 1 if M_DIL <= m <= M_X else 2
                    if m >= same:
                        pe.wait_ge(probs_done, layer * PIECES + m - same + 1)

                def times_v(m, blocks, w):
                    base = layer * PIECES + m
                    pt_waits(pe, layer, m)
                    if m >= 2:
                        pe.wait_ge(o_taken, base - 1)
                    for i, (b, v) in enumerate(blocks):
                        last = pe.matmul(ps[:, 6 + m % 2, 0:w], probs_t(m)[:, P * b:P * b + P], v,
                                         start=(i == 0), stop=(i == len(blocks) - 1))
                    last.then_inc(pv_done, 1)

                for m in range(N_MLA + 1):
                    if m < N_MLA:
                        hd, t = divmod(m, 2)
                        logits_free(m)
                        z = logits_of(m)
                        pe.matmul(z, mq[0:QK, hd, t * P:(t + 1) * P], mk[0:QK, hd, 0:key_w(m)], start=True, stop=False)
                        pe.matmul(z[:, t * P:(t + 1) * P], ident[:, :], causal[:, :], start=False,
                                  stop=True).then_inc(logits_ps, 1)
                    if m >= 1:
                        turn_probs(m - 1)
                    dil_unit(U_DQK + 2 * HEADS + 1 + m)
                    if m >= 1:
                        hd, t = divmod(m - 1, 2)
                        times_v(m - 1, [(b, mv[:, b, hd * HD:(hd + 1) * HD]) for b in range(t + 1)], HD)
                for u in range(U_DQK + 2 * HEADS + 2 + N_MLA, U_GATE):
                    dil_unit(u)

                def gate_unit(u):
                    i = u - U_GATE
                    if i < 24:
                        feature_out(layer, D_GATE + i, u)
                    elif i < 28:
                        feature_out(layer, D_GATE + i, u, v_hi, v_lo)
                    else:
                        token_out(layer, D_MV, u, i - 28, v_hi, v_lo)

                out_taken(pe, layer, D_DV + 2 * NG - 2)
                out_taken(pe, layer, D_DV + 2 * NG - 1)
                for i in range(N_DIL + 1):
                    m = M_DIL + i
                    if i < N_DIL:
                        hd, t = divmod(i, 2)
                        r = slice(HD * (hd % 2), HD * (hd % 2) + HD)
                        kw = P * (t + 1)
                        logits_free(m)
                        if t == 0:
                            pe.wait_ge(bias_in[hd % 2], (layer * (HEADS // 2) + hd // 2 + 1) * 16)
                            pe.matmul(ps[:, 2, 0:NG * P].rearrange("p (g k) -> p g k", g=NG), flip[:, :],
                                      bias3[:, hd % 2, :, P:S], start=True, stop=False)
                        else:
                            pe.matmul(ps[:, 2, :].rearrange("p (g k) -> p g k", g=2), flip[:, :],
                                      bias3[:, hd % 2, 0:2, :], start=True, stop=False)
                            pe.matmul(ps[:, 3, 0:S], flip[:, :], bias3[:, hd % 2, 2, :], start=True, stop=False)
                        for g in range(NG):
                            c = g * kw
                            last = pe.matmul(ps[:, 2 + c // 512, c % 512:c % 512 + kw], dq[r, g, hd // 2, t * P:(t + 1) * P],
                                             dk[r, g, hd // 2, 0:kw], start=False, stop=(g == NG - 1 or c + kw == 512))
                        last.then_inc(logits_ps, 1)
                    if i >= 1:
                        turn_probs(m - 1)
                    if i < N_DIL:
                        gate_unit(U_GATE + 2 * i)
                    if i >= 1:
                        hd, t = divmod(i - 1, 2)
                        times_v(m - 1, [(g * (t + 1) + b, dv[:, g, b, hd * HD:(hd + 1) * HD])
                                        for g in range(NG) for b in range(t + 1)], HD)
                    if i < N_DIL:
                        gate_unit(U_GATE + 2 * i + 1)

                def turn_heads(n, src, banks):
                    for t in range(TT):
                        for k in range(4):
                            last = pe.transpose(ps[:, banks[t], k * P:(k + 1) * P],
                                                src[:, t * WIDTH + k * P:t * WIDTH + (k + 1) * P], ident[:, :])
                        last.then_inc(o_turned, 1)

                def branch(b):
                    for j in range(4):
                        d, u = D_BR + 4 * b + j, U_BR + 4 * b + j
                        bank_free(layer, d)
                        ready(layer, u)
                        for f in range(2):
                            for k in range(4):
                                c = k * 2 * P + f * P
                                x = slice((b % 2) * 4 * S + k * S, (b % 2) * 4 * S + (k + 1) * S)
                                last = mm3(ps[:, d % 2, f * S:(f + 1) * S], slot(w_hi, u)[:, c:c + P],
                                           slot(w_lo, u)[:, c:c + P], u_hi[:, x], u_lo[:, x], k == 0, k == 3)
                        last.then_inc(unit_used, 1)

                pe.wait_ge(o_taken, layer * PIECES + M_X)
                turn_heads(0, o_b, (4, 5))
                pe.wait_ge(o_lo, layer * O_SPLITS + 1)
                branch(0)
                turn_heads(2, o_c, (6, 7))
                pe.wait_ge(o_lo, layer * O_SPLITS + 3)
                branch(1)
                pe.wait_ge(o_lo, layer * O_SPLITS + 5)
                branch(2)
                out_taken(pe, layer, D_BR + 10)
                out_taken(pe, layer, D_BR + 11)
                for k in range(KT):
                    pe.wait_ge(merged_lo, layer * 4 + k // 2 + 1)
                    row_unit(layer, U_MIX + k, U_MIX + k, v_hi, v_lo, k, k == 0, k == KT - 1)

                turn_norm(layer, N_XA, (4, 5, 6, 7))
                normed(layer, N_XA)
                for f in range(4):
                    feature_out(layer, D_XQ + f, U_XQ + f)
                out_taken(pe, layer, D_XQ + 2)
                out_taken(pe, layer, D_XQ + 3)
                for i in range(N_X + 1):
                    m = M_X + i
                    if i < N_X:
                        hd, t = divmod(i, 2)
                        logits_free(m)
                        pe.matmul(ps[:, 2 + m % 2, 0:M], x_q[:, hd, t * P:(t + 1) * P], x_k[:, hd, :],
                                  start=True, stop=True).then_inc(logits_ps, 1)
                    if i >= 1:
                        turn_probs(m - 1)
                        hd, t = divmod(i - 1, 2)
                        times_v(m - 1, [(b, x_v[:, b, hd * XD:(hd + 1) * XD]) for b in range(2)], XD)
                pe.wait_ge(o_taken, layer * PIECES + PIECES)
                turn_heads(4, o_b, (6, 7))
                pe.wait_ge(o_lo, layer * O_SPLITS + 7)
                for k in range(XH):
                    row_unit(layer, U_XO + k, U_XO + k, v_hi, v_lo, k, k == 0, k == XH - 1)

                turn_norm(layer, N_FFN2, (4, 5, 6, 7))
                normed(layer, N_FFN2)
                ffn(layer, U_FFN2, 1)


_OUTS = [((1, S, D), "float32")]


def kernel(**inputs):
    import numpy as _np
    import concourse.bacc as _bacc
    from concourse import mybir as _mybir
    from concourse.bass_utils import run_bass_kernel_spmd as _run

    nc = _bacc.Bacc("TRN2", target_bir_lowering=False, num_devices=1)
    laid = {name: _np.asarray(value) for name, value in inputs.items()}
    weights = pack_weights({name: laid.pop(name) for name in STREAMED}, _np)
    laid["gate_bias"] = laid["gate_bias"].reshape(DEPTH, 24, P).transpose(0, 2, 1)
    laid.update(constants(), weights=weights)
    arrays, aps = {}, {}
    for name, value in laid.items():
        v = _np.ascontiguousarray(value)
        arrays[f"in_{name}"] = v
        aps[name] = nc.dram_tensor(f"in_{name}", v.shape, _mybir.dt.from_np(v.dtype), kind="ExternalInput").ap()
    out = nc.dram_tensor("out_0", _OUTS[0][0], _mybir.dt.float32, kind="ExternalOutput").ap()
    trunk(nc, aps, out)
    r = _run(nc, [arrays], core_ids=[0])
    return r.results[0]["out_0"]
```

```python
import math
from contextlib import ExitStack

import numpy as np
import concourse.bass as bass
from concourse import mybir

F32 = mybir.dt.float32
F32R = mybir.dt.float32r
ALU = mybir.AluOpType
ACT = mybir.ActivationFunctionType
AX = mybir.AxisListType

P = 128
D = 1024
S = 256
M = 256
DEPTH = 2
D_FF = 2816
KT = D // P
TT = S // P
FT = D_FF // P
EPS = 1e-6
NEG = -1e30
HEADS = 8
HD = 64
WIDTH = HEADS * HD
Q_RANK, KV_RANK, NOPE, ROPE = 384, 128, 64, 32
QK = NOPE + ROPE
GROUPS = ((128, 1), (512, 4), (2048, 16))
NG = len(GROUPS)
BUCKETS, MAX_DIST = 32, 2048
XH, XD = 4, 128
RING = 4

C_SBQ, C_SBK, C_SBV = 0, WIDTH, 2 * WIDTH
C_LAT = 3 * WIDTH
C_KR = C_LAT + Q_RANK + KV_RANK
C_DIL = C_KR + ROPE
C_GATE = C_DIL + 3 * NG * WIDTH

FFN_UNITS = 3 * FT
U_FFN1 = 0
U_LAT = U_FFN1 + FFN_UNITS
U_SBQ = U_LAT + KT
U_SBK = U_SBQ + 4
U_SBV = U_SBK + 4
U_UQ = U_SBV + 4
U_UKV = U_UQ + 3
U_DQK = U_UKV + 1
U_DV = U_DQK + 8 * NG
U_GATE = U_DV + 4 * NG
U_MK = U_GATE + 8 * 3
U_MV = U_MK + 4
U_BR = U_MV + 4
U_MIX = U_BR + 12
U_XQ = U_MIX + 8
U_XO = U_XQ + 4
U_FFN2 = U_XO + 4
UNITS = U_FFN2 + FFN_UNITS
assert UNITS % RING == 0 and (12 % RING) == 0

D_SBQ = 0
D_SBK = D_SBQ + 4
D_SBV = D_SBK + 4
D_UQ = D_SBV + 2
D_UKV = D_UQ + 4
D_DQK = D_UKV + 4
D_DV = D_DQK + 8 * NG
D_GATE = D_DV + 2 * NG
D_MK = D_GATE + 24
D_MV = D_MK + 4
D_BR = D_MV + 2
D_XQ = D_BR + 12
OUTS = D_XQ + 2
assert OUTS % 2 == 0

N_MLA, N_DIL, N_X = 2 * HEADS, 2 * HEADS, 2 * XH
M_DIL = N_MLA
M_X = M_DIL + N_DIL
PIECES = M_X + N_X
N_FFN1, N_MIX, N_MEM, N_XA, N_FFN2, NORMS = 0, 1, 2, 3, 4, 5
RESIDUALS = 4
LAG = 3
LAT = Q_RANK + KV_RANK + ROPE

BIAS_W = 384


def ffn_unit(i):
    return 2 * i if i < LAG else 2 * LAG + 3 * (i - LAG)


def down_unit(i):
    return 2 * LAG + 3 * i + 2 if i < FT - LAG else FFN_UNITS - FT + i


def constants():
    i = np.arange(P)
    key, query = i[:, None], i[None, :]
    strict = (key < query).astype(np.float32)
    block = np.where(strict > 0, 0.0, NEG).astype(np.float32)
    strict_neg = np.concatenate([block, np.zeros((P, P), np.float32), block], 1)
    causal = np.where(i[None, :] <= i[:, None], 0.0, NEG).astype(np.float32)
    tri = np.where(key >= query, -1.0, 0.0).astype(np.float32)
    half = ROPE // 2
    freqs = np.float32(10000.0) ** (-np.arange(half, dtype=np.float32) / np.float32(half))
    ang = np.arange(S, dtype=np.float32)[:, None] * freqs[None, :].astype(np.float32)
    cs = np.stack([np.cos(ang), np.sin(ang)], 1).astype(np.float32)
    cs = cs.reshape(TT, P, 2, half).transpose(1, 2, 0, 3).reshape(P, 2 * TT * half)
    dist = 255 - np.arange(BIAS_W)
    exact = BUCKETS // 2
    d = np.maximum(dist, exact).astype(np.float32)
    large = exact + (np.log(d / exact) / math.log(MAX_DIST / exact) * (BUCKETS - exact)).astype(np.int32)
    bucket = np.where(dist < exact, np.maximum(dist, 0), np.minimum(large, BUCKETS - 1))
    onehot = (bucket[None, :] == np.arange(BUCKETS)[:, None]).astype(np.float32)
    allowed = np.stack([(dist >= 0) & (dist % r == 0) & (dist // r <= w // r) for w, r in GROUPS])
    window = np.repeat(np.where(allowed, 0.0, NEG).astype(np.float32), HEADS, 0)
    return {
        "c_ident": np.eye(P, dtype=np.float32), "c_tri": tri, "c_strict": strict,
        "c_strict_neg": strict_neg, "c_flip": np.ascontiguousarray(np.eye(P, dtype=np.float32)[::-1]), "c_causal": causal, "c_rope": np.ascontiguousarray(cs),
        "c_onehot": onehot, "c_window": np.ascontiguousarray(window),
    }


def pack_weights(w, np):
    stream = np.zeros((DEPTH, UNITS, P, 1024), np.float32)

    def tiles(u, m, k0, k1, c0, c1):
        n = (k1 - k0) * (c1 - c0)
        part = m[:, k0 * P:k1 * P, c0:c1].reshape(DEPTH, k1 - k0, P, c1 - c0)
        stream[:, u, :, 0:n] = part.transpose(0, 2, 1, 3).reshape(DEPTH, P, n)

    def feature_major(u0, m, c, n):
        for j in range(n):
            tiles(u0 + j, m, 0, KT, c + P * j, c + P * j + P)

    def token_major(u0, m, c):
        for j in range(4):
            tiles(u0 + j, m, 2 * j, 2 * j + 2, c, c + 512)

    def rows(u0, m, n):
        for k in range(n):
            tiles(u0 + k, m, k, k + 1, 0, D)

    for u0, gate, up, down in ((U_FFN1, "ffn1_w_gate", "ffn1_w_up", "ffn1_w_down"),
                               (U_FFN2, "ffn2_w_gate", "ffn2_w_up", "ffn2_w_down")):
        for i in range(FT):
            u = u0 + ffn_unit(i)
            feature_major(u, w[gate], P * i, 1)
            feature_major(u + 1, w[up], P * i, 1)
            tiles(u0 + down_unit(i), w[down], i, i + 1, 0, D)
    w_in = w["w_in"]
    for k in range(KT):
        tiles(U_LAT + k, w_in, k, k + 1, C_LAT, C_LAT + LAT)
    feature_major(U_SBQ, w_in, C_SBQ, 8)
    token_major(U_SBV, w_in, C_SBV)
    for k in range(3):
        tiles(U_UQ + k, w["mla_w_uq"], k, k + 1, 0, 768)
    tiles(U_UKV, w["mla_w_ukv"], 0, 1, 0, 1024)
    for g in range(NG):
        feature_major(U_DQK + 8 * g, w_in, C_DIL + 3 * WIDTH * g, 8)
        token_major(U_DV + 4 * g, w_in, C_DIL + 3 * WIDTH * g + 2 * WIDTH)
    feature_major(U_GATE, w_in, C_GATE, 24)
    feature_major(U_MK, w["xattn_w_kv"], 0, 4)
    token_major(U_MV, w["xattn_w_kv"], XH * XD)
    for b, name in enumerate(("w_branch_a", "w_branch_b", "w_branch_c")):
        for j in range(4):
            tiles(U_BR + 4 * b + j, w[name], 0, 4, 2 * P * j, 2 * P * j + 2 * P)
    rows(U_MIX, w["w_mix_out"], KT)
    feature_major(U_XQ, w["xattn_w_q"], 0, 4)
    rows(U_XO, w["xattn_w_o"], XH)
    return stream.reshape(DEPTH * UNITS, P, 1024)


STREAMED = ("ffn1_w_gate", "ffn1_w_up", "ffn1_w_down", "w_in", "mla_w_uq", "mla_w_ukv", "w_branch_a",
            "w_branch_b", "w_branch_c", "w_mix_out", "xattn_w_q", "xattn_w_kv", "xattn_w_o",
            "ffn2_w_gate", "ffn2_w_up", "ffn2_w_down")


def trunk(nc, a, out):
    ctx = ExitStack()
    with ctx:
        def sb(name, n, dt=F32, parts=P):
            return ctx.enter_context(nc.sbuf_tensor(name, [parts, n], dt))

        def sem(name):
            return ctx.enter_context(nc.semaphore(name))

        raw = sb("raw", RING * 1024)
        w_hi = sb("w_hi", RING * 1024, F32R)
        w_lo = sb("w_lo", RING * 1024, F32R)
        u_hi = sb("u_hi", KT * S, F32R)
        u_lo = sb("u_lo", KT * S, F32R)
        v_hi = sb("v_hi", KT * S, F32R)
        v_lo = sb("v_lo", KT * S, F32R)
        h = sb("h", TT * D)
        dil_q = sb("dil_q", NG * 4 * S)
        dil_k = sb("dil_k", NG * 4 * S)
        dil_v = sb("dil_v", NG * TT * WIDTH)
        mla_q = sb("mla_q", HEADS * S)
        mla_k = sb("mla_k", HEADS * S)
        mla_v = sb("mla_v", TT * WIDTH)
        o_a = sb("o_a", 4 * S)
        o_b = sb("o_b", TT * WIDTH)
        o_c = sb("o_c", TT * WIDTH)
        sg = sb("sg", 3 * KT * S)
        work = sb("work", 3072)
        bias_sb = sb("bias_sb", 2 * NG * S)
        lat_gain = sb("lat_gain", Q_RANK + KV_RANK)
        ident = sb("ident", P)
        tri = sb("tri", P)
        minus1 = sb("minus1", P)
        strict = sb("strict", P)
        strict_neg = sb("strict_neg", 3 * P)
        causal = sb("causal", P)
        flip = sb("flip", P)
        rope_cs = sb("rope_cs", 2 * TT * 16)
        gate_b = sb("gate_b", 24)
        k_raw = sb("k_raw", TT * ROPE)
        k_pe = sb("k_pe", TT * ROPE)
        sumsq = sb("sumsq", 2 * TT)
        half_mean = sb("half_mean", TT)
        mean = sb("mean", TT)
        rstd = sb("rstd", TT)
        lat_ss = sb("lat_ss", 4)
        lat_ms = sb("lat_ms", 4)
        lat_rs = sb("lat_rs", 4)
        half_neg = sb("half_neg", 4)
        p_max = sb("p_max", 2)
        p_negmax = sb("p_negmax", 2)
        p_sum = sb("p_sum", 2)
        p_inv = sb("p_inv", 2)
        ps = ctx.enter_context(nc.psum_tensor("ps", [P, 8, 512], F32))
        bias_dram = nc.dram_tensor("bias_rows", (NG * HEADS, BIAS_W), F32, kind="Internal").ap()

        norm_x = sg[:, 0:2 * D].rearrange("p (t d) -> p t d", t=TT)
        gain = sg[:, 2 * D:3 * D]
        q_tok = sg[:, 3 * D:3 * D + 1536].rearrange("p (t h c) -> p t h c", t=TT, h=HEADS)
        k_cat = sg[:, 3 * D + 1536:6 * D].rearrange("p (t h c) -> p t h c", t=TT, h=HEADS)
        lat_n = mla_q[:, 0:TT * 512].rearrange("p (t c) -> p t c", t=TT)
        sb_q = dil_v[:, 0:4 * S].rearrange("p (f t) -> p f t", f=4)
        sb_k = dil_v[:, 4 * S:8 * S].rearrange("p (f t) -> p f t", f=4)
        sb_v = dil_v[:, 8 * S:12 * S].rearrange("p (t c) -> p t c", t=TT)
        dq = dil_q[:, :].rearrange("p (g f t) -> p g f t", g=NG, f=4)
        dk = dil_k[:, :].rearrange("p (g f t) -> p g f t", g=NG, f=4)
        dv = dil_v[:, :].rearrange("p (g t c) -> p g t c", g=NG, t=TT)
        mq = mla_q[:, :].rearrange("p (h t) -> p h t", h=HEADS)
        mk = mla_k[:, :].rearrange("p (h t) -> p h t", h=HEADS)
        mv = mla_v[:, :].rearrange("p (t c) -> p t c", t=TT)
        x_k = mla_q[:, 0:XH * M].rearrange("p (h t) -> p h t", h=XH)
        x_v = mla_q[:, XH * M:2 * XH * M].rearrange("p (t c) -> p t c", t=TT)
        x_q = mla_k[:, 0:XH * S].rearrange("p (h t) -> p h t", h=XH)
        oa = o_a[:, :].rearrange("p (f t) -> p f t", f=4)
        merged = dil_q[:, 0:KT * S].rearrange("p (j c) -> p j c", j=4)
        addend = dil_q[:, KT * S:KT * S + 1024].rearrange("p (b c) -> p b c", b=2)
        bias3 = bias_sb[:, :].rearrange("p (b g k) -> p b g k", b=2, g=NG)
        junk = bias_sb[:, 0:D].rearrange("p (b c) -> p b c", b=2)
        cosv = rope_cs[:, 0:TT * 16].rearrange("p (t c) -> p t c", t=TT)
        sinv = rope_cs[:, TT * 16:2 * TT * 16].rearrange("p (t c) -> p t c", t=TT)
        rope_t = work[:, 2304:2304 + 512].rearrange("p (b c) -> p b c", b=4)

        def probs_sb(m):
            return work[:, 768 * (m % 2):768 * (m % 2) + 768]

        def probs_t(m):
            return work[:, 1536 + 768 * (m % 2):1536 + 768 * (m % 2) + 768]

        def sb_soft(hd):
            return work[:, 384 * (hd % 2):384 * (hd % 2) + 384]

        def sb_sp(hd):
            return work[:, 768 + 384 * (hd % 2):768 + 384 * (hd % 2) + 384]

        def sb_w(hd):
            return work[:, 1536 + 384 * (hd % 2):1536 + 384 * (hd % 2) + 384]

        def silu_b(i):
            return work[:, S * (i % 2):S * (i % 2) + S]

        def prod_b(i):
            return work[:, 2 * S + S * (i % 2):2 * S + S * (i % 2) + S]

        def prod_t(t, i):
            return t[:, S * (i % 4):S * (i % 4) + S]

        def kt(t, k):
            return t[:, k * S:(k + 1) * S]

        def slot(t, u):
            return t[:, 1024 * (u % RING):1024 * (u % RING) + 1024]

        const_in = sem("const_in")
        x_in = sem("x_in")
        setup_mem = sem("setup_mem")
        bias_mm = sem("bias_mm")
        bias_row = sem("bias_row")
        bias_out = sem("bias_out")
        raw_in = [sem(f"raw_in{i}") for i in range(RING)]
        hi_made = sem("hi_made")
        lo_made = sem("lo_made")
        unit_used = sem("unit_used")
        taken = [sem("taken0"), sem("taken1")]
        gain_in = sem("gain_in")
        mem_in = sem("mem_in")
        small_in = sem("small_in")
        sq_done = sem("sq_done")
        mean_done = sem("mean_done")
        rstd_done = sem("rstd_done")
        x_normed = sem("x_normed")
        x_turned = sem("x_turned")
        x_hi = sem("x_hi")
        x_lo = sem("x_lo")
        y_part = sem("y_part")
        resid = sem("resid")
        silu_done = sem("silu_done")
        prod_done = sem("prod_done")
        prod_hi = sem("prod_hi")
        prod_lo = sem("prod_lo")
        lat_sq = sem("lat_sq")
        lat_mean = sem("lat_mean")
        lat_rstd = sem("lat_rstd")
        lat_normed = sem("lat_normed")
        lat_turned = sem("lat_turned")
        lat_hi = sem("lat_hi")
        lat_lo = sem("lat_lo")
        kr_copied = sem("kr_copied")
        rope_step = sem("rope_step")
        mla_turned = sem("mla_turned")
        mla_copied = sem("mla_copied")
        uq_done = sem("uq_done")
        ukv_done = sem("ukv_done")
        z_done = sem("z_done")
        z_abs = sem("z_abs")
        z_exp = sem("z_exp")
        z_ln = sem("z_ln")
        sp_done = sem("sp_done")
        sp_masked = sem("sp_masked")
        stick_sum = sem("stick_sum")
        stick_arg = sem("stick_arg")
        stick_w = sem("stick_w")
        stick_o = sem("stick_o")
        oa_copied = sem("oa_copied")
        bias_in = [sem("bias_in0"), sem("bias_in1")]
        logits_ps = sem("logits_ps")
        max_done = sem("max_done")
        negmax_done = sem("negmax_done")
        probs_done = sem("probs_done")
        probs_turned = sem("probs_turned")
        probs_t_act = sem("probs_t_act")
        probs_t_dve = sem("probs_t_dve")
        inv_done = sem("inv_done")
        pv_done = sem("pv_done")
        o_taken = sem("o_taken")
        o_turned = sem("o_turned")
        o_hi = sem("o_hi")
        o_lo = sem("o_lo")
        sig_done = sem("sig_done")
        merged_sum = sem("merged_sum")
        merged_hi = sem("merged_hi")
        merged_lo = sem("merged_lo")
        final_sem = sem("final_sem")
        out_sent = sem("out_sent")

        POOL_STEPS = 8 + 2 * 6
        O_SPLITS = 1 + 2 + 2 + 2
        O_TURNS = 6
        N_PT_DVE = N_MLA + N_DIL // 2 + N_X

        def pt_waits(eng, layer, m):
            if m < M_DIL:
                eng.wait_ge(probs_t_dve, layer * N_PT_DVE + m + 1)
            elif m < M_X:
                n = m - M_DIL
                eng.wait_ge(probs_t_act, layer * N_DIL + n + 1)
                if n % 2:
                    eng.wait_ge(probs_t_dve, layer * N_PT_DVE + N_MLA + n // 2 + 1)
            else:
                eng.wait_ge(probs_t_dve, layer * N_PT_DVE + N_MLA + N_DIL // 2 + m - M_X + 1)

        def out_taken(eng, layer, d):
            eng.wait_ge(taken[d % 2], layer * (OUTS // 2) + d // 2 + 1)

        def key_w(m):
            if m < M_DIL:
                return P * (m % 2 + 1)
            if m < M_X:
                return NG * P * (m % 2 + 1)
            return M

        def logits_of(m):
            if M_DIL <= m < M_X:
                return ps[:, 2:4, :].rearrange("p b c -> p (b c)")[:, 0:key_w(m)]
            return ps[:, 2 + m % 2, 0:key_w(m)]

        block = ctx.enter_context(nc.Block())

        @block.sync
        def _(sp):
            sp.dma_start(h[:, :].rearrange("p (t d) -> p t d", t=TT),
                         a["x"][0].rearrange("(t p) d -> p t d", p=P)).then_inc(x_in, 16)
            stream = a["weights"]
            for r in range(RING):
                sp.dma_start(slot(raw, r), stream[r]).then_inc(raw_in[r], 16)
            with sp.Fori(1, DEPTH * UNITS // RING) as i:
                for r in range(RING):
                    sp.wait_ge(lo_made, i * RING + (r + 1 - RING))
                    sp.dma_start(slot(raw, r), stream[i * RING + r]).then_inc(raw_in[r], 16)
            sp.wait_ge(final_sem, TT)
            sp.dma_start(out[0].rearrange("(t p) d -> p t d", p=P), norm_x).then_inc(out_sent, 16)
            sp.wait_ge(out_sent, 16)

        @block.gpsimd
        def _(pool):
            for dst, name in ((ident, "c_ident"), (tri, "c_tri"), (strict, "c_strict"),
                              (strict_neg, "c_strict_neg"), (causal, "c_causal"), (flip, "c_flip"), (rope_cs, "c_rope")):
                pool.dma_start(dst[:, :], a[name]).then_inc(const_in, 16)
            pool.dma_start(work[0:BUCKETS, 0:BIAS_W], a["c_onehot"]).then_inc(const_in, 16)
            pool.dma_start(work[0:NG * HEADS, BIAS_W:2 * BIAS_W], a["c_window"]).then_inc(const_in, 16)
            pool.dma_start(work[0:BUCKETS, 2 * BIAS_W:2 * BIAS_W + NG * HEADS], a["rel_bias"]).then_inc(const_in, 16)
            pool.memset(minus1[:, :], -1.0).then_inc(setup_mem, 1)
            pool.memset(half_neg[:, :], -0.5).then_inc(setup_mem, 1)
            pool.wait_ge(setup_mem, 2)
            pool.wait_ge(bias_row, 1)
            pool.dma_start(bias_dram, work[0:NG * HEADS, 3 * BIAS_W:4 * BIAS_W]).then_inc(bias_out, 16)

            def wait(s, value):
                value = pool.compute_val(value)
                pool.wait_ge(setup_mem, 2)
                pool.wait_ge(s, value)

            def load_gain(layer, j, src):
                if j:
                    wait(x_normed, layer * (4 * NORMS) + 4 * j)
                pool.dma_start(gain, src.partition_broadcast(P)).then_inc(gain_in, 16)

            def rstd_of(n):
                for t in range(TT):
                    wait(sq_done, n * 4 + 2 * t + 1)
                    pool.tensor_scalar(half_mean[:, t:t + 1], sumsq[:, 2 * t:2 * t + 1], 1.0 / D, EPS,
                                       ALU.mult, ALU.add).then_inc(mean_done, 1)
                    wait(mean_done, n * 4 + 2 * t + 1)
                    wait(sq_done, n * 4 + 2 * t + 2)
                    pool.tensor_scalar(mean[:, t:t + 1], sumsq[:, 2 * t + 1:2 * t + 2], 1.0 / D,
                                       half_mean[:, t:t + 1], ALU.mult, ALU.add).then_inc(mean_done, 1)
                    wait(mean_done, n * 4 + 2 * t + 2)
                    pool.tensor_tensor(rstd[:, t:t + 1], mean[:, t:t + 1], half_neg[:, 0:1],
                                       ALU.pow).then_inc(rstd_done, 1)

            with pool.Fori(0, DEPTH) as layer:
                load_gain(layer, N_FFN1, a["ffn1_norm"][layer])
                rstd_of(layer * NORMS + N_FFN1)
                load_gain(layer, N_MIX, a["mix_norm"][layer])
                pool.dma_start(lat_gain[:, 0:Q_RANK], a["mla_q_norm"][layer].partition_broadcast(P)).then_inc(small_in, 16)
                pool.dma_start(lat_gain[:, Q_RANK:Q_RANK + KV_RANK],
                               a["mla_kv_norm"][layer].partition_broadcast(P)).then_inc(small_in, 16)
                pool.dma_start(gate_b[:, :], a["gate_bias"][layer]).then_inc(small_in, 16)
                rstd_of(layer * NORMS + N_MIX)
                wait(x_turned, layer * (4 * NORMS) + 4 * N_MIX + 4)
                pool.dma_start(norm_x, a["mem"][0].rearrange("(t p) d -> p t d", p=P)).then_inc(mem_in, 16)
                load_gain(layer, N_MEM, a["mem_norm"][layer])
                wait(lat_sq, layer * 4 + 4)
                for c, rank in ((0, Q_RANK), (1, KV_RANK)):
                    pool.tensor_scalar(lat_ms[:, 2 * c:2 * c + 2], lat_ss[:, 2 * c:2 * c + 2], 1.0 / rank, EPS,
                                       ALU.mult, ALU.add).then_inc(lat_mean, 1)
                wait(lat_mean, layer * 2 + 2)
                pool.tensor_tensor(lat_rs[:, :], lat_ms[:, :], half_neg[:, :], ALU.pow).then_inc(lat_rstd, 1)

                step = [0]

                def tick(ins):
                    step[0] += 1
                    ins.then_inc(rope_step, 1)

                def settled():
                    wait(rope_step, layer * POOL_STEPS + step[0])

                def rotate(x1, x2, y1, y2, cos, sin, t):
                    tick(pool.tensor_tensor(t[0], x1, cos, ALU.mult))
                    tick(pool.tensor_tensor(t[1], x2, sin, ALU.mult))
                    tick(pool.tensor_tensor(t[2], x1, sin, ALU.mult))
                    tick(pool.tensor_tensor(t[3], x2, cos, ALU.mult))
                    settled()
                    tick(pool.tensor_tensor(y1, t[0], t[1], ALU.subtract))
                    tick(pool.tensor_tensor(y2, t[2], t[3], ALU.add))
                    settled()

                wait(kr_copied, layer * TT + TT)
                kr = k_raw[:, :].rearrange("p (t c) -> p t c", t=TT)
                kp = k_pe[:, :].rearrange("p (t c) -> p t c", t=TT)
                tk = [rope_t[:, b, 0:TT * 16].rearrange("p (t c) -> p t c", t=TT) for b in range(4)]
                rotate(kr[:, :, 0:16], kr[:, :, 16:32], kp[:, :, 0:16], kp[:, :, 16:32], cosv, sinv, tk)
                for t in range(TT):
                    tick(pool.tensor_copy(k_cat[:, t, :, NOPE:QK],
                                          kp[:, t, :].unsqueeze(1).broadcast_to([P, HEADS, ROPE])))
                for d in (D_UQ + 2, D_UQ + 3):
                    wait(taken[d % 2], layer * (OUTS // 2) + d // 2 + 1)
                for t in range(TT):
                    tq = [rope_t[:, b, :].rearrange("p (h c) -> p h c", h=HEADS) for b in range(4)]
                    rotate(q_tok[:, t, :, NOPE:NOPE + 16], q_tok[:, t, :, NOPE + 16:QK],
                           q_tok[:, t, :, NOPE:NOPE + 16], q_tok[:, t, :, NOPE + 16:QK],
                           cosv[:, t, :].unsqueeze(1).broadcast_to([P, HEADS, 16]),
                           sinv[:, t, :].unsqueeze(1).broadcast_to([P, HEADS, 16]), tq)
                assert step[0] == POOL_STEPS
                rstd_of(layer * NORMS + N_MEM)

                pool.wait_ge(bias_out, 16)
                for hd in range(HEADS):
                    if hd >= 2:
                        wait(logits_ps, layer * PIECES + M_DIL + 2 * (hd - 1))
                    src = bass.AP(tensor=bias_dram.tensor, offset=hd * BIAS_W,
                                  ap=[[1, P], [HEADS * BIAS_W, NG], [1, S]])
                    pool.dma_start(bias3[:, hd % 2], src).then_inc(bias_in[hd % 2], 16)

                for d in (D_BR + 10, D_BR + 11):
                    wait(taken[d % 2], layer * (OUTS // 2) + d // 2 + 1)
                load_gain(layer, N_XA, a["xattn_norm"][layer])
                rstd_of(layer * NORMS + N_XA)
                load_gain(layer, N_FFN2, a["ffn2_norm"][layer])
                rstd_of(layer * NORMS + N_FFN2)
                wait(x_normed, layer * (4 * NORMS) + 4 * NORMS)
            load_gain(DEPTH, 0, a["final_norm"])
            rstd_of(DEPTH * NORMS)

        @block.scalar
        def _(act):
            def split(layer, u, n):
                act.wait_ge(raw_in[n % RING], (layer * (UNITS // RING) + 1) * 16 + (u - n % RING) * (16 // RING))
                if not (isinstance(u, int) and u < RING):
                    act.wait_ge(unit_used, layer * UNITS + u - (RING - 1))
                act.activation(slot(w_hi, n), slot(raw, n), ACT.Copy).then_inc(hi_made, 1)

            done = [0]

            def ahead(layer, n):
                while done[0] < min(n, UNITS):
                    split(layer, done[0], done[0])
                    done[0] += 1

            def square(n, t, resid_at=None):
                for b in range(2):
                    if resid_at is None:
                        x = norm_x[:, t, 512 * b:512 * b + 512]
                    else:
                        x = h[:, t * D + 512 * b:t * D + 512 * b + 512]
                        act.wait_ge(resid, resid_at + 2 * t + b + 1)
                    if t:
                        act.wait_ge(sq_done, n * 4 + b + 1)
                    act.activation(junk[:, b], x, ACT.Square,
                                   accum_out=sumsq[:, 2 * t + b:2 * t + b + 1]).then_inc(sq_done, 1)

            def norm_hi(n, t, dst, banks):
                for b in range(2):
                    act.wait_ge(x_turned, n * 4 + 2 * t + b + 1)
                    o = dst[:, :].rearrange("p (k t) -> p k t", k=KT)[:, 4 * b:4 * b + 4, t * P:(t + 1) * P]
                    act.activation(o, ps[:, banks[2 * t + b], :].rearrange("p (k c) -> p k c", k=4),
                                   ACT.Copy).then_inc(x_hi, 1)

            def norm(layer, j, r, u):
                n = layer * NORMS + j
                square(n, 0, layer * (4 * RESIDUALS) + 4 * r)
                ahead(layer, u + 1)
                norm_hi(n, 0, u_hi, (4, 5, 6, 7))
                square(n, 1, layer * (4 * RESIDUALS) + 4 * r)
                ahead(layer, u + RING)
                norm_hi(n, 1, u_hi, (4, 5, 6, 7))

            def ffn(layer, u0, f):
                def step(i, s):
                    u = u0 + ffn_unit(i) + 1 if isinstance(i, int) else i * 3 + (u0 - LAG + 1)
                    act.wait_ge(unit_used, layer * UNITS + u + 1)
                    c = layer * (2 * FT) + f * FT
                    act.activation(silu_b(s), ps[:, 4 + s % 4, 0:S], ACT.Silu).then_inc(silu_done, 1)
                    act.wait_ge(prod_done, c + i + 1)
                    act.activation(prod_t(v_hi, s), prod_b(s), ACT.Copy).then_inc(prod_hi, 1)

                for i in range(LAG):
                    ahead(layer, u0 + 3 * i + LAG)
                    step(i, i)
                with act.Fori(0, 4) as t:
                    for s in range(4):
                        for j in range(3):
                            n = u0 + 3 * (LAG + s) + j
                            split(layer, t * 12 + n, n)
                        step(t * 4 + (LAG + s), LAG + s)
                done[0] += 48
                for i in range(LAG + 16, FT):
                    ahead(layer, u0 + 3 * i + LAG)
                    step(i, i)

            act.wait_ge(const_in, 16 * 10)
            with act.Fori(0, DEPTH) as layer:
                done[0] = 0
                norm(layer, N_FFN1, 0, U_FFN1)
                ffn(layer, U_FFN1, 0)
                norm(layer, N_MIX, 1, U_LAT)

                def take(d, u, dst, src, **kw):
                    assert d % 2 == 0
                    ahead(layer, u + 4)
                    act.wait_ge(unit_used, layer * UNITS + u + 1)
                    act.activation(dst, src, kw.pop("func", ACT.Copy), **kw).then_inc(taken[0], 1)
                    ahead(layer, u + 5)

                def take_f(d, u, dst, scale=1.0):
                    take(d, u, dst, ps[:, 0, 0:S], scale=scale)

                ahead(layer, U_SBQ + 3)
                act.wait_ge(unit_used, layer * UNITS + U_SBQ)
                for t in range(TT):
                    for c, (bank, w) in enumerate(((2, Q_RANK), (3, KV_RANK))):
                        if t:
                            act.wait_ge(lat_sq, layer * 4 + c + 1)
                        act.activation(junk[:, c, 0:w], ps[:, bank + 2 * t, 0:w], ACT.Square,
                                       accum_out=lat_ss[:, 2 * c + t:2 * c + t + 1]).then_inc(lat_sq, 1)
                ahead(layer, U_SBQ + 4)
                for f in range(0, 4, 2):
                    take_f(D_SBQ + f, U_SBQ + f, sb_q[:, f, :], HD ** -0.5)
                for t in range(TT):
                    act.wait_ge(lat_turned, layer * TT + t + 1)
                    act.activation(v_hi[:, 0:4 * S].rearrange("p (k t) -> p k t", k=4)[:, :, t * P:(t + 1) * P],
                                   ps[:, 6 + t, :].rearrange("p (k c) -> p k c", k=4), ACT.Copy).then_inc(lat_hi, 1)
                for f in range(0, 4, 2):
                    take_f(D_SBK + f, U_SBK + f, sb_k[:, f, :])
                take(D_SBV, U_SBV + 3, sb_v[:, 0, :], ps[:, 0, :])
                for c in range(2):
                    ahead(layer, U_UQ + RING)
                    if c == 0:
                        act.wait_ge(uq_done, layer * 3 + 1)
                    else:
                        act.wait_ge(uq_done, layer * 3 + 3)
                    act.activation(q_tok[:, 0, 4 * c:4 * c + 4, :],
                                   ps[:, 0, 0:384].rearrange("p (h c) -> p h c", h=4), ACT.Copy,
                                   scale=QK ** -0.5).then_inc(taken[0], 1)
                for c in range(2):
                    ahead(layer, U_UKV + 4)
                    act.wait_ge(ukv_done, layer * 3 + 2 * c + 1)
                    kv = ps[:, 0, :].rearrange("p (h c) -> p h c", h=4)
                    act.activation(k_cat[:, 0, 4 * c:4 * c + 4, 0:NOPE], kv[:, :, 0:NOPE], ACT.Copy)
                    act.activation(mv[:, 0, 256 * c:256 * c + 256].rearrange("p (h c) -> p h c", h=4),
                                   kv[:, :, NOPE:NOPE + HD], ACT.Copy).then_inc(taken[0], 1)

                def take_dil(u):
                    if u < U_DV:
                        i = u - U_DQK
                        g, part, f = i // 8, i % 8 // 4, i % 4
                        if i % 2 == 0:
                            take_f(D_DQK + i, u, (dq, dk)[part][:, g, f, :], (HD ** -0.5, 1.0)[part])
                    elif (u - U_DV) % 4 == 3:
                        g = (u - U_DV) // 4
                        take(D_DV + 2 * g, u, dv[:, g, 0, :], ps[:, 0, :])
                    ahead(layer, u + 5)

                for hd in range(HEADS + 1):
                    u = U_DQK + 2 * hd
                    n = layer * HEADS + hd
                    if hd < HEADS:
                        z = ps[:, 2 + hd % 2, 0:384]
                        act.wait_ge(z_done, n + 1)
                        if hd >= 2:
                            act.wait_ge(sp_done, n - 1)
                        act.activation(sb_soft(hd), z, ACT.Abs).then_inc(z_abs, 1)
                        act.wait_ge(z_abs, n + 1)
                        act.activation(sb_soft(hd), sb_soft(hd), ACT.Exp, scale=-1.0).then_inc(z_exp, 1)
                        act.wait_ge(z_exp, n + 1)
                        act.activation(sb_soft(hd), sb_soft(hd), ACT.Ln, bias=1.0).then_inc(z_ln, 1)
                    if hd >= 1:
                        act.wait_ge(stick_arg, n)
                        act.activation(sb_w(hd - 1), sb_w(hd - 1), ACT.Exp).then_inc(stick_w, 1)
                    take_dil(u)
                    if hd < HEADS:
                        take_dil(u + 1)
                    if hd == HEADS - 3:
                        act.wait_ge(mem_in, layer * 16 + 16)
                        for t in range(TT):
                            square(layer * NORMS + N_MEM, t)

                for t in range(TT):
                    norm_hi(layer * NORMS + N_MEM, t, v_hi, (2, 3, 4, 5))
                take_dil(U_DQK + 2 * HEADS + 1)

                def exp_piece(m):
                    act.wait_ge(negmax_done, layer * PIECES + m + 1)
                    if m >= 2:
                        act.wait_ge(probs_turned, layer * PIECES + m - 1)
                    act.activation(probs_sb(m)[:, 0:key_w(m)], logits_of(m), ACT.Exp, bias=p_negmax[:, m % 2:m % 2 + 1],
                                   accum_out=p_sum[:, m % 2:m % 2 + 1]).then_inc(probs_done, 1)

                for m in range(N_MLA + 1):
                    if m < N_MLA:
                        exp_piece(m)
                    take_dil(U_DQK + 2 * HEADS + 2 + m)
                for u in range(U_DQK + 2 * HEADS + 3 + N_MLA, U_GATE):
                    take_dil(u)

                def take_gate(u):
                    i = u - U_GATE
                    if i < 24:
                        if i % 2 == 0:
                            take(D_GATE + i, u, kt(sg, i), ps[:, 0, 0:S], func=ACT.Identity, bias=gate_b[:, i:i + 1])
                    elif i < 28:
                        if i % 2 == 0:
                            take_f(D_GATE + i, u, x_k[:, i - 24, :])
                    elif i == 31:
                        take(D_MV, u, x_v[:, 0, :], ps[:, 0, :])
                    ahead(layer, u + 5)

                act.wait_ge(small_in, layer * 48 + 48)
                for i in range(N_DIL + 1):
                    m = M_DIL + i
                    if i < N_DIL:
                        exp_piece(m)
                    if i >= 1:
                        act.wait_ge(probs_turned, layer * PIECES + m)
                        if m - 1 >= 2:
                            act.wait_ge(pv_done, layer * PIECES + m - 2)
                        w = min(key_w(m - 1), 512)
                        act.activation(probs_t(m - 1)[:, 0:w], ps[:, 4, 0:w], ACT.Copy).then_inc(probs_t_act, 1)
                    if i < N_DIL:
                        take_gate(U_GATE + 2 * i)
                        take_gate(U_GATE + 2 * i + 1)

                act.wait_ge(oa_copied, layer * 4 + 4)
                act.activation(u_hi[:, 0:4 * S], o_a[:, :], ACT.Copy).then_inc(o_hi, 1)
                out_taken(act, layer, D_GATE + 23)
                for b in range(3):
                    out_taken(act, layer, D_GATE + 22)
                    s = sg[:, b * KT * S:(b + 1) * KT * S]
                    act.activation(s, s, ACT.Sigmoid).then_inc(sig_done, 1)
                    if b:
                        ahead(layer, U_BR + 4 * b + RING)
                    if b < 2:
                        if b == 1:
                            act.wait_ge(unit_used, layer * UNITS + U_BR + 4)
                        for t in range(TT):
                            act.wait_ge(o_turned, layer * O_TURNS + 2 * b + t + 1)
                            o = u_hi[:, (1 - b) * 4 * S:(2 - b) * 4 * S].rearrange("p (k t) -> p k t", k=4)
                            act.activation(o[:, :, t * P:(t + 1) * P],
                                           ps[:, 4 + 2 * b + t, :].rearrange("p (k c) -> p k c", k=4),
                                           ACT.Copy).then_inc(o_hi, 1)
                for j in range(4):
                    ahead(layer, U_BR + 8 + j + 5)
                    act.wait_ge(merged_sum, layer * 8 + 4 + j + 1)
                    act.activation(v_hi[:, 512 * j:512 * j + 512], merged[:, j, :], ACT.Copy).then_inc(merged_hi, 1)
                ahead(layer, U_XQ)
                norm(layer, N_XA, 2, U_XQ)
                take(D_XQ, U_XQ + 3, x_q[:, 0:4:2, :], ps[:, 0, :].rearrange("p (f t) -> p f t", f=2), scale=XD ** -0.5)
                ahead(layer, U_FFN2)
                for m in range(M_X, PIECES):
                    exp_piece(m)
                for t in range(TT):
                    act.wait_ge(o_turned, layer * O_TURNS + 4 + t + 1)
                    act.activation(v_hi[:, 0:4 * S].rearrange("p (k t) -> p k t", k=4)[:, :, t * P:(t + 1) * P],
                                   ps[:, 6 + t, :].rearrange("p (k c) -> p k c", k=4), ACT.Copy).then_inc(o_hi, 1)
                ahead(layer, U_FFN2)
                norm(layer, N_FFN2, 3, U_FFN2)
                ffn(layer, U_FFN2, 1)
                assert done[0] == UNITS
            for t in range(TT):
                square(DEPTH * NORMS, t, DEPTH * 4 * RESIDUALS)

        @block.vector
        def _(dve):
            def split(layer, u, n):
                dve.wait_ge(hi_made, layer * UNITS + u + 1)
                dve.tensor_tensor(slot(w_lo, n), slot(raw, n), slot(w_hi, n).bitcast(F32), ALU.subtract).then_inc(lo_made, 1)

            done = [0]

            def ahead(layer, n):
                while done[0] < min(n, UNITS):
                    split(layer, done[0], done[0])
                    done[0] += 1

            def rest(dst, src, hi, s, n=1):
                dve.tensor_tensor(dst, src, hi.bitcast(F32), ALU.subtract).then_inc(s, n)

            def normalise(n, t, src, dst=None):
                dve.wait_ge(rstd_done, n * TT + t + 1)
                for b in range(2):
                    w = slice(512 * b, 512 * b + 512)
                    dve.scalar_tensor_tensor(out=norm_x[:, t, w], in0=src[:, w], scalar=rstd[:, t:t + 1],
                                             in1=gain[:, w], op0=ALU.mult, op1=ALU.mult).then_inc(x_normed, 1)

            def norm_lo(n, t, hi, lo, banks):
                for b in range(2):
                    dve.wait_ge(x_hi, n * 4 + 2 * t + b + 1)

                    def part(x):
                        return x[:, :].rearrange("p (k t) -> p k t", k=KT)[:, 4 * b:4 * b + 4, t * P:(t + 1) * P]
                    rest(part(lo), ps[:, banks[2 * t + b], :].rearrange("p (k c) -> p k c", k=4), part(hi), x_lo)

            def residual(layer, r, t, u, scale):
                for c in range(2):
                    if 2 * t + c < 3:
                        dve.wait_ge(y_part, layer * (3 * RESIDUALS) + 3 * r + 2 * t + c + 1)
                    else:
                        dve.wait_ge(unit_used, layer * UNITS + u + 1)
                    hh = h[:, t * D + 512 * c:t * D + 512 * c + 512]
                    dve.scalar_tensor_tensor(out=hh, in0=ps[:, 2 * t + c, :], scalar=scale, in1=hh,
                                             op0=ALU.mult, op1=ALU.add).then_inc(resid, 1)

            def norm(layer, j, u, second):
                n = layer * NORMS + j
                dve.wait_ge(gain_in, (n + 1) * 16)
                normalise(n, 0, h[:, 0:D])
                ahead(layer, u + 1)
                second()
                norm_lo(n, 0, u_hi, u_lo, (4, 5, 6, 7))
                normalise(n, 1, h[:, D:2 * D])
                ahead(layer, u + RING)
                norm_lo(n, 1, u_hi, u_lo, (4, 5, 6, 7))

            def ffn(layer, u0, f):
                c = layer * (2 * FT) + f * FT

                def step(i, s):
                    dve.wait_ge(silu_done, c + i + 1)
                    dve.tensor_tensor(prod_b(s), ps[:, 4 + s % 4, S:2 * S], silu_b(s), ALU.mult).then_inc(prod_done, 1)
                    dve.wait_ge(prod_hi, c + i + 1)
                    rest(prod_t(v_lo, s), prod_b(s), prod_t(v_hi, s), prod_lo)

                for i in range(LAG):
                    ahead(layer, u0 + 3 * i + LAG)
                    step(i, i)
                with dve.Fori(0, 4) as t:
                    for s in range(4):
                        for j in range(3):
                            n = u0 + 3 * (LAG + s) + j
                            split(layer, t * 12 + n, n)
                        step(t * 4 + (LAG + s), LAG + s)
                done[0] += 48
                for i in range(LAG + 16, FT):
                    ahead(layer, u0 + 3 * i + LAG)
                    step(i, i)

            dve.wait_ge(const_in, 16 * 10)
            dve.wait_ge(x_in, 16)
            dve.wait_ge(bias_mm, 1)
            dve.tensor_tensor(work[0:NG * HEADS, 3 * BIAS_W:4 * BIAS_W], ps[0:NG * HEADS, 0, 0:BIAS_W],
                              work[0:NG * HEADS, BIAS_W:2 * BIAS_W], ALU.add).then_inc(bias_row, 1)
            dve.wait_ge(bias_out, 16)
            for x in (p_max, p_negmax, p_sum, p_inv):
                dve.memset(x[:, :], 0.0).then_inc(resid, 1)
            with dve.Fori(0, DEPTH) as layer:
                done[0] = 0
                norm(layer, N_FFN1, U_FFN1, lambda: None)
                ffn(layer, U_FFN1, 0)
                residual(layer, 0, 0, U_LAT - 1, 0.5)
                norm(layer, N_MIX, U_LAT, lambda: residual(layer, 0, 1, U_LAT - 1, 0.5))

                def take(d, u, dst, src, op=None):
                    assert d % 2 == 1
                    ahead(layer, u + 4)
                    dve.wait_ge(unit_used, layer * UNITS + u + 1)
                    if op is None:
                        ins = dve.tensor_copy(dst, src)
                    else:
                        ins = dve.tensor_scalar(dst, src, op[1], None, op[0])
                    ins.then_inc(taken[1], 1)
                    ahead(layer, u + 5)

                def take_f(d, u, dst, scale=None):
                    take(d, u, dst, ps[:, 1, 0:S], None if scale is None else (ALU.mult, scale))

                ahead(layer, U_SBQ + 3)
                for t in range(TT):
                    dve.wait_ge(lat_sq, layer * 4 + 2 * t + 2)
                    dve.tensor_copy(k_raw[:, t * ROPE:(t + 1) * ROPE], ps[:, 3 + 2 * t, KV_RANK:KV_RANK + ROPE])\
                        .then_inc(kr_copied, 1)
                ahead(layer, U_SBQ + 4)
                dve.wait_ge(small_in, layer * 48 + 48)
                dve.wait_ge(lat_rstd, layer + 1)
                for t in range(TT):
                    for c, (bank, lo, hi) in enumerate(((2, 0, Q_RANK), (3, Q_RANK, 512))):
                        last = dve.scalar_tensor_tensor(out=lat_n[:, t, lo:hi], in0=ps[:, bank + 2 * t, 0:hi - lo],
                                                        scalar=lat_rs[:, 2 * c + t:2 * c + t + 1],
                                                        in1=lat_gain[:, lo:hi], op0=ALU.mult, op1=ALU.mult)
                    last.then_inc(lat_normed, 1)
                for f in range(1, 4, 2):
                    take_f(D_SBQ + f, U_SBQ + f, sb_q[:, f, :], HD ** -0.5)
                for t in range(TT):
                    dve.wait_ge(lat_hi, layer * TT + t + 1)

                    def part(x):
                        return x[:, 0:4 * S].rearrange("p (k t) -> p k t", k=4)[:, :, t * P:(t + 1) * P]
                    rest(part(v_lo), ps[:, 6 + t, :].rearrange("p (k c) -> p k c", k=4), part(v_hi), lat_lo)
                for f in range(1, 4, 2):
                    take_f(D_SBK + f, U_SBK + f, sb_k[:, f, :])
                take(D_SBV + 1, U_SBV + 3, sb_v[:, 1, :], ps[:, 1, :])
                for c in range(2):
                    ahead(layer, U_UQ + RING)
                    if c == 0:
                        dve.wait_ge(uq_done, layer * 3 + 2)
                    else:
                        dve.wait_ge(unit_used, layer * UNITS + U_UKV)
                    dve.tensor_scalar(q_tok[:, 1, 4 * c:4 * c + 4, :],
                                      ps[:, 1, 0:384].rearrange("p (h c) -> p h c", h=4), QK ** -0.5, None,
                                      ALU.mult).then_inc(taken[1], 1)
                for c in range(2):
                    ahead(layer, U_UKV + 4)
                    if c == 0:
                        dve.wait_ge(ukv_done, layer * 3 + 2)
                    else:
                        dve.wait_ge(unit_used, layer * UNITS + U_UKV + 1)
                    kv = ps[:, 1, :].rearrange("p (h c) -> p h c", h=4)
                    dve.tensor_copy(k_cat[:, 1, 4 * c:4 * c + 4, 0:NOPE], kv[:, :, 0:NOPE])
                    dve.tensor_copy(mv[:, 1, 256 * c:256 * c + 256].rearrange("p (h c) -> p h c", h=4),
                                    kv[:, :, NOPE:NOPE + HD]).then_inc(taken[1], 1)

                def take_dil(u):
                    if u < U_DV:
                        i = u - U_DQK
                        g, part, f = i // 8, i % 8 // 4, i % 4
                        if i % 2 == 1:
                            take_f(D_DQK + i, u, (dq, dk)[part][:, g, f, :], (HD ** -0.5, None)[part])
                    elif (u - U_DV) % 4 == 3:
                        g = (u - U_DV) // 4
                        take(D_DV + 2 * g + 1, u, dv[:, g, 1, :], ps[:, 1, :])
                    ahead(layer, u + 5)

                dve.wait_ge(gain_in, (layer * NORMS + N_MEM + 1) * 16)
                for hd in range(HEADS + 1):
                    u = U_DQK + 2 * hd
                    n = layer * HEADS + hd
                    if hd >= 1:
                        e = sb_w(hd - 1)
                        dve.wait_ge(stick_sum, n)
                        if hd - 1 >= 2:
                            dve.wait_ge(stick_o, n - 2)
                        dve.tensor_tensor(e, ps[:, 2 + (hd - 1) % 2, 0:384], strict_neg[:, :], ALU.add).then_inc(stick_arg, 1)
                    if hd < HEADS:
                        dve.wait_ge(z_ln, n + 1)
                        if hd >= 2:
                            dve.wait_ge(stick_sum, n - 1)
                        dve.scalar_tensor_tensor(out=sb_sp(hd), in0=ps[:, 2 + hd % 2, 0:384], scalar=0.0,
                                                 in1=sb_soft(hd), op0=ALU.max, op1=ALU.add).then_inc(sp_done, 1)
                        dve.wait_ge(sp_done, n + 1)
                        diag = sb_sp(hd).rearrange("p (b c) -> p b c", b=3)[:, 0:3:2, :]
                        dve.tensor_tensor(diag, diag, strict[:, :].unsqueeze(1).broadcast_to([P, 2, P]),
                                          ALU.mult).then_inc(sp_masked, 1)
                    take_dil(u)
                    if hd < HEADS:
                        dve.wait_ge(mla_turned, n + 1)
                        dst = (mk if hd < 4 else mq)[0:QK, 2 * (hd % 4):2 * (hd % 4) + 2, :]
                        dve.tensor_copy(dst, ps[0:QK, 6 + hd % 2, :].rearrange("p (h t) -> p h t", h=2)).then_inc(mla_copied, 1)
                        take_dil(u + 1)
                    if hd == HEADS:
                        for t in range(TT):
                            normalise(layer * NORMS + N_MEM, t, norm_x[:, t, :])
                    if hd >= 1 and hd % 2 == 0:
                        pair = (hd - 1) // 2
                        dve.wait_ge(stick_o, n)
                        dve.tensor_copy(oa[:, pair, :], ps[:, 4 + pair % 2, 0:S]).then_inc(oa_copied, 1)

                for t in range(TT):
                    norm_lo(layer * NORMS + N_MEM, t, v_hi, v_lo, (2, 3, 4, 5))
                take_dil(U_DQK + 2 * HEADS + 1)

                def soft_front(m):
                    base = layer * PIECES + m
                    dve.wait_ge(logits_ps, base + 1)
                    if m >= 2:
                        dve.wait_ge(probs_done, base - 1)
                    dve.reduce_max(p_max[:, m % 2:m % 2 + 1], logits_of(m), AX.X).then_inc(max_done, 1)
                    dve.wait_ge(max_done, base + 1)
                    dve.tensor_scalar(p_negmax[:, m % 2:m % 2 + 1], p_max[:, m % 2:m % 2 + 1], -1.0, None,
                                      ALU.mult).then_inc(negmax_done, 1)

                def soft_back(m):
                    base = layer * PIECES + m
                    w = key_w(m)
                    if m < M_DIL or m >= M_X or m % 2:
                        dve.wait_ge(probs_turned, base + 1)
                        if m >= 2:
                            dve.wait_ge(pv_done, base - 1)
                        if m < M_DIL or m >= M_X:
                            dve.tensor_copy(probs_t(m)[:, 0:w], ps[:, 4 + m % 2, 0:w]).then_inc(probs_t_dve, 1)
                        else:
                            dve.tensor_copy(probs_t(m)[:, 512:w], ps[:, 5, 0:w - 512]).then_inc(probs_t_dve, 1)
                    dve.wait_ge(probs_done, base + 1)
                    dve.reciprocal(p_inv[:, m % 2:m % 2 + 1], p_sum[:, m % 2:m % 2 + 1]).then_inc(inv_done, 1)

                def take_o(m):
                    base = layer * PIECES + m
                    if m < M_DIL:
                        t, c, dst = m % 2, HD * (m // 2), o_b
                        w = HD
                    elif m < M_X:
                        t, c, dst = m % 2, HD * ((m - M_DIL) // 2), o_c
                        w = HD
                    else:
                        t, c, dst = m % 2, XD * ((m - M_X) // 2), o_b
                        w = XD
                    dve.wait_ge(inv_done, base + 1)
                    dve.wait_ge(pv_done, base + 1)
                    dve.tensor_scalar(dst[:, t * WIDTH + c:t * WIDTH + c + w], ps[:, 6 + m % 2, 0:w],
                                      p_inv[:, m % 2:m % 2 + 1], None, ALU.mult).then_inc(o_taken, 1)

                for m in range(N_MLA + 1):
                    if m < N_MLA:
                        soft_front(m)
                    if m >= 1:
                        soft_back(m - 1)
                    take_dil(U_DQK + 2 * HEADS + 2 + m)
                    if m >= 1:
                        take_o(m - 1)
                for u in range(U_DQK + 2 * HEADS + 3 + N_MLA, U_GATE):
                    take_dil(u)

                def take_gate(u):
                    i = u - U_GATE
                    if i < 24:
                        if i % 2 == 1:
                            take(D_GATE + i, u, kt(sg, i), ps[:, 1, 0:S], (ALU.add, gate_b[:, i:i + 1]))
                    elif i < 28:
                        if i % 2 == 1:
                            take_f(D_GATE + i, u, x_k[:, i - 24, :])
                    elif i == 31:
                        take(D_MV + 1, u, x_v[:, 1, :], ps[:, 1, :])
                    ahead(layer, u + 5)

                for i in range(N_DIL + 1):
                    m = M_DIL + i
                    if i < N_DIL:
                        soft_front(m)
                    if i >= 1:
                        soft_back(m - 1)
                    if i < N_DIL:
                        take_gate(U_GATE + 2 * i)
                    if i >= 1:
                        take_o(m - 1)
                    if i < N_DIL:
                        take_gate(U_GATE + 2 * i + 1)

                dve.wait_ge(o_hi, layer * O_SPLITS + 1)
                rest(u_lo[:, 0:4 * S], o_a[:, :], u_hi[:, 0:4 * S], o_lo)
                for b in range(3):
                    if b < 2:
                        for t in range(TT):
                            dve.wait_ge(o_hi, layer * O_SPLITS + 1 + 2 * b + t + 1)

                            def part(x):
                                return x[:, (1 - b) * 4 * S:(2 - b) * 4 * S].rearrange(
                                    "p (k t) -> p k t", k=4)[:, :, t * P:(t + 1) * P]
                            rest(part(u_lo), ps[:, 4 + 2 * b + t, :].rearrange("p (k c) -> p k c", k=4), part(u_hi), o_lo)
                    dve.wait_ge(sig_done, layer * 3 + b + 1)
                    for j in range(4):
                        d = D_BR + 4 * b + j
                        u = U_BR + 4 * b + j
                        ahead(layer, u + 5)
                        dve.wait_ge(unit_used, layer * UNITS + u + 1)
                        g = sg[:, b * KT * S + 512 * j:b * KT * S + 512 * j + 512]
                        if b == 0:
                            dve.tensor_tensor(merged[:, j, :], ps[:, d % 2, :], g, ALU.mult).then_inc(taken[d % 2], 1)
                        else:
                            if 4 * b + j - 4 >= 2:
                                dve.wait_ge(merged_sum, layer * 8 + 4 * (b - 1) + j - 1)
                            dve.tensor_tensor(addend[:, j % 2, :], ps[:, d % 2, :], g, ALU.mult).then_inc(taken[d % 2], 1)
                            out_taken(dve, layer, d)
                        if b == 0:
                            continue
                        dve.tensor_tensor(merged[:, j, :], merged[:, j, :], addend[:, j % 2, :], ALU.add)\
                            .then_inc(merged_sum, 1)
                for j in range(4):
                    dve.wait_ge(merged_hi, layer * 4 + j + 1)
                    rest(v_lo[:, 512 * j:512 * j + 512], merged[:, j, :], v_hi[:, 512 * j:512 * j + 512], merged_lo)
                    ahead(layer, U_MIX + j + 4)
                ahead(layer, U_XQ)
                residual(layer, 1, 0, U_XQ - 1, 1.0)
                norm(layer, N_XA, U_XQ, lambda: residual(layer, 1, 1, U_XQ - 1, 1.0))
                take(D_XQ + 1, U_XQ + 3, x_q[:, 1:4:2, :], ps[:, 1, :].rearrange("p (f t) -> p f t", f=2),
                     (ALU.mult, XD ** -0.5))
                ahead(layer, U_FFN2)
                for i in range(N_X + 1):
                    m = M_X + i
                    if i < N_X:
                        soft_front(m)
                    if i >= 1:
                        soft_back(m - 1)
                        take_o(m - 1)
                for t in range(TT):
                    dve.wait_ge(o_hi, layer * O_SPLITS + 5 + t + 1)

                    def part(x):
                        return x[:, 0:4 * S].rearrange("p (k t) -> p k t", k=4)[:, :, t * P:(t + 1) * P]
                    rest(part(v_lo), ps[:, 6 + t, :].rearrange("p (k c) -> p k c", k=4), part(v_hi), o_lo)
                ahead(layer, U_FFN2)
                residual(layer, 2, 0, U_FFN2 - 1, 1.0)
                norm(layer, N_FFN2, U_FFN2, lambda: residual(layer, 2, 1, U_FFN2 - 1, 1.0))
                ffn(layer, U_FFN2, 1)
                for t in range(TT):
                    residual(layer, 3, t, UNITS - 1, 0.5)
                assert done[0] == UNITS
            dve.wait_ge(gain_in, (DEPTH * NORMS + 1) * 16)
            for t in range(TT):
                dve.wait_ge(rstd_done, DEPTH * 2 * NORMS + t + 1)
                dve.scalar_tensor_tensor(out=norm_x[:, t, :], in0=h[:, t * D:(t + 1) * D], scalar=rstd[:, t:t + 1],
                                         in1=gain, op0=ALU.mult, op1=ALU.mult).then_inc(final_sem, 1)

        @block.tensor
        def _(pe):
            def ready(layer, u):
                pe.wait_ge(lo_made, layer * UNITS + u + 1)

            def mm3(o, ah, al, bh, bl, first, last):
                pe.matmul(o, ah, bh, start=first, stop=False)
                pe.matmul(o, ah, bl, start=False, stop=False)
                return pe.matmul(o, al, bh, start=False, stop=last)

            def weights_still(o, n, j, c, x_hi_, x_lo_, k, first, last):
                w = slice(j * c, j * c + P)
                return mm3(o, slot(w_hi, n)[:, w], slot(w_lo, n)[:, w], kt(x_hi_, k), kt(x_lo_, k), first, last)

            def tokens_still(o, x_hi_, x_lo_, k, t, n, c0, c1, first, last):
                x = slice(k * S + t * P, k * S + t * P + P)
                return mm3(o, x_hi_[:, x], x_lo_[:, x], slot(w_hi, n)[:, c0:c1], slot(w_lo, n)[:, c0:c1], first, last)

            def feature_unit(layer, u, n, o, x_hi_, x_lo_):
                ready(layer, u)
                for k in range(KT):
                    last = weights_still(o, n, k, P, x_hi_, x_lo_, k, k == 0, k == KT - 1)
                last.then_inc(unit_used, 1)

            def bank_free(layer, d):
                if d >= 2:
                    pe.wait_ge(taken[d % 2], layer * (OUTS // 2) + d // 2)

            def feature_out(layer, d, u, x_hi_=u_hi, x_lo_=u_lo):
                bank_free(layer, d)
                feature_unit(layer, u, u, ps[:, d % 2, 0:S], x_hi_, x_lo_)

            def token_unit(layer, u, j, banks, x_hi_=u_hi, x_lo_=u_lo):
                ready(layer, u)
                for kk in range(2):
                    k = 2 * j + kk
                    for t in range(TT):
                        last = tokens_still(ps[:, banks[t], :], x_hi_, x_lo_, k, t, u, 512 * kk, 512 * kk + 512,
                                            k == 0, k == KT - 1)
                last.then_inc(unit_used, 1)

            def token_out(layer, d, u, j, x_hi_=u_hi, x_lo_=u_lo):
                if j == 0:
                    bank_free(layer, d)
                    bank_free(layer, d + 1)
                token_unit(layer, u, j, (d % 2, (d + 1) % 2), x_hi_, x_lo_)

            def row_unit(layer, u, n, x_hi_, x_lo_, k, first, last):
                ready(layer, u)
                for t in range(TT):
                    for c in range(2):
                        ins = tokens_still(ps[:, 2 * t + c, :], x_hi_, x_lo_, k, t, n, 512 * c, 512 * c + 512,
                                           first, last)
                ins.then_inc(unit_used, 1)

            def row_tail(layer, u0, n, x_hi_, x_lo_, k0, slots, whole=False):
                for i in range(2 * TT):
                    t, c = divmod(i, 2)
                    for j in range(n):
                        if i == 0:
                            ready(layer, u0 + j)
                        last = tokens_still(ps[:, i, :], x_hi_, x_lo_, slots(k0 + j), t, u0 + j,
                                            512 * c, 512 * c + 512, whole and j == 0, j == n - 1)
                        if i == 2 * TT - 1:
                            last.then_inc(unit_used, 1)
                        elif j == n - 1:
                            last.then_inc(y_part, 1)

            def turn_norm(n, t, banks):
                for b in range(2):
                    pe.wait_ge(x_normed, n * 4 + 2 * t + b + 1)
                    for k in range(4):
                        last = pe.transpose(ps[:, banks[2 * t + b], P * k:P * k + P],
                                            norm_x[:, t, (4 * b + k) * P:(4 * b + k + 1) * P], ident[:, :])
                    last.then_inc(x_turned, 1)

            def tokens_after_norm(layer, j, u, part):
                n = layer * NORMS + j
                turn_norm(n, 0, (4, 5, 6, 7))
                for i in range(RING):
                    if i == 2:
                        turn_norm(n, 1, (4, 5, 6, 7))
                    ready(layer, u + i)
                    if i == 0:
                        pe.wait_ge(x_lo, n * 4 + 2)
                    part(i, 0)
                pe.wait_ge(x_lo, n * 4 + 4)
                for i in range(RING):
                    part(i, 1).then_inc(unit_used, 1)

            def feature_after_norm(layer, j, u, o):
                n = layer * NORMS + j
                turn_norm(n, 0, (4, 5, 6, 7))
                turn_norm(n, 1, (4, 5, 6, 7))
                ready(layer, u)
                for k in range(KT):
                    if k % 4 == 0:
                        pe.wait_ge(x_lo, n * 4 + 3 + k // 4)
                    last = weights_still(o, u, k, P, u_hi, u_lo, k, k == 0, k == KT - 1)
                last.then_inc(unit_used, 1)

            def ffn(layer, u0, f):
                c = layer * (2 * FT) + f * FT

                def gate_up(u, n, s):
                    for j in range(2):
                        feature_unit(layer, u + j, n + j, ps[:, 4 + s % 4, j * S:(j + 1) * S], u_hi, u_lo)

                def down(i, u, n, s, first):
                    pe.wait_ge(prod_lo, c + i + 1)
                    row_unit(layer, u, n, v_hi, v_lo, s % 4, first, False)

                feature_after_norm(layer, (N_FFN1, N_FFN2)[f], u0, ps[:, 4, 0:S])
                feature_unit(layer, u0 + 1, u0 + 1, ps[:, 4, S:2 * S], u_hi, u_lo)
                gate_up(u0 + 2, u0 + 2, 1)
                gate_up(u0 + 4, u0 + 4, 2)
                gate_up(u0 + 6, u0 + 6, 3)
                down(0, u0 + 8, u0 + 8, 0, True)
                for s in range(3):
                    gate_up(u0 + 9 + 3 * s, u0 + 9 + 3 * s, 4 + s)
                    down(1 + s, u0 + 11 + 3 * s, u0 + 11 + 3 * s, 1 + s, False)
                with pe.Fori(0, 3) as t:
                    for s in range(4):
                        n = u0 + 18 + 3 * s
                        gate_up(t * 12 + n, n, 7 + s)
                        down(t * 4 + (4 + s), t * 12 + (n + 2), n + 2, 4 + s, False)
                for i in range(19, FT):
                    gate_up(u0 + ffn_unit(i), u0 + ffn_unit(i), i)
                    down(i - LAG, u0 + down_unit(i - LAG), u0 + down_unit(i - LAG), i - LAG, False)
                pe.wait_ge(prod_lo, c + FT)
                row_tail(layer, u0 + FFN_UNITS - LAG, LAG, v_hi, v_lo, FT - LAG, lambda i: i % 4)

            pe.wait_ge(const_in, 16 * 10)
            pe.wait_ge(setup_mem, 2)
            pe.matmul(ps[0:NG * HEADS, 0, 0:BIAS_W], work[0:BUCKETS, 2 * BIAS_W:2 * BIAS_W + NG * HEADS],
                      work[0:BUCKETS, 0:BIAS_W], start=True, stop=True).then_inc(bias_mm, 1)
            with pe.Fori(0, DEPTH) as layer:
                ffn(layer, U_FFN1, 0)

                def latent(i, t):
                    tokens_still(ps[:, 2 + 2 * t, 0:Q_RANK], u_hi, u_lo, i, t, U_LAT + i, 0, Q_RANK,
                                 i == 0, i == KT - 1)
                    return tokens_still(ps[:, 3 + 2 * t, 0:256], u_hi, u_lo, i, t, U_LAT + i, Q_RANK, Q_RANK + 256,
                                        i == 0, i == KT - 1)

                tokens_after_norm(layer, N_MIX, U_LAT, latent)
                for i in range(RING, KT):
                    ready(layer, U_LAT + i)
                    for t in range(TT):
                        last = latent(i, t)
                    last.then_inc(unit_used, 1)
                for f in range(4):
                    feature_out(layer, D_SBQ + f, U_SBQ + f)
                for t in range(TT):
                    pe.wait_ge(lat_normed, layer * TT + t + 1)
                    for k in range(4):
                        last = pe.transpose(ps[:, 6 + t, k * P:(k + 1) * P], lat_n[:, t, k * P:(k + 1) * P], ident[:, :])
                    last.then_inc(lat_turned, 1)
                for f in range(4):
                    feature_out(layer, D_SBK + f, U_SBK + f)
                for j in range(4):
                    token_out(layer, D_SBV, U_SBV + j, j)
                pe.wait_ge(lat_lo, layer * TT + TT)
                for c in range(2):
                    for t in range(TT):
                        bank_free(layer, D_UQ + 2 * c + t)
                        for k in range(3):
                            if c == 0 and t == 0:
                                ready(layer, U_UQ + k)
                            last = tokens_still(ps[:, t, 0:384], v_hi, v_lo, k, t, U_UQ + k, 384 * c, 384 * c + 384,
                                                k == 0, k == 2)
                            if c == 1 and t == 1:
                                last.then_inc(unit_used, 1)
                        if c == 0 or t == 0:
                            last.then_inc(uq_done, 1)
                ready(layer, U_UKV)
                for c in range(2):
                    for t in range(TT):
                        bank_free(layer, D_UKV + 2 * c + t)
                        last = tokens_still(ps[:, t, :], v_hi, v_lo, 3, t, U_UKV, 512 * c, 512 * c + 512, True, True)
                        if c == 0 or t == 0:
                            last.then_inc(ukv_done, 1)
                last.then_inc(unit_used, 1)

                def dil_unit(u):
                    if u < U_DV:
                        feature_out(layer, D_DQK + u - U_DQK, u)
                    else:
                        g, j = divmod(u - U_DV, 4)
                        token_out(layer, D_DV + 2 * g, u, j)

                out_taken(pe, layer, D_SBV)
                out_taken(pe, layer, D_SBV + 1)
                for hd in range(HEADS + 1):
                    n = layer * HEADS + hd
                    u = U_DQK + 2 * hd
                    if hd < HEADS:
                        r = slice(HD * (hd % 2), HD * (hd % 2) + HD)
                        f = hd // 2
                        if hd >= 2:
                            pe.wait_ge(stick_arg, n - 1)
                        z = ps[:, 2 + hd % 2, :]
                        pe.matmul(z[:, 0:S], sb_k[r, f, 0:P], sb_q[r, f, :], start=True, stop=True)
                        pe.matmul(z[:, S:S + P], sb_k[r, f, P:S], sb_q[r, f, P:S], start=False, stop=True,
                                  skip_group_check=True).then_inc(z_done, 1)
                    if hd >= 1:
                        z = ps[:, 2 + (hd - 1) % 2, :]
                        sp_ = sb_sp(hd - 1)
                        pe.wait_ge(sp_masked, n)
                        pe.matmul(z[:, 0:S], tri[:, :], sp_[:, 0:S], start=False, stop=True, skip_group_check=True)
                        pe.matmul(z[:, P:S], minus1[:, :], sp_[:, S:S + P], start=False, stop=True,
                                  skip_group_check=True)
                        pe.matmul(z[:, S:S + P], tri[:, :], sp_[:, S:S + P], start=False, stop=True,
                                  skip_group_check=True).then_inc(stick_sum, 1)
                    dil_unit(u)
                    if hd < HEADS:
                        src = k_cat if hd < 4 else q_tok
                        if hd == 0:
                            out_taken(pe, layer, D_UKV + 2)
                            out_taken(pe, layer, D_UKV + 3)
                            pe.wait_ge(rope_step, layer * POOL_STEPS + 8)
                        if hd == 4:
                            pe.wait_ge(rope_step, layer * POOL_STEPS + POOL_STEPS)
                        if hd >= 2:
                            pe.wait_ge(mla_copied, n - 1)
                        for x in range(2):
                            for t in range(TT):
                                last = pe.transpose(ps[0:QK, 6 + hd % 2, S * x + P * t:S * x + P * t + P],
                                                    src[:, t, 2 * (hd % 4) + x, :], ident[:, :])
                        last.then_inc(mla_turned, 1)
                        dil_unit(u + 1)
                    if hd >= 1:
                        g = hd - 1
                        r = slice(HD * (g % 2), HD * (g % 2) + HD)
                        o = ps[r, 4 + (g // 2) % 2, :]
                        pe.wait_ge(stick_w, n)
                        if g % 2 == 0 and g >= 4:
                            pe.wait_ge(oa_copied, layer * 4 + g // 2 - 1)
                        pe.matmul(o[:, 0:S], sb_v[:, 0, g * HD:(g + 1) * HD], sb_w(g)[:, 0:S], start=True, stop=False)
                        pe.matmul(o[:, P:S], sb_v[:, 1, g * HD:(g + 1) * HD], sb_w(g)[:, S:S + P], start=False,
                                  stop=True).then_inc(stick_o, 1)

                pe.wait_ge(stick_arg, layer * HEADS + HEADS)
                pe.wait_ge(oa_copied, layer * 4 + 4)
                for t in range(TT):
                    turn_norm(layer * NORMS + N_MEM, t, (2, 3, 4, 5))
                dil_unit(U_DQK + 2 * HEADS + 1)
                pe.wait_ge(x_lo, (layer * NORMS + N_MEM + 1) * 4)
                pe.wait_ge(mla_copied, layer * HEADS + HEADS)

                def turn_probs(m):
                    base = layer * PIECES + m
                    pe.wait_ge(probs_done, base + 1)
                    src = probs_sb(m)
                    b0 = 4 if M_DIL <= m < M_X else 4 + m % 2
                    for b in range(key_w(m) // P):
                        last = pe.transpose(ps[:, b0 + b // 4, P * (b % 4):P * (b % 4) + P],
                                            src[:, P * b:P * b + P], ident[:, :])
                    last.then_inc(probs_turned, 1)

                def logits_free(m):
                    same = 1 if M_DIL <= m <= M_X else 2
                    if m >= same:
                        pe.wait_ge(probs_done, layer * PIECES + m - same + 1)

                def times_v(m, blocks, w):
                    base = layer * PIECES + m
                    pt_waits(pe, layer, m)
                    if m >= 2:
                        pe.wait_ge(o_taken, base - 1)
                    for i, (b, v) in enumerate(blocks):
                        last = pe.matmul(ps[:, 6 + m % 2, 0:w], probs_t(m)[:, P * b:P * b + P], v,
                                         start=(i == 0), stop=(i == len(blocks) - 1))
                    last.then_inc(pv_done, 1)

                for m in range(N_MLA + 1):
                    if m < N_MLA:
                        hd, t = divmod(m, 2)
                        logits_free(m)
                        z = logits_of(m)
                        pe.matmul(z, mq[0:QK, hd, t * P:(t + 1) * P], mk[0:QK, hd, 0:key_w(m)], start=True, stop=False)
                        pe.matmul(z[:, t * P:(t + 1) * P], ident[:, :], causal[:, :], start=False,
                                  stop=True).then_inc(logits_ps, 1)
                    if m >= 1:
                        turn_probs(m - 1)
                    dil_unit(U_DQK + 2 * HEADS + 2 + m)
                    if m >= 1:
                        hd, t = divmod(m - 1, 2)
                        times_v(m - 1, [(b, mv[:, b, hd * HD:(hd + 1) * HD]) for b in range(t + 1)], HD)
                for u in range(U_DQK + 2 * HEADS + 3 + N_MLA, U_GATE):
                    dil_unit(u)

                def gate_unit(u):
                    i = u - U_GATE
                    if i < 24:
                        feature_out(layer, D_GATE + i, u)
                    elif i < 28:
                        feature_out(layer, D_GATE + i, u, v_hi, v_lo)
                    else:
                        token_out(layer, D_MV, u, i - 28, v_hi, v_lo)

                out_taken(pe, layer, D_DV + 2 * NG - 2)
                out_taken(pe, layer, D_DV + 2 * NG - 1)
                for i in range(N_DIL + 1):
                    m = M_DIL + i
                    if i < N_DIL:
                        hd, t = divmod(i, 2)
                        r = slice(HD * (hd % 2), HD * (hd % 2) + HD)
                        kw = P * (t + 1)
                        logits_free(m)
                        if t == 0:
                            pe.wait_ge(bias_in[hd % 2], (layer * (HEADS // 2) + hd // 2 + 1) * 16)
                            pe.matmul(ps[:, 2, 0:NG * P].rearrange("p (g k) -> p g k", g=NG), flip[:, :],
                                      bias3[:, hd % 2, :, P:S], start=True, stop=False)
                        else:
                            pe.matmul(ps[:, 2, :].rearrange("p (g k) -> p g k", g=2), flip[:, :],
                                      bias3[:, hd % 2, 0:2, :], start=True, stop=False)
                            pe.matmul(ps[:, 3, 0:S], flip[:, :], bias3[:, hd % 2, 2, :], start=True, stop=False)
                        for g in range(NG):
                            c = g * kw
                            last = pe.matmul(ps[:, 2 + c // 512, c % 512:c % 512 + kw], dq[r, g, hd // 2, t * P:(t + 1) * P],
                                             dk[r, g, hd // 2, 0:kw], start=False, stop=(g == NG - 1 or c + kw == 512))
                        last.then_inc(logits_ps, 1)
                    if i >= 1:
                        turn_probs(m - 1)
                    if i < N_DIL:
                        gate_unit(U_GATE + 2 * i)
                    if i >= 1:
                        hd, t = divmod(i - 1, 2)
                        times_v(m - 1, [(g * (t + 1) + b, dv[:, g, b, hd * HD:(hd + 1) * HD])
                                        for g in range(NG) for b in range(t + 1)], HD)
                    if i < N_DIL:
                        gate_unit(U_GATE + 2 * i + 1)

                def turn_heads(n, src, banks):
                    for t in range(TT):
                        for k in range(4):
                            last = pe.transpose(ps[:, banks[t], k * P:(k + 1) * P],
                                                src[:, t * WIDTH + k * P:t * WIDTH + (k + 1) * P], ident[:, :])
                        last.then_inc(o_turned, 1)

                def branch(b):
                    for j in range(4):
                        d, u = D_BR + 4 * b + j, U_BR + 4 * b + j
                        bank_free(layer, d)
                        ready(layer, u)
                        for f in range(2):
                            for k in range(4):
                                c = k * 2 * P + f * P
                                x = slice((b % 2) * 4 * S + k * S, (b % 2) * 4 * S + (k + 1) * S)
                                last = mm3(ps[:, d % 2, f * S:(f + 1) * S], slot(w_hi, u)[:, c:c + P],
                                           slot(w_lo, u)[:, c:c + P], u_hi[:, x], u_lo[:, x], k == 0, k == 3)
                        last.then_inc(unit_used, 1)

                pe.wait_ge(o_taken, layer * PIECES + M_X)
                turn_heads(0, o_b, (4, 5))
                pe.wait_ge(o_lo, layer * O_SPLITS + 1)
                branch(0)
                turn_heads(2, o_c, (6, 7))
                pe.wait_ge(o_lo, layer * O_SPLITS + 3)
                branch(1)
                pe.wait_ge(o_lo, layer * O_SPLITS + 5)
                branch(2)
                out_taken(pe, layer, D_BR + 10)
                out_taken(pe, layer, D_BR + 11)
                for k in range(4):
                    pe.wait_ge(merged_lo, layer * 4 + k // 2 + 1)
                    row_unit(layer, U_MIX + k, U_MIX + k, v_hi, v_lo, k, k == 0, False)
                pe.wait_ge(merged_lo, layer * 4 + 4)
                row_tail(layer, U_MIX + 4, 4, v_hi, v_lo, 4, lambda k: k)

                feature_after_norm(layer, N_XA, U_XQ, ps[:, 0, 0:S])
                for i in range(1, 4):
                    feature_unit(layer, U_XQ + i, U_XQ + i, ps[:, i % 2, (i // 2) * S:(i // 2 + 1) * S], u_hi, u_lo)
                out_taken(pe, layer, D_XQ)
                out_taken(pe, layer, D_XQ + 1)
                for i in range(N_X + 1):
                    m = M_X + i
                    if i < N_X:
                        hd, t = divmod(i, 2)
                        logits_free(m)
                        pe.matmul(ps[:, 2 + m % 2, 0:M], x_q[:, hd, t * P:(t + 1) * P], x_k[:, hd, :],
                                  start=True, stop=True).then_inc(logits_ps, 1)
                    if i >= 1:
                        turn_probs(m - 1)
                        hd, t = divmod(i - 1, 2)
                        times_v(m - 1, [(b, x_v[:, b, hd * XD:(hd + 1) * XD]) for b in range(2)], XD)
                pe.wait_ge(o_taken, layer * PIECES + PIECES)
                turn_heads(4, o_b, (6, 7))
                pe.wait_ge(o_lo, layer * O_SPLITS + 7)
                row_tail(layer, U_XO, XH, v_hi, v_lo, 0, lambda k: k, True)
                ffn(layer, U_FFN2, 1)


_OUTS = [((1, S, D), "float32")]


def kernel(**inputs):
    import numpy as _np
    import concourse.bacc as _bacc
    from concourse import mybir as _mybir
    from concourse.bass_utils import run_bass_kernel_spmd as _run

    nc = _bacc.Bacc("TRN2", target_bir_lowering=False, num_devices=1)
    laid = {name: _np.asarray(value) for name, value in inputs.items()}
    weights = pack_weights({name: laid.pop(name) for name in STREAMED}, _np)
    laid["gate_bias"] = laid["gate_bias"].reshape(DEPTH, 24, P).transpose(0, 2, 1)
    laid.update(constants(), weights=weights)
    arrays, aps = {}, {}
    for name, value in laid.items():
        v = _np.ascontiguousarray(value)
        arrays[f"in_{name}"] = v
        aps[name] = nc.dram_tensor(f"in_{name}", v.shape, _mybir.dt.from_np(v.dtype), kind="ExternalInput").ap()
    out = nc.dram_tensor("out_0", _OUTS[0][0], _mybir.dt.float32, kind="ExternalOutput").ap()
    trunk(nc, aps, out)
    r = _run(nc, [arrays], core_ids=[0])
    return r.results[0]["out_0"]
```

```python
import math
from contextlib import ExitStack

import numpy as np
import concourse.bass as bass
from concourse import mybir

F32 = mybir.dt.float32
F32R = mybir.dt.float32r
ALU = mybir.AluOpType
ACT = mybir.ActivationFunctionType
AX = mybir.AxisListType

P = 128
D = 1024
S = 256
M = 256
DEPTH = 2
D_FF = 2816
KT = D // P
TT = S // P
FT = D_FF // P
EPS = 1e-6
NEG = -1e30
HEADS = 8
HD = 64
WIDTH = HEADS * HD
Q_RANK, KV_RANK, NOPE, ROPE = 384, 128, 64, 32
QK = NOPE + ROPE
GROUPS = ((128, 1), (512, 4), (2048, 16))
NG = len(GROUPS)
BUCKETS, MAX_DIST = 32, 2048
XH, XD = 4, 128
RING = 4

C_SBQ, C_SBK, C_SBV = 0, WIDTH, 2 * WIDTH
C_LAT = 3 * WIDTH
C_KR = C_LAT + Q_RANK + KV_RANK
C_DIL = C_KR + ROPE
C_GATE = C_DIL + 3 * NG * WIDTH

FFN_UNITS = 3 * FT
U_FFN1 = 0
U_LAT = U_FFN1 + FFN_UNITS
U_SBQ = U_LAT + KT
U_SBK = U_SBQ + 4
U_SBV = U_SBK + 4
U_UQ = U_SBV + 4
U_UKV = U_UQ + 3
U_DQK = U_UKV + 1
U_DV = U_DQK + 8 * NG
U_GATE = U_DV + 4 * NG
U_MK = U_GATE + 8 * 3
U_MV = U_MK + 4
U_BR = U_MV + 4
U_MIX = U_BR + 12
U_XQ = U_MIX + 8
U_XO = U_XQ + 4
U_FFN2 = U_XO + 4
UNITS = U_FFN2 + FFN_UNITS
assert UNITS % RING == 0 and (12 % RING) == 0
assert U_DQK + 2 * HEADS + 3 + 2 * HEADS + 1 == U_GATE

D_SBQ = 0
D_SBK = D_SBQ + 4
D_SBV = D_SBK + 4
D_UQ = D_SBV + 2
D_UKV = D_UQ + 4
D_DQK = D_UKV + 4
D_DV = D_DQK + 8 * NG
D_GATE = D_DV + 2 * NG
D_MK = D_GATE + 24
D_MV = D_MK + 4
D_BR = D_MV + 2
D_XQ = D_BR + 12
WARM = 14
X_TURN = 6
OUTS = D_XQ + 2
assert OUTS % 2 == 0

N_MLA, N_DIL, N_X = 2 * HEADS, 2 * HEADS, 2 * XH
M_DIL = N_MLA
M_X = M_DIL + N_DIL
PIECES = M_X + N_X
N_FFN1, N_MIX, N_MEM, N_XA, N_FFN2, NORMS = 0, 1, 2, 3, 4, 5
RESIDUALS = 4
LAG = 3
LAT = Q_RANK + KV_RANK + ROPE

BIAS_W = 384


def ffn_unit(i):
    return 2 * i if i < LAG else 2 * LAG + 3 * (i - LAG)


def down_unit(i):
    return 2 * LAG + 3 * i + 2 if i < FT - LAG else FFN_UNITS - FT + i


def constants():
    i = np.arange(P)
    key, query = i[:, None], i[None, :]
    strict = (key < query).astype(np.float32)
    block = np.where(strict > 0, 0.0, NEG).astype(np.float32)
    strict_neg = np.concatenate([block, np.zeros((P, P), np.float32), block], 1)
    causal = np.where(i[None, :] <= i[:, None], 0.0, NEG).astype(np.float32)
    tri = np.where(key >= query, -1.0, 0.0).astype(np.float32)
    half = ROPE // 2
    freqs = np.float32(10000.0) ** (-np.arange(half, dtype=np.float32) / np.float32(half))
    ang = np.arange(S, dtype=np.float32)[:, None] * freqs[None, :].astype(np.float32)
    cs = np.stack([np.cos(ang), np.sin(ang)], 1).astype(np.float32)
    cs = cs.reshape(TT, P, 2, half).transpose(1, 2, 0, 3).reshape(P, 2 * TT * half)
    dist = np.arange(BIAS_W) - (P - 1)
    exact = BUCKETS // 2
    d = np.maximum(dist, exact).astype(np.float32)
    large = exact + (np.log(d / exact) / math.log(MAX_DIST / exact) * (BUCKETS - exact)).astype(np.int32)
    bucket = np.where(dist < exact, np.maximum(dist, 0), np.minimum(large, BUCKETS - 1))
    onehot = (bucket[None, :] == np.arange(BUCKETS)[:, None]).astype(np.float32)
    allowed = np.stack([(dist >= 0) & (dist % r == 0) & (dist // r <= w // r) for w, r in GROUPS])
    window = np.repeat(np.where(allowed, 0.0, NEG).astype(np.float32), HEADS, 0)
    return {
        "c_ident": np.eye(P, dtype=np.float32), "c_tri": tri, "c_strict": strict,
        "c_strict_neg": strict_neg, "c_causal": causal, "c_rope": np.ascontiguousarray(cs),
        "c_onehot": onehot, "c_window": np.ascontiguousarray(window),
    }


def pack_weights(w, np):
    stream = np.zeros((DEPTH, UNITS, P, 1024), np.float32)

    def tiles(u, m, k0, k1, c0, c1):
        n = (k1 - k0) * (c1 - c0)
        part = m[:, k0 * P:k1 * P, c0:c1].reshape(DEPTH, k1 - k0, P, c1 - c0)
        stream[:, u, :, 0:n] = part.transpose(0, 2, 1, 3).reshape(DEPTH, P, n)

    def feature_major(u0, m, c, n):
        for j in range(n):
            tiles(u0 + j, m, 0, KT, c + P * j, c + P * j + P)

    def token_major(u0, m, c):
        for j in range(4):
            tiles(u0 + j, m, 2 * j, 2 * j + 2, c, c + 512)

    def rows(u0, m, n):
        for k in range(n):
            tiles(u0 + k, m, k, k + 1, 0, D)

    for u0, gate, up, down in ((U_FFN1, "ffn1_w_gate", "ffn1_w_up", "ffn1_w_down"),
                               (U_FFN2, "ffn2_w_gate", "ffn2_w_up", "ffn2_w_down")):
        for i in range(FT):
            u = u0 + ffn_unit(i)
            feature_major(u, w[gate], P * i, 1)
            feature_major(u + 1, w[up], P * i, 1)
            tiles(u0 + down_unit(i), w[down], i, i + 1, 0, D)
    w_in = w["w_in"]
    for k in range(KT):
        tiles(U_LAT + k, w_in, k, k + 1, C_LAT, C_LAT + LAT)
    feature_major(U_SBQ, w_in, C_SBQ, 8)
    token_major(U_SBV, w_in, C_SBV)
    for k in range(3):
        tiles(U_UQ + k, w["mla_w_uq"], k, k + 1, 0, 768)
    tiles(U_UKV, w["mla_w_ukv"], 0, 1, 0, 1024)
    for g in range(NG):
        feature_major(U_DQK + 8 * g, w_in, C_DIL + 3 * WIDTH * g, 8)
        token_major(U_DV + 4 * g, w_in, C_DIL + 3 * WIDTH * g + 2 * WIDTH)
    feature_major(U_GATE, w_in, C_GATE, 24)
    feature_major(U_MK, w["xattn_w_kv"], 0, 4)
    token_major(U_MV, w["xattn_w_kv"], XH * XD)
    for b, name in enumerate(("w_branch_a", "w_branch_b", "w_branch_c")):
        for j in range(4):
            tiles(U_BR + 4 * b + j, w[name], 0, 4, 2 * P * j, 2 * P * j + 2 * P)
    rows(U_MIX, w["w_mix_out"], KT)
    feature_major(U_XQ, w["xattn_w_q"], 0, 4)
    rows(U_XO, w["xattn_w_o"], XH)
    return stream.reshape(DEPTH * UNITS, P, 1024)


STREAMED = ("ffn1_w_gate", "ffn1_w_up", "ffn1_w_down", "w_in", "mla_w_uq", "mla_w_ukv", "w_branch_a",
            "w_branch_b", "w_branch_c", "w_mix_out", "xattn_w_q", "xattn_w_kv", "xattn_w_o",
            "ffn2_w_gate", "ffn2_w_up", "ffn2_w_down")


def trunk(nc, a, out):
    ctx = ExitStack()
    with ctx:
        def sb(name, n, dt=F32, parts=P):
            return ctx.enter_context(nc.sbuf_tensor(name, [parts, n], dt))

        def sem(name):
            return ctx.enter_context(nc.semaphore(name))

        raw = sb("raw", RING * 1024)
        w_hi = sb("w_hi", RING * 1024, F32R)
        w_lo = sb("w_lo", RING * 1024, F32R)
        u_hi = sb("u_hi", KT * S, F32R)
        u_lo = sb("u_lo", KT * S, F32R)
        v_hi = sb("v_hi", KT * S, F32R)
        v_lo = sb("v_lo", KT * S, F32R)
        h = sb("h", TT * D)
        dil_q = sb("dil_q", NG * 4 * S)
        dil_k = sb("dil_k", NG * 4 * S)
        dil_v = sb("dil_v", NG * TT * WIDTH)
        mla_q = sb("mla_q", HEADS * S)
        mla_k = sb("mla_k", HEADS * S)
        mla_v = sb("mla_v", TT * WIDTH)
        o_a = sb("o_a", 4 * S)
        o_b = sb("o_b", TT * WIDTH)
        o_c = sb("o_c", TT * WIDTH)
        sg = sb("sg", 3 * KT * S)
        work = sb("work", 3072)
        bias_sb = sb("bias_sb", 2 * NG * S)
        lat_gain = sb("lat_gain", Q_RANK + KV_RANK)
        ident = sb("ident", P)
        tri = sb("tri", P)
        minus1 = sb("minus1", P)
        strict = sb("strict", P)
        strict_neg = sb("strict_neg", 3 * P)
        causal = sb("causal", P)
        rope_cs = sb("rope_cs", 2 * TT * 16)
        gate_b = sb("gate_b", 24)
        k_raw = sb("k_raw", TT * ROPE)
        k_pe = sb("k_pe", TT * ROPE)
        sumsq = sb("sumsq", 2 * TT)
        half_mean = sb("half_mean", TT)
        mean = sb("mean", TT)
        rstd = sb("rstd", TT)
        half_neg = sb("half_neg", 4)
        lat_ss = sb("lat_ss", 4)
        lat_ms = sb("lat_ms", 4)
        lat_rs = sb("lat_rs", 4)
        p_max = sb("p_max", 2)
        p_negmax = sb("p_negmax", 2)
        p_sum = sb("p_sum", 2)
        p_inv = sb("p_inv", 2)
        ps = ctx.enter_context(nc.psum_tensor("ps", [P, 8, 512], F32))
        bias_dram = nc.dram_tensor("bias_rows", (NG * HEADS, BIAS_W), F32, kind="Internal").ap()

        norm_x = sg[:, 0:2 * D].rearrange("p (t d) -> p t d", t=TT)
        gain = sg[:, 2 * D:3 * D]
        q_tok = sg[:, 3 * D:3 * D + 1536].rearrange("p (t h c) -> p t h c", t=TT, h=HEADS)
        k_cat = sg[:, 3 * D + 1536:6 * D].rearrange("p (t h c) -> p t h c", t=TT, h=HEADS)
        lat_n = mla_q[:, 0:TT * 512].rearrange("p (t c) -> p t c", t=TT)
        sb_q = dil_v[:, 0:4 * S].rearrange("p (f t) -> p f t", f=4)
        sb_k = dil_v[:, 4 * S:8 * S].rearrange("p (f t) -> p f t", f=4)
        sb_v = dil_v[:, 8 * S:12 * S].rearrange("p (t c) -> p t c", t=TT)
        dq = dil_q[:, :].rearrange("p (g f t) -> p g f t", g=NG, f=4)
        dk = dil_k[:, :].rearrange("p (g f t) -> p g f t", g=NG, f=4)
        dv = dil_v[:, :].rearrange("p (g t c) -> p g t c", g=NG, t=TT)
        mq = mla_q[:, :].rearrange("p (h t) -> p h t", h=HEADS)
        mk = mla_k[:, :].rearrange("p (h t) -> p h t", h=HEADS)
        mv = mla_v[:, :].rearrange("p (t c) -> p t c", t=TT)
        x_k = mla_q[:, 0:XH * M].rearrange("p (h t) -> p h t", h=XH)
        x_v = mla_q[:, XH * M:2 * XH * M].rearrange("p (t c) -> p t c", t=TT)
        x_q = mla_k[:, 0:XH * S].rearrange("p (h t) -> p h t", h=XH)
        oa = o_a[:, :].rearrange("p (f t) -> p f t", f=4)
        merged = dil_q[:, 0:KT * S].rearrange("p (j c) -> p j c", j=4)
        addend = dil_q[:, KT * S:KT * S + 1024].rearrange("p (b c) -> p b c", b=2)
        bias3 = bias_sb[:, :].rearrange("p (b g k) -> p b g k", b=2, g=NG)
        junk = bias_sb[:, 0:D].rearrange("p (b c) -> p b c", b=2)
        cosv = rope_cs[:, 0:TT * 16].rearrange("p (t c) -> p t c", t=TT)
        sinv = rope_cs[:, TT * 16:2 * TT * 16].rearrange("p (t c) -> p t c", t=TT)
        rope_t = work[:, 2304:2304 + 512].rearrange("p (b c) -> p b c", b=4)

        def probs_sb(m):
            return work[:, 768 * (m % 2):768 * (m % 2) + 768]

        def probs_t(m):
            return work[:, 1536 + 768 * (m % 2):1536 + 768 * (m % 2) + 768]

        def sb_soft(hd):
            return work[:, 384 * (hd % 2):384 * (hd % 2) + 384]

        def sb_sp(hd):
            return work[:, 768 + 384 * (hd % 2):768 + 384 * (hd % 2) + 384]

        def sb_w(hd):
            return work[:, 1536 + 384 * (hd % 2):1536 + 384 * (hd % 2) + 384]

        def silu_b(i):
            return work[:, S * (i % 2):S * (i % 2) + S]

        def prod_b(i):
            return work[:, 2 * S + S * (i % 2):2 * S + S * (i % 2) + S]

        def prod_t(t, i):
            return t[:, S * (i % 4):S * (i % 4) + S]

        def kt(t, k):
            return t[:, k * S:(k + 1) * S]

        def slot(t, u):
            return t[:, 1024 * (u % RING):1024 * (u % RING) + 1024]

        const_in = sem("const_in")
        first_in = sem("first_in")
        x_in = [sem("x_in0"), sem("x_in1")]
        setup_mem = sem("setup_mem")
        bias_mm = sem("bias_mm")
        bias_row = sem("bias_row")
        bias_out = sem("bias_out")
        raw_in = [sem(f"raw_in{i}") for i in range(RING)]
        hi_made = sem("hi_made")
        lo_made = sem("lo_made")
        unit_used = sem("unit_used")
        taken = [sem("taken0"), sem("taken1")]
        gain_in = sem("gain_in")
        mem_in = sem("mem_in")
        small_in = sem("small_in")
        sq_done = sem("sq_done")
        half_done = sem("half_done")
        mean_done = sem("mean_done")
        rstd_done = sem("rstd_done")
        x_normed = sem("x_normed")
        x_turned = sem("x_turned")
        x_hi = sem("x_hi")
        x_lo = sem("x_lo")
        y_part = sem("y_part")
        resid = sem("resid")
        silu_done = sem("silu_done")
        prod_done = sem("prod_done")
        prod_hi = sem("prod_hi")
        prod_lo = sem("prod_lo")
        lat_sq = sem("lat_sq")
        lat_mean = sem("lat_mean")
        lat_rstd = sem("lat_rstd")
        lat_normed = sem("lat_normed")
        lat_turned = sem("lat_turned")
        lat_hi = sem("lat_hi")
        lat_lo = sem("lat_lo")
        kr_copied = sem("kr_copied")
        rope_step = sem("rope_step")
        mla_turned = sem("mla_turned")
        mla_copied = sem("mla_copied")
        uq_done = sem("uq_done")
        ukv_done = sem("ukv_done")
        z_done = sem("z_done")
        z_abs = sem("z_abs")
        z_exp = sem("z_exp")
        z_ln = sem("z_ln")
        sp_done = sem("sp_done")
        sp_masked = sem("sp_masked")
        stick_sum = sem("stick_sum")
        stick_arg = sem("stick_arg")
        stick_w = sem("stick_w")
        stick_o = sem("stick_o")
        oa_copied = sem("oa_copied")
        bias_in = [sem("bias_in0"), sem("bias_in1")]
        logits_ps = sem("logits_ps")
        max_done = sem("max_done")
        negmax_done = sem("negmax_done")
        probs_done = sem("probs_done")
        probs_turned = sem("probs_turned")
        probs_t_act = sem("probs_t_act")
        probs_t_dve = sem("probs_t_dve")
        inv_done = sem("inv_done")
        pv_done = sem("pv_done")
        o_taken = sem("o_taken")
        o_turned = sem("o_turned")
        o_hi = sem("o_hi")
        o_lo = sem("o_lo")
        sig_done = sem("sig_done")
        masked = sem("masked")
        biased = sem("biased")
        merged_sum = sem("merged_sum")
        merged_hi = sem("merged_hi")
        merged_lo = sem("merged_lo")
        final_sem = sem("final_sem")
        out_sent = sem("out_sent")

        POOL_STEPS = 8 + 2 * 6
        O_SPLITS = 1 + 2 + 2 + 2
        O_TURNS = 6
        N_PT_DVE = N_MLA + N_DIL // 2 + N_X

        def pt_waits(eng, layer, m):
            if m < M_DIL:
                eng.wait_ge(probs_t_dve, layer * N_PT_DVE + m + 1)
            elif m < M_X:
                n = m - M_DIL
                eng.wait_ge(probs_t_act, layer * N_DIL + n + 1)
                if n % 2:
                    eng.wait_ge(probs_t_dve, layer * N_PT_DVE + N_MLA + n // 2 + 1)
            else:
                eng.wait_ge(probs_t_dve, layer * N_PT_DVE + N_MLA + N_DIL // 2 + m - M_X + 1)

        def out_taken(eng, layer, d):
            eng.wait_ge(taken[d % 2], layer * (OUTS // 2) + d // 2 + 1)

        def key_w(m):
            if m < M_DIL:
                return P * (m % 2 + 1)
            if m < M_X:
                return NG * P * (m % 2 + 1)
            return M

        def logits_of(m):
            if M_DIL <= m < M_X:
                return ps[:, 2:4, :].rearrange("p b c -> p (b c)")[:, 0:key_w(m)]
            return ps[:, 2 + m % 2, 0:key_w(m)]

        block = ctx.enter_context(nc.Block())

        @block.sync
        def _(sp):
            for dst, name in ((work[0:BUCKETS, 0:BIAS_W], "c_onehot"),
                              (work[0:NG * HEADS, BIAS_W:2 * BIAS_W], "c_window"),
                              (work[0:BUCKETS, 2 * BIAS_W:2 * BIAS_W + NG * HEADS], "rel_bias"),
                              (ident[:, :], "c_ident")):
                sp.dma_start(dst, a[name]).then_inc(first_in, 16)
            for t in range(TT):
                sp.dma_start(h[:, t * D:(t + 1) * D], a["x"][0, t * P:(t + 1) * P]).then_inc(x_in[t], 16)
            stream = a["weights"]
            for r in range(RING):
                sp.dma_start(slot(raw, r), stream[r]).then_inc(raw_in[r], 16)
            for dst, name in ((tri, "c_tri"), (strict, "c_strict"), (strict_neg, "c_strict_neg"),
                              (causal, "c_causal"), (rope_cs, "c_rope")):
                sp.dma_start(dst[:, :], a[name]).then_inc(const_in, 16)
            sp.wait_ge(bias_row, 1)
            sp.dma_start(bias_dram, work[0:NG * HEADS, 3 * BIAS_W:4 * BIAS_W]).then_inc(bias_out, 16)
            with sp.Fori(1, DEPTH * UNITS // RING) as i:
                for r in range(RING):
                    sp.wait_ge(lo_made, i * RING + (r + 1 - RING))
                    sp.dma_start(slot(raw, r), stream[i * RING + r]).then_inc(raw_in[r], 16)
            for t in range(TT):
                sp.wait_ge(final_sem, t + 1)
                sp.dma_start(out[0, t * P:(t + 1) * P], norm_x[:, t, :]).then_inc(out_sent, 16)
            sp.wait_ge(out_sent, TT * 16)

        @block.gpsimd
        def _(pool):
            pool.memset(minus1[:, :], -1.0).then_inc(setup_mem, 1)
            pool.memset(half_neg[:, :], -0.5).then_inc(setup_mem, 1)
            pool.wait_ge(setup_mem, 2)

            def wait(s, value):
                value = pool.compute_val(value)
                pool.wait_ge(setup_mem, 2)
                pool.wait_ge(s, value)

            def load_gain(layer, j, src):
                if j:
                    wait(x_normed, layer * (4 * NORMS) + 4 * j)
                pool.dma_start(gain, src.partition_broadcast(P)).then_inc(gain_in, 16)

            def rstd_of(n):
                for t in range(TT):
                    wait(mean_done, n * TT + t + 1)
                    pool.tensor_tensor(rstd[:, t:t + 1], mean[:, t:t + 1], half_neg[:, 0:1],
                                       ALU.pow).then_inc(rstd_done, 1)

            with pool.Fori(0, DEPTH) as layer:
                load_gain(layer, N_FFN1, a["ffn1_norm"][layer])
                rstd_of(layer * NORMS + N_FFN1)
                load_gain(layer, N_MIX, a["mix_norm"][layer])
                pool.dma_start(lat_gain[:, 0:Q_RANK], a["mla_q_norm"][layer].partition_broadcast(P)).then_inc(small_in, 16)
                pool.dma_start(lat_gain[:, Q_RANK:Q_RANK + KV_RANK],
                               a["mla_kv_norm"][layer].partition_broadcast(P)).then_inc(small_in, 16)
                pool.dma_start(gate_b[:, :], a["gate_bias"][layer]).then_inc(small_in, 16)
                rstd_of(layer * NORMS + N_MIX)
                wait(lat_sq, layer * 4 + 4)
                for c, rank in ((0, Q_RANK), (1, KV_RANK)):
                    pool.tensor_scalar(lat_ms[:, 2 * c:2 * c + 2], lat_ss[:, 2 * c:2 * c + 2], 1.0 / rank, EPS,
                                       ALU.mult, ALU.add).then_inc(lat_mean, 1)
                wait(lat_mean, layer * 2 + 2)
                pool.tensor_tensor(lat_rs[:, :], lat_ms[:, :], half_neg[:, :], ALU.pow).then_inc(lat_rstd, 1)

                wait(x_turned, layer * (4 * NORMS) + 4 * N_MIX + 4)
                pool.dma_start(norm_x, a["mem"][0].rearrange("(t p) d -> p t d", p=P)).then_inc(mem_in, 16)
                load_gain(layer, N_MEM, a["mem_norm"][layer])
                pool.wait_ge(const_in, 16 * 5)
                pool.wait_ge(bias_out, 16)
                step = [0]

                def tick(ins):
                    step[0] += 1
                    ins.then_inc(rope_step, 1)

                def settled():
                    wait(rope_step, layer * POOL_STEPS + step[0])

                def rotate(x1, x2, y1, y2, cos, sin, t):
                    tick(pool.tensor_tensor(t[0], x1, cos, ALU.mult))
                    tick(pool.tensor_tensor(t[1], x2, sin, ALU.mult))
                    tick(pool.tensor_tensor(t[2], x1, sin, ALU.mult))
                    tick(pool.tensor_tensor(t[3], x2, cos, ALU.mult))
                    settled()
                    tick(pool.tensor_tensor(y1, t[0], t[1], ALU.subtract))
                    tick(pool.tensor_tensor(y2, t[2], t[3], ALU.add))
                    settled()

                wait(kr_copied, layer * TT + TT)
                kr = k_raw[:, :].rearrange("p (t c) -> p t c", t=TT)
                kp = k_pe[:, :].rearrange("p (t c) -> p t c", t=TT)
                tk = [rope_t[:, b, 0:TT * 16].rearrange("p (t c) -> p t c", t=TT) for b in range(4)]
                rotate(kr[:, :, 0:16], kr[:, :, 16:32], kp[:, :, 0:16], kp[:, :, 16:32], cosv, sinv, tk)
                for t in range(TT):
                    tick(pool.tensor_copy(k_cat[:, t, :, NOPE:QK],
                                          kp[:, t, :].unsqueeze(1).broadcast_to([P, HEADS, ROPE])))
                for d in (D_UQ + 2, D_UQ + 3):
                    wait(taken[d % 2], layer * (OUTS // 2) + d // 2 + 1)
                for t in range(TT):
                    tq = [rope_t[:, b, :].rearrange("p (h c) -> p h c", h=HEADS) for b in range(4)]
                    rotate(q_tok[:, t, :, NOPE:NOPE + 16], q_tok[:, t, :, NOPE + 16:QK],
                           q_tok[:, t, :, NOPE:NOPE + 16], q_tok[:, t, :, NOPE + 16:QK],
                           cosv[:, t, :].unsqueeze(1).broadcast_to([P, HEADS, 16]),
                           sinv[:, t, :].unsqueeze(1).broadcast_to([P, HEADS, 16]), tq)
                assert step[0] == POOL_STEPS

                rstd_of(layer * NORMS + N_MEM)

                pool.wait_ge(bias_out, 16)
                for hd in range(HEADS):
                    if hd >= 2:
                        wait(biased, layer * N_DIL + 2 * (hd - 1))
                    src = bass.AP(tensor=bias_dram.tensor, offset=hd * BIAS_W,
                                  ap=[[1, P], [HEADS * BIAS_W, NG], [1, S]])
                    pool.dma_start(bias3[:, hd % 2], src).then_inc(bias_in[hd % 2], 16)

                for j in range(4):
                    c = slice(512 * j, 512 * j + 512)
                    wait(merged_hi, layer * 4 + j + 1)
                    pool.tensor_tensor(v_lo[:, c], merged[:, j, :], v_hi[:, c].bitcast(F32), ALU.subtract)\
                        .then_inc(merged_lo, 1)

                for d in (D_BR + 10, D_BR + 11):
                    wait(taken[d % 2], layer * (OUTS // 2) + d // 2 + 1)
                load_gain(layer, N_XA, a["xattn_norm"][layer])
                rstd_of(layer * NORMS + N_XA)
                load_gain(layer, N_FFN2, a["ffn2_norm"][layer])
                rstd_of(layer * NORMS + N_FFN2)
                wait(x_normed, layer * (4 * NORMS) + 4 * NORMS)
            load_gain(DEPTH, 0, a["final_norm"])
            rstd_of(DEPTH * NORMS)

        @block.scalar
        def _(act):
            def split(layer, u, n):
                act.wait_ge(raw_in[n % RING], (layer * (UNITS // RING) + 1) * 16 + (u - n % RING) * (16 // RING))
                if not (isinstance(u, int) and u < RING):
                    act.wait_ge(unit_used, layer * UNITS + u - (RING - 1))
                act.activation(slot(w_hi, n), slot(raw, n), ACT.Copy).then_inc(hi_made, 1)

            done = [0]

            def ahead(layer, n):
                while done[0] < min(n, UNITS):
                    split(layer, done[0], done[0])
                    done[0] += 1

            def square(n, t, resid_at=None, halves=(0, 1)):
                for b in halves:
                    if resid_at is None:
                        x = norm_x[:, t, 512 * b:512 * b + 512]
                    else:
                        x = h[:, t * D + 512 * b:t * D + 512 * b + 512]
                        act.wait_ge(resid, resid_at + 2 * t + b + 1)
                    if t:
                        act.wait_ge(sq_done, n * 4 + b + 1)
                    act.activation(junk[:, b], x, ACT.Square, scale=D ** -0.5,
                                   accum_out=sumsq[:, 2 * t + b:2 * t + b + 1]).then_inc(sq_done, 1)

            def norm_hi(n, t, dst, banks, halves=(0, 1)):
                for b in halves:
                    act.wait_ge(x_turned, n * 4 + 2 * t + b + 1)
                    o = dst[:, :].rearrange("p (k t) -> p k t", k=KT)[:, 4 * b:4 * b + 4, t * P:(t + 1) * P]
                    act.activation(o, ps[:, banks[2 * t + b], :].rearrange("p (k c) -> p k c", k=4),
                                   ACT.Copy).then_inc(x_hi, 1)

            def norm(layer, j, r, u):
                n = layer * NORMS + j
                square(n, 0, layer * (4 * RESIDUALS) + 4 * r)
                ahead(layer, u + 1)
                for b in range(2):
                    square(n, 1, layer * (4 * RESIDUALS) + 4 * r, (b,))
                    norm_hi(n, 0, u_hi, (4, 5, 6, 7), (b,))
                ahead(layer, u + 3)
                norm_hi(n, 1, u_hi, (4, 5, 6, 7))
                ahead(layer, u + RING)

            def ffn(layer, u0, f):
                def step(i, s):
                    u = u0 + ffn_unit(i) + 1 if isinstance(i, int) else i * 3 + (u0 - LAG + 1)
                    act.wait_ge(unit_used, layer * UNITS + u + 1)
                    c = layer * (2 * FT) + f * FT
                    act.activation(silu_b(s), ps[:, 4 + s % 4, 0:S], ACT.Silu).then_inc(silu_done, 1)
                    act.wait_ge(prod_done, c + i + 1)
                    act.activation(prod_t(v_hi, s), prod_b(s), ACT.Copy).then_inc(prod_hi, 1)

                for i in range(LAG):
                    ahead(layer, u0 + 3 * i + LAG)
                    step(i, i)
                with act.Fori(0, 4) as t:
                    for s in range(4):
                        for j in range(3):
                            n = u0 + 3 * (LAG + s) + j
                            split(layer, t * 12 + n, n)
                        step(t * 4 + (LAG + s), LAG + s)
                done[0] += 48
                for i in range(LAG + 16, FT):
                    ahead(layer, u0 + 3 * i + LAG - (1 if i == FT - 1 else 0))
                    step(i, i)
                ahead(layer, u0 + FFN_UNITS)

            with act.Fori(0, DEPTH) as layer:
                done[0] = 0
                norm(layer, N_FFN1, 0, U_FFN1)
                act.wait_ge(bias_out, 16)
                ffn(layer, U_FFN1, 0)
                norm(layer, N_MIX, 1, U_LAT)

                def take(d, u, dst, src, more=True, **kw):
                    assert d % 2 == 0
                    ahead(layer, u + 4)
                    act.wait_ge(unit_used, layer * UNITS + u + 1)
                    act.activation(dst, src, kw.pop("func", ACT.Copy), **kw).then_inc(taken[0], 1)
                    if more:
                        ahead(layer, u + 5)

                def take_f(d, u, dst, scale=1.0, more=True):
                    take(d, u, dst, ps[:, 0, 0:S], more, scale=scale)

                ahead(layer, U_SBQ + 3)
                act.wait_ge(unit_used, layer * UNITS + U_SBQ)
                for t in range(TT):
                    for c, (bank, w) in enumerate(((2, Q_RANK), (3, KV_RANK))):
                        if t:
                            act.wait_ge(lat_sq, layer * 4 + c + 1)
                        act.activation(junk[:, c, 0:w], ps[:, bank + 2 * t, 0:w], ACT.Square,
                                       accum_out=lat_ss[:, 2 * c + t:2 * c + t + 1]).then_inc(lat_sq, 1)
                ahead(layer, U_SBQ + 4)
                for f in range(0, 4, 2):
                    take_f(D_SBQ + f, U_SBQ + f, sb_q[:, f, :], HD ** -0.5)
                for t in range(TT):
                    act.wait_ge(lat_turned, layer * TT + t + 1)
                    act.activation(v_hi[:, 0:4 * S].rearrange("p (k t) -> p k t", k=4)[:, :, t * P:(t + 1) * P],
                                   ps[:, 6 + t, :].rearrange("p (k c) -> p k c", k=4), ACT.Copy).then_inc(lat_hi, 1)
                for f in range(0, 4, 2):
                    take_f(D_SBK + f, U_SBK + f, sb_k[:, f, :])
                take(D_SBV, U_SBV + 3, sb_v[:, 0, :], ps[:, 2, :])
                for c in range(2):
                    ahead(layer, U_UQ + RING)
                    if c == 0:
                        act.wait_ge(uq_done, layer * 3 + 1)
                    else:
                        act.wait_ge(uq_done, layer * 3 + 3)
                    act.activation(q_tok[:, 0, 4 * c:4 * c + 4, :],
                                   ps[:, 2 * c, 0:384].rearrange("p (h c) -> p h c", h=4), ACT.Copy,
                                   scale=QK ** -0.5).then_inc(taken[0], 1)
                for c in range(2):
                    ahead(layer, U_UKV + 4)
                    act.wait_ge(ukv_done, layer * 3 + 2 * c + 1)
                    kv = ps[:, 4 + 2 * c, :].rearrange("p (h c) -> p h c", h=4)
                    act.activation(k_cat[:, 0, 4 * c:4 * c + 4, 0:NOPE], kv[:, :, 0:NOPE], ACT.Copy)
                    act.activation(mv[:, 0, 256 * c:256 * c + 256].rearrange("p (h c) -> p h c", h=4),
                                   kv[:, :, NOPE:NOPE + HD], ACT.Copy).then_inc(taken[0], 1)

                def take_dil(u):
                    if u < U_DV:
                        i = u - U_DQK
                        g, part, f = i // 8, i % 8 // 4, i % 4
                        if i % 2 == 0:
                            take_f(D_DQK + i, u, (dq, dk)[part][:, g, f, :], (HD ** -0.5, 1.0)[part])
                    elif (u - U_DV) % 4 == 3:
                        g = (u - U_DV) // 4
                        take(D_DV + 2 * g, u, dv[:, g, 0, :], ps[:, 0, :])
                    ahead(layer, u + 5)

                for hd in range(HEADS + 1):
                    u = U_DQK + 2 * hd
                    n = layer * HEADS + hd
                    if hd < HEADS:
                        z = ps[:, 2 + hd % 2, 0:384]
                        act.wait_ge(z_done, n + 1)
                        if hd >= 2:
                            act.wait_ge(sp_done, n - 1)
                        act.activation(sb_soft(hd), z, ACT.Abs).then_inc(z_abs, 1)
                        act.wait_ge(z_abs, n + 1)
                        act.activation(sb_soft(hd), sb_soft(hd), ACT.Exp, scale=-1.0).then_inc(z_exp, 1)
                        act.wait_ge(z_exp, n + 1)
                        act.activation(sb_soft(hd), sb_soft(hd), ACT.Ln, bias=1.0).then_inc(z_ln, 1)
                    if hd >= 1:
                        act.wait_ge(stick_arg, n)
                        act.activation(sb_w(hd - 1), sb_w(hd - 1), ACT.Exp).then_inc(stick_w, 1)
                    take_dil(u)
                    if hd < HEADS:
                        take_dil(u + 1)
                    if hd == HEADS - 3:
                        act.wait_ge(mem_in, layer * 16 + 16)
                        for t in range(TT):
                            square(layer * NORMS + N_MEM, t)

                norm_hi(layer * NORMS + N_MEM, 0, v_hi, (6, 7, 2, 3))
                take_dil(U_DQK + 2 * HEADS + 1)
                norm_hi(layer * NORMS + N_MEM, 1, v_hi, (6, 7, 2, 3))
                take_dil(U_DQK + 2 * HEADS + 2)

                def exp_piece(m):
                    act.wait_ge(negmax_done, layer * PIECES + m + 1)
                    if m >= 2:
                        act.wait_ge(probs_turned, layer * PIECES + m - 1)
                    p = probs_sb(m)[:, 0:key_w(m)]
                    act.activation(p, p if M_DIL <= m < M_X else logits_of(m), ACT.Exp, bias=p_negmax[:, m % 2:m % 2 + 1],
                                   accum_out=p_sum[:, m % 2:m % 2 + 1]).then_inc(probs_done, 1)

                for m in range(N_MLA + 1):
                    if m < N_MLA:
                        exp_piece(m)
                    take_dil(U_DQK + 2 * HEADS + 3 + m)

                def take_gate(u):
                    i = u - U_GATE
                    if i < 24:
                        if i % 2 == 0:
                            take(D_GATE + i, u, kt(sg, i), ps[:, 0, 0:S], False, func=ACT.Identity, bias=gate_b[:, i:i + 1])
                    elif i < 28:
                        if i % 2 == 0:
                            take_f(D_GATE + i, u, x_k[:, i - 24, :], more=False)
                    elif i == 31:
                        take(D_MV, u, x_v[:, 0, :], ps[:, 0, :], False)

                act.wait_ge(small_in, layer * 48 + 48)
                def probs_turn_copy(m):
                    act.wait_ge(probs_turned, layer * PIECES + m + 1)
                    act.wait_ge(pv_done, layer * PIECES + m - 1)
                    w = min(key_w(m), 512)
                    act.activation(probs_t(m)[:, 0:w], ps[:, 4, 0:w], ACT.Copy).then_inc(probs_t_act, 1)

                def heads_hi(turn, dst, bank, t):
                    act.wait_ge(o_turned, layer * O_TURNS + turn + 1)
                    act.activation(dst.rearrange("p (k t) -> p k t", k=4)[:, :, t * P:(t + 1) * P],
                                   ps[:, bank, :].rearrange("p (k c) -> p k c", k=4), ACT.Copy).then_inc(o_hi, 1)

                for i in range(N_DIL):
                    m = M_DIL + i
                    if i >= 1:
                        probs_turn_copy(m - 1)
                    exp_piece(m)
                    ahead(layer, U_GATE + 2 * i + 4)
                    take_gate(U_GATE + 2 * i)
                    ahead(layer, U_GATE + 2 * i + 5)
                    if i == N_DIL - 2:
                        act.wait_ge(unit_used, layer * UNITS + U_MK)
                        act.wait_ge(oa_copied, layer * 4 + 4)
                        act.activation(u_hi[:, 0:4 * S], o_a[:, :], ACT.Copy).then_inc(o_hi, 1)
                    if i == N_DIL - 1:
                        probs_turn_copy(m)
                        for t in range(TT):
                            heads_hi(t, u_hi[:, 4 * S:8 * S], 2 + t, t)
                    take_gate(U_GATE + 2 * i + 1)
                ahead(layer, U_BR + 4)

                out_taken(act, layer, D_GATE + 23)
                for b in range(3):
                    if b == 2:
                        ahead(layer, U_BR + 8)
                        act.wait_ge(unit_used, layer * UNITS + U_BR + 4)
                        for t in range(TT):
                            heads_hi(TT + t, u_hi[:, 0:4 * S], 6 + t, t)
                    out_taken(act, layer, D_GATE + 22)
                    s = sg[:, b * KT * S:(b + 1) * KT * S]
                    act.activation(s, s, ACT.Sigmoid).then_inc(sig_done, 1)
                ahead(layer, U_BR + 8 + RING)
                for j in range(4):
                    ahead(layer, U_BR + 8 + j + 5)
                    act.wait_ge(merged_sum, layer * 8 + 4 + j + 1)
                    act.activation(v_hi[:, 512 * j:512 * j + 512], merged[:, j, :], ACT.Copy).then_inc(merged_hi, 1)
                ahead(layer, U_XQ)
                norm(layer, N_XA, 2, U_XQ)
                take(D_XQ, U_XQ + 1, x_q[:, 0:2, :], ps[:, 0, :].rearrange("p (f t) -> p f t", f=2), scale=XD ** -0.5)
                ahead(layer, U_XO + 3)
                for i in range(N_X):
                    exp_piece(M_X + i)
                    if i == 2:
                        ahead(layer, U_XO + XH)
                    if i == X_TURN:
                        heads_hi(2 * TT, v_hi[:, 0:4 * S], 1, 0)
                heads_hi(2 * TT + 1, v_hi[:, 0:4 * S], 6, 1)
                norm(layer, N_FFN2, 3, U_FFN2)
                ffn(layer, U_FFN2, 1)
                assert done[0] == UNITS
            for t in range(TT):
                square(DEPTH * NORMS, t, DEPTH * 4 * RESIDUALS)

        @block.vector
        def _(dve):
            def split(layer, u, n):
                dve.wait_ge(hi_made, layer * UNITS + u + 1)
                dve.tensor_tensor(slot(w_lo, n), slot(raw, n), slot(w_hi, n).bitcast(F32), ALU.subtract).then_inc(lo_made, 1)

            done = [0]

            def ahead(layer, n):
                while done[0] < min(n, UNITS):
                    split(layer, done[0], done[0])
                    done[0] += 1

            def rest(dst, src, hi, s, n=1):
                dve.tensor_tensor(dst, src, hi.bitcast(F32), ALU.subtract).then_inc(s, n)

            def mean_of(n, t):
                dve.wait_ge(sq_done, n * 4 + 2 * t + 1)
                dve.tensor_scalar(half_mean[:, t:t + 1], sumsq[:, 2 * t:2 * t + 1], EPS, None,
                                  ALU.add).then_inc(half_done, 1)
                dve.wait_ge(half_done, n * TT + t + 1)
                dve.wait_ge(sq_done, n * 4 + 2 * t + 2)
                dve.tensor_tensor(mean[:, t:t + 1], sumsq[:, 2 * t + 1:2 * t + 2], half_mean[:, t:t + 1],
                                  ALU.add).then_inc(mean_done, 1)

            def normalise(n, t, src, mean=True):
                if mean:
                    mean_of(n, t)
                dve.wait_ge(rstd_done, n * TT + t + 1)
                for b in range(2):
                    w = slice(512 * b, 512 * b + 512)
                    dve.scalar_tensor_tensor(out=norm_x[:, t, w], in0=src[:, w], scalar=rstd[:, t:t + 1],
                                             in1=gain[:, w], op0=ALU.mult, op1=ALU.mult).then_inc(x_normed, 1)

            def norm_lo(n, t, hi, lo, banks, halves=(0, 1)):
                for b in halves:
                    dve.wait_ge(x_hi, n * 4 + 2 * t + b + 1)

                    def part(x):
                        return x[:, :].rearrange("p (k t) -> p k t", k=KT)[:, 4 * b:4 * b + 4, t * P:(t + 1) * P]
                    rest(part(lo), ps[:, banks[2 * t + b], :].rearrange("p (k c) -> p k c", k=4), part(hi), x_lo)

            def residual(layer, r, t, u, scale, halves=(0, 1)):
                for c in halves:
                    if 2 * t + c < 3:
                        dve.wait_ge(y_part, layer * (3 * RESIDUALS) + 3 * r + 2 * t + c + 1)
                    else:
                        dve.wait_ge(unit_used, layer * UNITS + u + 1)
                    hh = h[:, t * D + 512 * c:t * D + 512 * c + 512]
                    dve.scalar_tensor_tensor(out=hh, in0=ps[:, 2 * t + c, :], scalar=scale, in1=hh,
                                             op0=ALU.mult, op1=ALU.add).then_inc(resid, 1)

            def norm(layer, j, u, second):
                n = layer * NORMS + j
                dve.wait_ge(gain_in, (n + 1) * 16)
                normalise(n, 0, h[:, 0:D])
                second((0,))
                ahead(layer, u + 1)
                second((1,))
                norm_lo(n, 0, u_hi, u_lo, (4, 5, 6, 7), (0,))
                mean_of(n, 1)
                norm_lo(n, 0, u_hi, u_lo, (4, 5, 6, 7), (1,))
                normalise(n, 1, h[:, D:2 * D], mean=False)
                ahead(layer, u + 2)
                norm_lo(n, 1, u_hi, u_lo, (4, 5, 6, 7))
                ahead(layer, u + RING)

            def ffn(layer, u0, f):
                c = layer * (2 * FT) + f * FT

                def step(i, s):
                    dve.wait_ge(silu_done, c + i + 1)
                    dve.tensor_tensor(prod_b(s), ps[:, 4 + s % 4, S:2 * S], silu_b(s), ALU.mult).then_inc(prod_done, 1)
                    dve.wait_ge(prod_hi, c + i + 1)
                    rest(prod_t(v_lo, s), prod_b(s), prod_t(v_hi, s), prod_lo)

                for i in range(LAG):
                    ahead(layer, u0 + 3 * i + LAG)
                    step(i, i)
                with dve.Fori(0, 4) as t:
                    for s in range(4):
                        for j in range(3):
                            n = u0 + 3 * (LAG + s) + j
                            split(layer, t * 12 + n, n)
                        step(t * 4 + (LAG + s), LAG + s)
                done[0] += 48
                for i in range(LAG + 16, FT):
                    ahead(layer, u0 + 3 * i + LAG - (1 if i == FT - 1 else 0))
                    step(i, i)
                ahead(layer, u0 + FFN_UNITS)

            dve.wait_ge(bias_mm, 1)
            dve.tensor_tensor(work[0:NG * HEADS, 3 * BIAS_W:4 * BIAS_W], ps[0:NG * HEADS, 0, 0:BIAS_W],
                              work[0:NG * HEADS, BIAS_W:2 * BIAS_W], ALU.add).then_inc(bias_row, 1)
            for i, x in enumerate((p_max, p_negmax, p_sum, p_inv)):
                dve.wait_ge(x_in[i // 2], 16)
                dve.memset(x[:, :], 0.0).then_inc(resid, 1)
            with dve.Fori(0, DEPTH) as layer:
                done[0] = 0
                norm(layer, N_FFN1, U_FFN1, lambda half: None)
                dve.wait_ge(bias_out, 16)
                ffn(layer, U_FFN1, 0)
                residual(layer, 0, 0, U_LAT - 1, 0.5)
                norm(layer, N_MIX, U_LAT, lambda half: residual(layer, 0, 1, U_LAT - 1, 0.5, half))

                def take(d, u, dst, src, op=None, more=True):
                    assert d % 2 == 1
                    ahead(layer, u + 4)
                    dve.wait_ge(unit_used, layer * UNITS + u + 1)
                    if op is None:
                        ins = dve.tensor_copy(dst, src)
                    else:
                        ins = dve.tensor_scalar(dst, src, op[1], None, op[0])
                    ins.then_inc(taken[1], 1)
                    if more:
                        ahead(layer, u + 5)

                def take_f(d, u, dst, scale=None, more=True):
                    take(d, u, dst, ps[:, 1, 0:S], None if scale is None else (ALU.mult, scale), more)

                ahead(layer, U_SBQ + 3)
                for t in range(TT):
                    dve.wait_ge(lat_sq, layer * 4 + 2 * t + 2)
                    dve.tensor_copy(k_raw[:, t * ROPE:(t + 1) * ROPE], ps[:, 3 + 2 * t, KV_RANK:KV_RANK + ROPE])\
                        .then_inc(kr_copied, 1)
                ahead(layer, U_SBQ + 4)
                dve.wait_ge(small_in, layer * 48 + 48)
                dve.wait_ge(lat_rstd, layer + 1)
                for t in range(TT):
                    for c, (bank, lo, hi) in enumerate(((2, 0, Q_RANK), (3, Q_RANK, 512))):
                        last = dve.scalar_tensor_tensor(out=lat_n[:, t, lo:hi], in0=ps[:, bank + 2 * t, 0:hi - lo],
                                                        scalar=lat_rs[:, 2 * c + t:2 * c + t + 1],
                                                        in1=lat_gain[:, lo:hi], op0=ALU.mult, op1=ALU.mult)
                    last.then_inc(lat_normed, 1)
                for f in range(1, 4, 2):
                    take_f(D_SBQ + f, U_SBQ + f, sb_q[:, f, :], HD ** -0.5)
                for t in range(TT):
                    dve.wait_ge(lat_hi, layer * TT + t + 1)

                    def part(x):
                        return x[:, 0:4 * S].rearrange("p (k t) -> p k t", k=4)[:, :, t * P:(t + 1) * P]
                    rest(part(v_lo), ps[:, 6 + t, :].rearrange("p (k c) -> p k c", k=4), part(v_hi), lat_lo)
                for f in range(1, 4, 2):
                    take_f(D_SBK + f, U_SBK + f, sb_k[:, f, :])
                take(D_SBV + 1, U_SBV + 3, sb_v[:, 1, :], ps[:, 3, :])
                for c in range(2):
                    ahead(layer, U_UQ + RING)
                    if c == 0:
                        dve.wait_ge(uq_done, layer * 3 + 2)
                    else:
                        dve.wait_ge(unit_used, layer * UNITS + U_UKV)
                    dve.tensor_scalar(q_tok[:, 1, 4 * c:4 * c + 4, :],
                                      ps[:, 2 * c + 1, 0:384].rearrange("p (h c) -> p h c", h=4), QK ** -0.5, None,
                                      ALU.mult).then_inc(taken[1], 1)
                for c in range(2):
                    ahead(layer, U_UKV + 4)
                    if c == 0:
                        dve.wait_ge(ukv_done, layer * 3 + 2)
                    else:
                        dve.wait_ge(unit_used, layer * UNITS + U_UKV + 1)
                    kv = ps[:, 5 + 2 * c, :].rearrange("p (h c) -> p h c", h=4)
                    dve.tensor_copy(k_cat[:, 1, 4 * c:4 * c + 4, 0:NOPE], kv[:, :, 0:NOPE])
                    dve.tensor_copy(mv[:, 1, 256 * c:256 * c + 256].rearrange("p (h c) -> p h c", h=4),
                                    kv[:, :, NOPE:NOPE + HD]).then_inc(taken[1], 1)

                def take_dil(u, more=True):
                    if u < U_DV:
                        i = u - U_DQK
                        g, part, f = i // 8, i % 8 // 4, i % 4
                        if i % 2 == 1:
                            take_f(D_DQK + i, u, (dq, dk)[part][:, g, f, :], (HD ** -0.5, None)[part], more)
                    elif (u - U_DV) % 4 == 3:
                        g = (u - U_DV) // 4
                        take(D_DV + 2 * g + 1, u, dv[:, g, 1, :], ps[:, 1, :], more=more)
                    if more:
                        ahead(layer, u + 5)

                def take_pair(pair):
                    dve.wait_ge(stick_o, layer * HEADS + 2 * pair + 2)
                    dve.tensor_copy(oa[:, pair, :], ps[:, 4 + pair % 2, 0:S]).then_inc(oa_copied, 1)

                dve.wait_ge(const_in, 16 * 5)
                dve.wait_ge(gain_in, (layer * NORMS + N_MEM + 1) * 16)
                for hd in range(HEADS + 1):
                    u = U_DQK + 2 * hd
                    n = layer * HEADS + hd
                    if hd >= 1:
                        e = sb_w(hd - 1)
                        dve.wait_ge(stick_sum, n)
                        if hd - 1 >= 2:
                            dve.wait_ge(stick_o, n - 2)
                        dve.tensor_tensor(e, ps[:, 2 + (hd - 1) % 2, 0:384], strict_neg[:, :], ALU.add).then_inc(stick_arg, 1)
                    if hd < HEADS:
                        dve.wait_ge(z_ln, n + 1)
                        if hd >= 2:
                            dve.wait_ge(stick_sum, n - 1)
                        dve.scalar_tensor_tensor(out=sb_sp(hd), in0=ps[:, 2 + hd % 2, 0:384], scalar=0.0,
                                                 in1=sb_soft(hd), op0=ALU.max, op1=ALU.add).then_inc(sp_done, 1)
                        dve.wait_ge(sp_done, n + 1)
                        diag = sb_sp(hd).rearrange("p (b c) -> p b c", b=3)[:, 0:3:2, :]
                        dve.tensor_tensor(diag, diag, strict[:, :].unsqueeze(1).broadcast_to([P, 2, P]),
                                          ALU.mult).then_inc(sp_masked, 1)
                    if hd == HEADS:
                        normalise(layer * NORMS + N_MEM, 1, norm_x[:, 1, :], mean=False)
                    take_dil(u)
                    if hd < HEADS:
                        dve.wait_ge(mla_turned, n + 1)
                        dst = (mk if hd < 4 else mq)[0:QK, 2 * (hd % 4):2 * (hd % 4) + 2, :]
                        dve.tensor_copy(dst, ps[0:QK, 6 + hd % 2, :].rearrange("p (h t) -> p h t", h=2)).then_inc(mla_copied, 1)
                        if hd == HEADS - 1:
                            normalise(layer * NORMS + N_MEM, 0, norm_x[:, 0, :], mean=False)
                        take_dil(u + 1)
                    if hd == HEADS - 2:
                        for t in range(TT):
                            mean_of(layer * NORMS + N_MEM, t)
                    if hd % 2 == 0 and 1 <= hd < HEADS:
                        take_pair(hd // 2 - 1)

                norm_lo(layer * NORMS + N_MEM, 0, v_hi, v_lo, (6, 7, 2, 3))
                take_dil(U_DQK + 2 * HEADS + 1, more=False)
                norm_lo(layer * NORMS + N_MEM, 1, v_hi, v_lo, (6, 7, 2, 3))
                ahead(layer, U_DQK + 2 * HEADS + 6)
                take_pair(3)
                take_dil(U_DQK + 2 * HEADS + 2)

                def soft_front(m):
                    base = layer * PIECES + m
                    dve.wait_ge(logits_ps, base + 1)
                    if m >= 2:
                        dve.wait_ge(probs_done, base - 1)
                    src = logits_of(m)
                    if m < M_DIL:
                        block = src[:, m % 2 * P:(m % 2 + 1) * P]
                        dve.tensor_tensor(block, block, causal[:, :], ALU.add).then_inc(masked, 1)
                        dve.wait_ge(masked, layer * N_MLA + m + 1)
                    if M_DIL <= m < M_X:
                        hd, t = divmod(m - M_DIL, 2)
                        kw = P * (t + 1)
                        if t == 0:
                            dve.wait_ge(bias_in[hd % 2], (layer * (HEADS // 2) + hd // 2 + 1) * 16)
                        dve.wait_ge(probs_turned, base - 1)
                        src = probs_sb(m)[:, 0:NG * kw]
                        rows = bias3[:, hd % 2]
                        last_key_down = bass.AP(tensor=rows.tensor, offset=rows.offset + kw - 1,
                                                ap=[rows.ap[0], [S, NG], [-1, kw]])
                        dve.tensor_tensor(src.rearrange("p (g k) -> p g k", g=NG),
                                          logits_of(m).rearrange("p (g k) -> p g k", g=NG), last_key_down,
                                          ALU.add).then_inc(biased, 1)
                        dve.wait_ge(biased, layer * N_DIL + m - M_DIL + 1)
                    dve.reduce_max(p_max[:, m % 2:m % 2 + 1], src, AX.X).then_inc(max_done, 1)
                    dve.wait_ge(max_done, base + 1)
                    dve.tensor_scalar(p_negmax[:, m % 2:m % 2 + 1], p_max[:, m % 2:m % 2 + 1], -1.0, None,
                                      ALU.mult).then_inc(negmax_done, 1)

                def soft_back(m):
                    base = layer * PIECES + m
                    w = key_w(m)
                    if m < M_DIL or m >= M_X or m % 2:
                        dve.wait_ge(probs_turned, base + 1)
                        if m >= 2:
                            dve.wait_ge(pv_done, base - 1)
                        if m < M_DIL or m >= M_X:
                            dve.tensor_copy(probs_t(m)[:, 0:w], ps[:, 4 + m % 2, 0:w]).then_inc(probs_t_dve, 1)
                        else:
                            dve.tensor_copy(probs_t(m)[:, 512:w], ps[:, 5, 0:w - 512]).then_inc(probs_t_dve, 1)
                    dve.wait_ge(probs_done, base + 1)
                    if m >= M_X + 2:
                        dve.wait_ge(o_taken, base - 1)
                    dve.reciprocal(p_inv[:, m % 2:m % 2 + 1], p_sum[:, m % 2:m % 2 + 1]).then_inc(inv_done, 1)

                def take_o(m):
                    base = layer * PIECES + m
                    if m < M_DIL:
                        t, c, dst = m % 2, HD * (m // 2), o_b
                        w = HD
                    elif m < M_X:
                        t, c, dst = m % 2, HD * ((m - M_DIL) // 2), o_c
                        w = HD
                    else:
                        t, c, dst = (m - M_X) // XH, XD * ((m - M_X) % XH), o_b
                        w = XD
                    dve.wait_ge(inv_done, base + 1)
                    dve.wait_ge(pv_done, base + 1)
                    dve.tensor_scalar(dst[:, t * WIDTH + c:t * WIDTH + c + w], ps[:, 6 + m % 2, 0:w],
                                      p_inv[:, m % 2:m % 2 + 1], None, ALU.mult).then_inc(o_taken, 1)

                for m in range(N_MLA + 1):
                    if m >= 1:
                        soft_back(m - 1)
                    if m < N_MLA:
                        soft_front(m)
                    ahead(layer, U_DQK + 2 * HEADS + 3 + m + 4)
                    take_dil(U_DQK + 2 * HEADS + 3 + m, more=False)
                    if m >= 1:
                        take_o(m - 1)

                def take_gate(u):
                    i = u - U_GATE
                    if i < 24:
                        if i % 2 == 1:
                            take(D_GATE + i, u, kt(sg, i), ps[:, 1, 0:S], (ALU.add, gate_b[:, i:i + 1]), False)
                    elif i < 28:
                        if i % 2 == 1:
                            take_f(D_GATE + i, u, x_k[:, i - 24, :], more=False)
                    elif i == 31:
                        take(D_MV + 1, u, x_v[:, 1, :], ps[:, 1, :], more=False)

                def heads_lo(turn, lo, hi, bank, t):
                    dve.wait_ge(o_hi, layer * O_SPLITS + 1 + turn + 1)

                    def part(x):
                        return x.rearrange("p (k t) -> p k t", k=4)[:, :, t * P:(t + 1) * P]
                    rest(part(lo), ps[:, bank, :].rearrange("p (k c) -> p k c", k=4), part(hi), o_lo)

                for i in range(N_DIL):
                    m = M_DIL + i
                    if i >= 1:
                        soft_back(m - 1)
                    soft_front(m)
                    ahead(layer, U_GATE + 2 * i + 4)
                    take_gate(U_GATE + 2 * i)
                    ahead(layer, U_GATE + 2 * i + 5)
                    if i >= 1:
                        take_o(m - 1)
                    if i == N_DIL - 2:
                        dve.wait_ge(o_hi, layer * O_SPLITS + 1)
                        rest(u_lo[:, 0:4 * S], o_a[:, :], u_hi[:, 0:4 * S], o_lo)
                    if i == N_DIL - 1:
                        soft_back(m)
                        for t in range(TT):
                            heads_lo(t, u_lo[:, 4 * S:8 * S], u_hi[:, 4 * S:8 * S], 2 + t, t)
                    take_gate(U_GATE + 2 * i + 1)
                ahead(layer, U_BR + 4)
                take_o(M_X - 1)

                for b in range(3):
                    if b == 1:
                        for t in range(TT):
                            heads_lo(TT + t, u_lo[:, 0:4 * S], u_hi[:, 0:4 * S], 6 + t, t)
                    dve.wait_ge(sig_done, layer * 3 + b + 1)
                    for j in range(4):
                        d = D_BR + 4 * b + j
                        u = U_BR + 4 * b + j
                        ahead(layer, u + 4)
                        dve.wait_ge(unit_used, layer * UNITS + u + 1)
                        g = sg[:, b * KT * S + 512 * j:b * KT * S + 512 * j + 512]
                        if b == 0:
                            dve.tensor_tensor(merged[:, j, :], ps[:, 4 + d % 2, :], g, ALU.mult).then_inc(taken[d % 2], 1)
                        else:
                            if 4 * b + j - 4 >= 2:
                                dve.wait_ge(merged_sum, layer * 8 + 4 * (b - 1) + j - 1)
                            dve.tensor_tensor(addend[:, j % 2, :], ps[:, 4 + d % 2, :], g, ALU.mult).then_inc(taken[d % 2], 1)
                            out_taken(dve, layer, d)
                            dve.tensor_tensor(merged[:, j, :], merged[:, j, :], addend[:, j % 2, :], ALU.add)\
                                .then_inc(merged_sum, 1)
                        ahead(layer, u + 5)
                ahead(layer, U_XQ)
                residual(layer, 1, 0, U_XQ - 1, 1.0)
                norm(layer, N_XA, U_XQ, lambda half: residual(layer, 1, 1, U_XQ - 1, 1.0, half))
                ahead(layer, U_XO + 3)
                dve.wait_ge(unit_used, layer * UNITS + U_XO)
                dve.tensor_scalar(x_q[:, 2:4, :], ps[:, 1, :].rearrange("p (f t) -> p f t", f=2), XD ** -0.5, None,
                                  ALU.mult).then_inc(taken[1], 1)
                for i in range(N_X + 2):
                    m = M_X + i
                    if i < N_X:
                        soft_front(m)
                    if 1 <= i <= N_X:
                        soft_back(m - 1)
                    if i == X_TURN + 1:
                        heads_lo(2 * TT, v_lo[:, 0:4 * S], v_hi[:, 0:4 * S], 1, 0)
                    if i >= 2:
                        take_o(m - 2)
                    if i == 3:
                        ahead(layer, U_XO + XH)
                heads_lo(2 * TT + 1, v_lo[:, 0:4 * S], v_hi[:, 0:4 * S], 6, 1)
                residual(layer, 2, 0, U_FFN2 - 1, 1.0)
                norm(layer, N_FFN2, U_FFN2, lambda half: residual(layer, 2, 1, U_FFN2 - 1, 1.0, half))
                ffn(layer, U_FFN2, 1)
                for t in range(TT):
                    residual(layer, 3, t, UNITS - 1, 0.5)
                assert done[0] == UNITS
            dve.wait_ge(gain_in, (DEPTH * NORMS + 1) * 16)
            for t in range(TT):
                mean_of(DEPTH * NORMS, t)
            for t in range(TT):
                dve.wait_ge(rstd_done, DEPTH * NORMS * TT + t + 1)
                dve.scalar_tensor_tensor(out=norm_x[:, t, :], in0=h[:, t * D:(t + 1) * D], scalar=rstd[:, t:t + 1],
                                         in1=gain, op0=ALU.mult, op1=ALU.mult).then_inc(final_sem, 1)

        @block.tensor
        def _(pe):
            def ready(layer, u):
                pe.wait_ge(lo_made, layer * UNITS + u + 1)

            def mm3(o, ah, al, bh, bl, first, last):
                pe.matmul(o, ah, bh, start=first, stop=False)
                pe.matmul(o, ah, bl, start=False, stop=False)
                return pe.matmul(o, al, bh, start=False, stop=last)

            def weights_still(o, n, j, c, x_hi_, x_lo_, k, first, last):
                w = slice(j * c, j * c + P)
                return mm3(o, slot(w_hi, n)[:, w], slot(w_lo, n)[:, w], kt(x_hi_, k), kt(x_lo_, k), first, last)

            def tokens_still(o, x_hi_, x_lo_, k, t, n, c0, c1, first, last):
                x = slice(k * S + t * P, k * S + t * P + P)
                return mm3(o, x_hi_[:, x], x_lo_[:, x], slot(w_hi, n)[:, c0:c1], slot(w_lo, n)[:, c0:c1], first, last)

            def feature_unit(layer, u, n, o, x_hi_, x_lo_):
                ready(layer, u)
                for k in range(KT):
                    last = weights_still(o, n, k, P, x_hi_, x_lo_, k, k == 0, k == KT - 1)
                last.then_inc(unit_used, 1)

            def bank_free(layer, d):
                if d >= 2:
                    pe.wait_ge(taken[d % 2], layer * (OUTS // 2) + d // 2)

            def feature_out(layer, d, u, x_hi_=u_hi, x_lo_=u_lo):
                bank_free(layer, d)
                feature_unit(layer, u, u, ps[:, d % 2, 0:S], x_hi_, x_lo_)

            def token_unit(layer, u, j, banks, x_hi_=u_hi, x_lo_=u_lo):
                ready(layer, u)
                for kk in range(2):
                    k = 2 * j + kk
                    for t in range(TT):
                        last = tokens_still(ps[:, banks[t], :], x_hi_, x_lo_, k, t, u, 512 * kk, 512 * kk + 512,
                                            k == 0, k == KT - 1)
                last.then_inc(unit_used, 1)

            def token_out(layer, d, u, j, x_hi_=u_hi, x_lo_=u_lo):
                if j == 0:
                    bank_free(layer, d)
                    bank_free(layer, d + 1)
                token_unit(layer, u, j, (d % 2, (d + 1) % 2), x_hi_, x_lo_)

            def row_unit(layer, u, n, x_hi_, x_lo_, k, first, last):
                ready(layer, u)
                for t in range(TT):
                    for c in range(2):
                        ins = tokens_still(ps[:, 2 * t + c, :], x_hi_, x_lo_, k, t, n, 512 * c, 512 * c + 512,
                                           first, last)
                ins.then_inc(unit_used, 1)

            def row_quarter(layer, i, u0, j0, j1, n, x_hi_, x_lo_, tiles, whole):
                t, c = divmod(i, 2)
                for j in range(j0, j1):
                    if i == 0:
                        ready(layer, u0 + j)
                    last = tokens_still(ps[:, i, :], x_hi_, x_lo_, tiles[j], t, u0 + j,
                                        512 * c, 512 * c + 512, whole and j == 0, j == n - 1)
                    if i == 2 * TT - 1:
                        last.then_inc(unit_used, 1)
                    elif j == n - 1:
                        last.then_inc(y_part, 1)

            def row_tail(layer, u0, n, x_hi_, x_lo_, tiles):
                for i in range(2 * TT):
                    row_quarter(layer, i, u0, 0, n, n, x_hi_, x_lo_, tiles, False)

            def turn_norm(n, t, banks):
                for b in range(2):
                    pe.wait_ge(x_normed, n * 4 + 2 * t + b + 1)
                    for k in range(4):
                        last = pe.transpose(ps[:, banks[2 * t + b], P * k:P * k + P],
                                            norm_x[:, t, (4 * b + k) * P:(4 * b + k + 1) * P], ident[:, :])
                    last.then_inc(x_turned, 1)

            def stay_warm():
                for _ in range(WARM):
                    pe.matmul(ps[:, 7, 0:P], ident[:, :], ident[:, :], start=True, stop=True)

            def tokens_after_norm(layer, j, u, part):
                n = layer * NORMS + j
                turn_norm(n, 0, (4, 5, 6, 7))
                stay_warm()
                for i in range(2):
                    if i == 1:
                        turn_norm(n, 1, (4, 5, 6, 7))
                    ready(layer, u + i)
                    if i == 0:
                        pe.wait_ge(x_lo, n * 4 + 2)
                    part(i, 0)
                pe.wait_ge(x_lo, n * 4 + 4)
                for i in range(2):
                    part(i, 1).then_inc(unit_used, 1)

            def feature_after_norm(layer, j, u, o):
                n = layer * NORMS + j
                turn_norm(n, 0, (4, 5, 6, 7))
                stay_warm()
                turn_norm(n, 1, (4, 5, 6, 7))
                ready(layer, u)
                for k in range(KT):
                    if k % 4 == 0:
                        pe.wait_ge(x_lo, n * 4 + 3 + k // 4)
                    last = weights_still(o, u, k, P, u_hi, u_lo, k, k == 0, k == KT - 1)
                last.then_inc(unit_used, 1)

            def ffn(layer, u0, f):
                c = layer * (2 * FT) + f * FT

                def gate_up(u, n, s):
                    for j in range(2):
                        feature_unit(layer, u + j, n + j, ps[:, 4 + s % 4, j * S:(j + 1) * S], u_hi, u_lo)

                def down(i, u, n, s, first):
                    pe.wait_ge(prod_lo, c + i + 1)
                    row_unit(layer, u, n, v_hi, v_lo, s % 4, first, False)

                feature_after_norm(layer, (N_FFN1, N_FFN2)[f], u0, ps[:, 4, 0:S])
                feature_unit(layer, u0 + 1, u0 + 1, ps[:, 4, S:2 * S], u_hi, u_lo)
                gate_up(u0 + 2, u0 + 2, 1)
                gate_up(u0 + 4, u0 + 4, 2)
                gate_up(u0 + 6, u0 + 6, 3)
                down(0, u0 + 8, u0 + 8, 0, True)
                for s in range(3):
                    gate_up(u0 + 9 + 3 * s, u0 + 9 + 3 * s, 4 + s)
                    down(1 + s, u0 + 11 + 3 * s, u0 + 11 + 3 * s, 1 + s, False)
                with pe.Fori(0, 3) as t:
                    for s in range(4):
                        n = u0 + 18 + 3 * s
                        gate_up(t * 12 + n, n, 7 + s)
                        down(t * 4 + (4 + s), t * 12 + (n + 2), n + 2, 4 + s, False)
                for i in range(19, FT):
                    gate_up(u0 + ffn_unit(i), u0 + ffn_unit(i), i)
                    down(i - LAG, u0 + down_unit(i - LAG), u0 + down_unit(i - LAG), i - LAG, False)
                pe.wait_ge(prod_lo, c + FT)
                row_tail(layer, u0 + FFN_UNITS - LAG, LAG, v_hi, v_lo, [i % 4 for i in range(FT - LAG, FT)])

            pe.wait_ge(first_in, 16 * 4)
            pe.wait_ge(setup_mem, 2)
            pe.matmul(ps[0:NG * HEADS, 0, 0:BIAS_W], work[0:BUCKETS, 2 * BIAS_W:2 * BIAS_W + NG * HEADS],
                      work[0:BUCKETS, 0:BIAS_W], start=True, stop=True).then_inc(bias_mm, 1)
            with pe.Fori(0, DEPTH) as layer:
                ffn(layer, U_FFN1, 0)
                pe.wait_ge(const_in, 16 * 5)

                def latent(i, t):
                    tokens_still(ps[:, 2 + 2 * t, 0:Q_RANK], u_hi, u_lo, i, t, U_LAT + i, 0, Q_RANK,
                                 i == 0, i == KT - 1)
                    return tokens_still(ps[:, 3 + 2 * t, 0:256], u_hi, u_lo, i, t, U_LAT + i, Q_RANK, Q_RANK + 256,
                                        i == 0, i == KT - 1)

                tokens_after_norm(layer, N_MIX, U_LAT, latent)
                for i in range(2, KT):
                    ready(layer, U_LAT + i)
                    for t in range(TT):
                        last = latent(i, t)
                    last.then_inc(unit_used, 1)
                for f in range(4):
                    feature_out(layer, D_SBQ + f, U_SBQ + f)
                for t in range(TT):
                    pe.wait_ge(lat_normed, layer * TT + t + 1)
                    for k in range(4):
                        last = pe.transpose(ps[:, 6 + t, k * P:(k + 1) * P], lat_n[:, t, k * P:(k + 1) * P], ident[:, :])
                    last.then_inc(lat_turned, 1)
                for f in range(4):
                    feature_out(layer, D_SBK + f, U_SBK + f)
                for j in range(4):
                    token_unit(layer, U_SBV + j, j, (2, 3))
                pe.wait_ge(lat_lo, layer * TT + TT)
                for c in range(2):
                    for t in range(TT):
                        out_taken(pe, layer, (D_SBK + 2, D_SBV)[c] + t)
                        for k in range(3):
                            if c == 0 and t == 0:
                                ready(layer, U_UQ + k)
                            last = tokens_still(ps[:, 2 * c + t, 0:384], v_hi, v_lo, k, t, U_UQ + k, 384 * c, 384 * c + 384,
                                                k == 0, k == 2)
                            if c == 1 and t == 1:
                                last.then_inc(unit_used, 1)
                        if c == 0 or t == 0:
                            last.then_inc(uq_done, 1)
                ready(layer, U_UKV)
                for c in range(2):
                    for t in range(TT):
                        last = tokens_still(ps[:, 4 + 2 * c + t, :], v_hi, v_lo, 3, t, U_UKV, 512 * c, 512 * c + 512, True, True)
                        if c == 0 or t == 0:
                            last.then_inc(ukv_done, 1)
                last.then_inc(unit_used, 1)

                def dil_unit(u):
                    if u < U_DV:
                        feature_out(layer, D_DQK + u - U_DQK, u)
                    else:
                        g, j = divmod(u - U_DV, 4)
                        token_out(layer, D_DV + 2 * g, u, j)

                def stick_times_v(g):
                    r = slice(HD * (g % 2), HD * (g % 2) + HD)
                    o = ps[r, 4 + (g // 2) % 2, :]
                    pe.wait_ge(stick_w, layer * HEADS + g + 1)
                    if g % 2 == 0 and g >= 4:
                        pe.wait_ge(oa_copied, layer * 4 + g // 2 - 1)
                    pe.matmul(o[:, 0:S], sb_v[:, 0, g * HD:(g + 1) * HD], sb_w(g)[:, 0:S], start=True, stop=False)
                    pe.matmul(o[:, P:S], sb_v[:, 1, g * HD:(g + 1) * HD], sb_w(g)[:, S:S + P], start=False,
                              stop=True).then_inc(stick_o, 1)

                out_taken(pe, layer, D_UQ + 2)
                out_taken(pe, layer, D_UQ + 3)
                for hd in range(HEADS + 1):
                    n = layer * HEADS + hd
                    u = U_DQK + 2 * hd
                    if hd < HEADS:
                        r = slice(HD * (hd % 2), HD * (hd % 2) + HD)
                        f = hd // 2
                        if hd >= 2:
                            pe.wait_ge(stick_arg, n - 1)
                        z = ps[:, 2 + hd % 2, :]
                        pe.matmul(z[:, 0:S], sb_k[r, f, 0:P], sb_q[r, f, :], start=True, stop=True)
                        pe.matmul(z[:, S:S + P], sb_k[r, f, P:S], sb_q[r, f, P:S], start=False, stop=True,
                                  skip_group_check=True).then_inc(z_done, 1)
                    if hd >= 1:
                        z = ps[:, 2 + (hd - 1) % 2, :]
                        sp_ = sb_sp(hd - 1)
                        pe.wait_ge(sp_masked, n)
                        pe.matmul(z[:, 0:S], tri[:, :], sp_[:, 0:S], start=False, stop=True, skip_group_check=True)
                        pe.matmul(z[:, P:S], minus1[:, :], sp_[:, S:S + P], start=False, stop=True,
                                  skip_group_check=True)
                        pe.matmul(z[:, S:S + P], tri[:, :], sp_[:, S:S + P], start=False, stop=True,
                                  skip_group_check=True).then_inc(stick_sum, 1)
                    dil_unit(u)
                    if hd < HEADS:
                        src = k_cat if hd < 4 else q_tok
                        if hd == 0:
                            out_taken(pe, layer, D_UKV + 2)
                            out_taken(pe, layer, D_UKV + 3)
                            pe.wait_ge(rope_step, layer * POOL_STEPS + 8)
                        if hd == 4:
                            pe.wait_ge(rope_step, layer * POOL_STEPS + POOL_STEPS)
                        if hd >= 2:
                            pe.wait_ge(mla_copied, n - 1)
                        for x in range(2):
                            for t in range(TT):
                                last = pe.transpose(ps[0:QK, 6 + hd % 2, S * x + P * t:S * x + P * t + P],
                                                    src[:, t, 2 * (hd % 4) + x, :], ident[:, :])
                        last.then_inc(mla_turned, 1)
                        dil_unit(u + 1)
                    if 1 <= hd < HEADS:
                        stick_times_v(hd - 1)

                pe.wait_ge(mla_copied, layer * HEADS + HEADS)
                turn_norm(layer * NORMS + N_MEM, 0, (6, 7, 2, 3))
                dil_unit(U_DQK + 2 * HEADS + 1)
                pe.wait_ge(stick_arg, layer * HEADS + HEADS)
                turn_norm(layer * NORMS + N_MEM, 1, (6, 7, 2, 3))
                stick_times_v(HEADS - 1)
                dil_unit(U_DQK + 2 * HEADS + 2)
                pe.wait_ge(x_lo, (layer * NORMS + N_MEM) * 4 + 4)

                def turn_probs(m):
                    base = layer * PIECES + m
                    pe.wait_ge(probs_done, base + 1)
                    src = probs_sb(m)
                    b0 = 4 if M_DIL <= m < M_X else 4 + m % 2
                    for b in range(key_w(m) // P):
                        last = pe.transpose(ps[:, b0 + b // 4, P * (b % 4):P * (b % 4) + P],
                                            src[:, P * b:P * b + P], ident[:, :])
                    last.then_inc(probs_turned, 1)

                def logits_free(m):
                    same = 1 if M_DIL <= m <= M_X else 2
                    if M_DIL < m < M_X:
                        pe.wait_ge(biased, layer * N_DIL + m - M_DIL)
                    elif m >= same:
                        pe.wait_ge(probs_done, layer * PIECES + m - same + 1)

                def times_v(m, blocks, w):
                    base = layer * PIECES + m
                    pt_waits(pe, layer, m)
                    if m >= 2:
                        pe.wait_ge(o_taken, base - 1)
                    for i, (b, v) in enumerate(blocks):
                        last = pe.matmul(ps[:, 6 + m % 2, 0:w], probs_t(m)[:, P * b:P * b + P], v,
                                         start=(i == 0), stop=(i == len(blocks) - 1))
                    last.then_inc(pv_done, 1)

                for m in range(N_MLA + 1):
                    if m < N_MLA:
                        hd, t = divmod(m, 2)
                        logits_free(m)
                        z = logits_of(m)
                        pe.matmul(z, mq[0:QK, hd, t * P:(t + 1) * P], mk[0:QK, hd, 0:key_w(m)], start=True,
                                  stop=True).then_inc(logits_ps, 1)
                    if m == 1:
                        pe.wait_ge(oa_copied, layer * 4 + 4)
                    if m >= 1:
                        turn_probs(m - 1)
                    dil_unit(U_DQK + 2 * HEADS + 3 + m)
                    if m >= 1:
                        hd, t = divmod(m - 1, 2)
                        times_v(m - 1, [(b, mv[:, b, hd * HD:(hd + 1) * HD]) for b in range(t + 1)], HD)

                def gate_unit(u):
                    i = u - U_GATE
                    if i < 24:
                        feature_out(layer, D_GATE + i, u)
                    elif i < 28:
                        feature_out(layer, D_GATE + i, u, v_hi, v_lo)
                    else:
                        token_out(layer, D_MV, u, i - 28, v_hi, v_lo)

                def dil_times_v(i):
                    hd, t = divmod(i, 2)
                    times_v(M_DIL + i, [(g * (t + 1) + b, dv[:, g, b, hd * HD:(hd + 1) * HD])
                                        for g in range(NG) for b in range(t + 1)], HD)

                def turn_heads(src, banks, tiles=range(TT)):
                    for t in tiles:
                        for k in range(4):
                            last = pe.transpose(ps[:, banks[t], k * P:(k + 1) * P],
                                                src[:, t * WIDTH + k * P:t * WIDTH + (k + 1) * P], ident[:, :])
                        last.then_inc(o_turned, 1)

                for i in range(N_DIL):
                    m = M_DIL + i
                    hd, t = divmod(i, 2)
                    r = slice(HD * (hd % 2), HD * (hd % 2) + HD)
                    kw = P * (t + 1)
                    logits_free(m)
                    for g in range(NG):
                        c = g * kw
                        last = pe.matmul(ps[:, 2 + c // 512, c % 512:c % 512 + kw], dq[r, g, hd // 2, t * P:(t + 1) * P],
                                         dk[r, g, hd // 2, 0:kw], start=True, stop=True)
                    last.then_inc(logits_ps, 1)
                    if i >= 1:
                        turn_probs(m - 1)
                    gate_unit(U_GATE + 2 * i)
                    if i == 1:
                        out_taken(pe, layer, D_DV + 2 * NG - 2)
                        out_taken(pe, layer, D_DV + 2 * NG - 1)
                    if i >= 1:
                        dil_times_v(i - 1)
                    if i == N_DIL - 1:
                        turn_probs(m)
                        turn_heads(o_b, (2, 3))
                    gate_unit(U_GATE + 2 * i + 1)
                dil_times_v(N_DIL - 1)

                def branch(b):
                    for j in range(4):
                        d, u = D_BR + 4 * b + j, U_BR + 4 * b + j
                        bank_free(layer, d)
                        ready(layer, u)
                        for f in range(2):
                            for k in range(4):
                                c = k * 2 * P + f * P
                                x = slice((b % 2) * 4 * S + k * S, (b % 2) * 4 * S + (k + 1) * S)
                                last = mm3(ps[:, 4 + d % 2, f * S:(f + 1) * S], slot(w_hi, u)[:, c:c + P],
                                           slot(w_lo, u)[:, c:c + P], u_hi[:, x], u_lo[:, x], k == 0, k == 3)
                        last.then_inc(unit_used, 1)

                pe.wait_ge(o_lo, layer * O_SPLITS + 1)
                branch(0)
                pe.wait_ge(o_taken, layer * PIECES + M_X)
                turn_heads(o_c, (6, 7))
                pe.wait_ge(o_lo, layer * O_SPLITS + 3)
                branch(1)
                pe.wait_ge(o_lo, layer * O_SPLITS + 5)
                branch(2)
                for k in range(4):
                    pe.wait_ge(merged_lo, layer * 4 + k // 2 + 1)
                    row_unit(layer, U_MIX + k, U_MIX + k, v_hi, v_lo, k, k == 0, False)
                pe.wait_ge(merged_lo, layer * 4 + 4)
                row_tail(layer, U_MIX + 4, 4, v_hi, v_lo, range(4, KT))

                feature_after_norm(layer, N_XA, U_XQ, ps[:, 0, 0:S])
                for i in range(1, 4):
                    feature_unit(layer, U_XQ + i, U_XQ + i, ps[:, i // 2, (i % 2) * S:(i % 2 + 1) * S], u_hi, u_lo)
                out_taken(pe, layer, D_XQ)

                for i in range(N_X + 2):
                    m = M_X + i
                    if i < N_X:
                        t, hd = divmod(i, XH)
                        if i == 2:
                            out_taken(pe, layer, D_XQ + 1)
                        logits_free(m)
                        pe.matmul(ps[:, 2 + m % 2, 0:M], x_q[:, hd, t * P:(t + 1) * P], x_k[:, hd, :],
                                  start=True, stop=True).then_inc(logits_ps, 1)
                    if 1 <= i <= N_X:
                        turn_probs(m - 1)
                    if i == N_X:
                        pe.wait_ge(o_lo, layer * O_SPLITS + 6)
                        row_quarter(layer, 0, U_XO, 0, 2, XH, v_hi, v_lo, range(XH), True)
                    if i >= 2:
                        hd = (i - 2) % XH
                        times_v(m - 2, [(b, x_v[:, b, hd * XD:(hd + 1) * XD]) for b in range(2)], XD)
                    if i == X_TURN:
                        pe.wait_ge(o_taken, layer * PIECES + M_X + XH)
                        turn_heads(o_b, (1, 6), (0,))
                row_quarter(layer, 0, U_XO, 2, XH, XH, v_hi, v_lo, range(XH), True)
                pe.wait_ge(o_taken, layer * PIECES + PIECES)
                turn_heads(o_b, (1, 6), (1,))
                row_quarter(layer, 1, U_XO, 0, XH, XH, v_hi, v_lo, range(XH), True)
                pe.wait_ge(o_lo, layer * O_SPLITS + 7)
                for i in range(2, 2 * TT):
                    row_quarter(layer, i, U_XO, 0, XH, XH, v_hi, v_lo, range(XH), True)
                ffn(layer, U_FFN2, 1)


_OUTS = [((1, S, D), "float32")]


def kernel(**inputs):
    import numpy as _np
    import concourse.bacc as _bacc
    from concourse import mybir as _mybir
    from concourse.bass_utils import run_bass_kernel_spmd as _run

    nc = _bacc.Bacc("TRN2", target_bir_lowering=False, num_devices=1)
    laid = {name: _np.asarray(value) for name, value in inputs.items()}
    weights = pack_weights({name: laid.pop(name) for name in STREAMED}, _np)
    laid["gate_bias"] = laid["gate_bias"].reshape(DEPTH, 24, P).transpose(0, 2, 1)
    laid.update(constants(), weights=weights)
    arrays, aps = {}, {}
    for name, value in laid.items():
        v = _np.ascontiguousarray(value)
        arrays[f"in_{name}"] = v
        aps[name] = nc.dram_tensor(f"in_{name}", v.shape, _mybir.dt.from_np(v.dtype), kind="ExternalInput").ap()
    out = nc.dram_tensor("out_0", _OUTS[0][0], _mybir.dt.float32, kind="ExternalOutput").ap()
    trunk(nc, aps, out)
    r = _run(nc, [arrays], core_ids=[0])
    return r.results[0]["out_0"]
```
